# Optimizing a Trainium2 kernel written in Bass

```python
import jax, jax.numpy as jnp
from jax import lax
import numpy as np
import jax
import jax.numpy as jnp

D_MODEL = 1024
BATCH = 1
SEQ = 512
DEPTH = 2

CHUNK = 64
MEM_LEN = 256
SGU_BLOCK = 128
A_GROUPS = 4
A_WIDTH = D_MODEL // 2
A_GROUP_DIM = A_WIDTH // A_GROUPS
POOL_WINDOWS = (2, 4, 8, 16)
B_WIDTH = D_MODEL // 2
B_GROUP_DIM = B_WIDTH // len(POOL_WINDOWS)
C_WIDTH = D_MODEL
CONV_K = 3
XATTN_HEADS = 4
XATTN_HEAD_DIM = D_MODEL // XATTN_HEADS
D_FF = ((8 * D_MODEL // 3 + 127) // 128) * 128
FFN_CONV_K = 3
LN_EPS = 1e-5
DEEPNORM_ALPHA = (2 * DEPTH) ** 0.25
DEEPNORM_BETA = (8 * DEPTH) ** -0.25
N_EVEN = (DEPTH + 1) // 2
N_ODD = DEPTH // 2


def layer_norm(x, g, b):
    xf = x.astype(jnp.float32)
    mu = jnp.mean(xf, axis=-1, keepdims=True)
    var = jnp.mean(jnp.square(xf - mu), axis=-1, keepdims=True)
    y = (xf - mu) * lax.rsqrt(var + LN_EPS)
    return (y * g.astype(jnp.float32) + b.astype(jnp.float32)).astype(x.dtype)

def causal_dwconv(x, w):
    k, c = w.shape
    return lax.conv_general_dilated(
        x, w[:, None, :].astype(x.dtype), window_strides=(1,), padding=[(k - 1, 0)],
        dimension_numbers=('NWC', 'WIO', 'NWC'), feature_group_count=c)

def trailing_mean_minus_self(v, window):
    seq = v.shape[1]
    vf = v.astype(jnp.float32)
    cs = jnp.cumsum(vf, axis=1)
    lagged = jnp.pad(cs, ((0, 0), (window, 0), (0, 0)))[:, :seq]
    count = jnp.minimum(jnp.arange(1, seq + 1), window).astype(jnp.float32)
    mean = (cs - lagged) / count[None, :, None]
    return (mean - vf).astype(v.dtype)

def mixer_ab(x, w_in, ln_g, ln_b, w_s, b_s, pool_w, pool_scale, w_out):
    bsz, seq, _ = x.shape
    proj = x @ w_in
    uv = jax.nn.gelu(proj[..., :2 * A_WIDTH])
    u, v = uv[..., :A_WIDTH], uv[..., A_WIDTH:]
    v = layer_norm(v, ln_g, ln_b)
    chunk_id = jnp.arange(SGU_BLOCK) // CHUNK
    mask = chunk_id[None, :] <= chunk_id[:, None]
    w_m = jnp.where(mask[None], w_s, 0.0).astype(v.dtype)
    vb = v.reshape(bsz, seq // SGU_BLOCK, SGU_BLOCK, A_GROUPS, A_GROUP_DIM)
    sp = jnp.einsum('gij,bnjgc->bnigc', w_m, vb) + b_s.T[None, None, :, :, None]
    y_a = u * sp.reshape(bsz, seq, A_WIDTH)
    xb = proj[..., 2 * A_WIDTH:].reshape(bsz, seq, len(POOL_WINDOWS), B_GROUP_DIM)
    pooled = jnp.stack([trailing_mean_minus_self(xb[:, :, g], w)
                        for g, w in enumerate(POOL_WINDOWS)], axis=2)
    y_b = jnp.einsum('bsgc,gcd->bsgd', pooled, pool_w).reshape(bsz, seq, B_WIDTH) * pool_scale
    return jnp.concatenate([y_a, y_b], axis=-1) @ w_out

def mixer_c(x, w_in, conv_w, w_out):
    proj = x @ w_in
    gate_b, gate_c, h = jnp.split(proj, 3, axis=-1)
    y = gate_b * causal_dwconv(gate_c * h, conv_w)
    return y @ w_out

def cross_attend(x, mem, wq, wkv, wo):
    bsz, seq, d = x.shape
    q = (x @ wq).reshape(bsz, seq, XATTN_HEADS, XATTN_HEAD_DIM)
    kv = mem @ wkv
    k = kv[..., :d].reshape(bsz, -1, XATTN_HEADS, XATTN_HEAD_DIM)
    v = kv[..., d:].reshape(bsz, -1, XATTN_HEADS, XATTN_HEAD_DIM)
    scores = jnp.einsum('bshd,bmhd->bhsm', q.astype(jnp.float32), k.astype(jnp.float32))
    probs = jax.nn.softmax(scores * (XATTN_HEAD_DIM ** -0.5), axis=-1).astype(x.dtype)
    out = jnp.einsum('bhsm,bmhd->bshd', probs, v).reshape(bsz, seq, d)
    return out @ wo

def conv_ffn(x, w_up, conv_w, conv_b, w_down):
    up = x @ w_up
    a, g = up[..., :D_FF], up[..., D_FF:]
    g = causal_dwconv(g, conv_w) + conv_b
    return (jax.nn.gelu(g) * a) @ w_down

def _normal(k, shape, scale):
    return jax.random.normal(k, shape, jnp.float32) * scale

def first_inputs(seed: int = 0) -> dict:
    key = jax.random.key(seed)
    ks = iter(jax.random.split(key, 32))
    d = D_MODEL
    beta = DEEPNORM_BETA
    x = _normal(next(ks), (BATCH, SEQ, d), 1.0)
    mem = _normal(next(ks), (BATCH, MEM_LEN, d), 1.0)
    ab_w_in = _normal(next(ks), (N_EVEN, d, 2 * A_WIDTH + B_WIDTH), d ** -0.5)
    sgu_ln_g = 1.0 + _normal(next(ks), (N_EVEN, A_WIDTH), 0.05)
    sgu_ln_b = _normal(next(ks), (N_EVEN, A_WIDTH), 0.02)
    sgu_w = _normal(next(ks), (N_EVEN, A_GROUPS, SGU_BLOCK, SGU_BLOCK), SGU_BLOCK ** -0.5)
    sgu_b = 1.0 + _normal(next(ks), (N_EVEN, A_GROUPS, SGU_BLOCK), 0.1)
    pool_w = _normal(next(ks), (N_EVEN, len(POOL_WINDOWS), B_GROUP_DIM, B_GROUP_DIM), B_GROUP_DIM ** -0.5)
    pool_scale = 1.0 + _normal(next(ks), (N_EVEN, B_WIDTH), 0.1)
    ab_w_out = _normal(next(ks), (N_EVEN, A_WIDTH + B_WIDTH, d), (A_WIDTH + B_WIDTH) ** -0.5 * beta)
    c_w_in = _normal(next(ks), (N_ODD, d, 3 * C_WIDTH), d ** -0.5)
    c_conv_w = _normal(next(ks), (N_ODD, CONV_K, C_WIDTH), CONV_K ** -0.5)
    c_w_out = _normal(next(ks), (N_ODD, C_WIDTH, d), C_WIDTH ** -0.5 * beta)
    ln_mix_g = 1.0 + _normal(next(ks), (DEPTH, d), 0.05)
    ln_mix_b = _normal(next(ks), (DEPTH, d), 0.02)
    xa_wq = _normal(next(ks), (DEPTH, d, d), d ** -0.5)
    xa_wk = _normal(next(ks), (DEPTH, d, d), d ** -0.5)
    xa_wv = _normal(next(ks), (DEPTH, d, d), d ** -0.5 * beta)
    xa_wkv = jnp.concatenate([xa_wk, xa_wv], axis=-1)
    xa_wo = _normal(next(ks), (DEPTH, d, d), d ** -0.5 * beta)
    ln_xa_g = 1.0 + _normal(next(ks), (DEPTH, d), 0.05)
    ln_xa_b = _normal(next(ks), (DEPTH, d), 0.02)
    ffn_w_up = _normal(next(ks), (DEPTH, d, 2 * D_FF), d ** -0.5)
    ffn_conv_w = _normal(next(ks), (DEPTH, FFN_CONV_K, D_FF), FFN_CONV_K ** -0.5)
    ffn_conv_b = _normal(next(ks), (DEPTH, D_FF), 0.02)
    ffn_w_down = _normal(next(ks), (DEPTH, D_FF, d), D_FF ** -0.5 * beta)
    ln_ffn_g = 1.0 + _normal(next(ks), (DEPTH, d), 0.05)
    ln_ffn_b = _normal(next(ks), (DEPTH, d), 0.02)
    return {"x": x, "mem": mem, "ab_w_in": ab_w_in, "sgu_ln_g": sgu_ln_g, "sgu_ln_b": sgu_ln_b,
            "sgu_w": sgu_w, "sgu_b": sgu_b, "pool_w": pool_w, "pool_scale": pool_scale,
            "ab_w_out": ab_w_out, "c_w_in": c_w_in, "c_conv_w": c_conv_w, "c_w_out": c_w_out,
            "ln_mix_g": ln_mix_g, "ln_mix_b": ln_mix_b, "xa_wq": xa_wq, "xa_wkv": xa_wkv,
            "xa_wo": xa_wo, "ln_xa_g": ln_xa_g, "ln_xa_b": ln_xa_b, "ffn_w_up": ffn_w_up,
            "ffn_conv_w": ffn_conv_w, "ffn_conv_b": ffn_conv_b, "ffn_w_down": ffn_w_down,
            "ln_ffn_g": ln_ffn_g, "ln_ffn_b": ln_ffn_b}

def first_block(x, mem, ab_w_in, sgu_ln_g, sgu_ln_b, sgu_w, sgu_b, pool_w, pool_scale,
              ab_w_out, c_w_in, c_conv_w, c_w_out, ln_mix_g, ln_mix_b, xa_wq, xa_wkv,
              xa_wo, ln_xa_g, ln_xa_b, ffn_w_up, ffn_conv_w, ffn_conv_b, ffn_w_down,
              ln_ffn_g, ln_ffn_b):
    alpha = DEEPNORM_ALPHA
    for layer in range(DEPTH):
        j = layer // 2
        if layer % 2 == 0:
            mix = mixer_ab(x, ab_w_in[j], sgu_ln_g[j], sgu_ln_b[j], sgu_w[j], sgu_b[j],
                           pool_w[j], pool_scale[j], ab_w_out[j])
        else:
            mix = mixer_c(x, c_w_in[j], c_conv_w[j], c_w_out[j])
        x = layer_norm(alpha * x + mix, ln_mix_g[layer], ln_mix_b[layer])
        x = layer_norm(alpha * x + cross_attend(x, mem, xa_wq[layer], xa_wkv[layer], xa_wo[layer]),
                       ln_xa_g[layer], ln_xa_b[layer])
        x = layer_norm(alpha * x + conv_ffn(x, ffn_w_up[layer], ffn_conv_w[layer],
                                            ffn_conv_b[layer], ffn_w_down[layer]),
                       ln_ffn_g[layer], ln_ffn_b[layer])
    return x


DEPTH_2 = 1

HEAD_DIM = 64
D_RWKV = 512
D_ATT = 512
D_MIX = D_RWKV + D_ATT
N_RWKV_HEADS = D_RWKV // HEAD_DIM
N_ATT_HEADS = D_ATT // HEAD_DIM
LORA_W = 64
LORA_A = 64
N_LEFT_CHUNKS = 8
BAND = (N_LEFT_CHUNKS + 1) * CHUNK
REL_CLIP = 128
N_REL = CHUNK + REL_CLIP
RMS_EPS = 1e-6
GN_EPS = 64e-5
D_SHIFT = 4 * D_RWKV + LORA_W + LORA_A
D_IN = D_SHIFT + 4 * D_ATT


def rms_norm(x, g):
    x32 = x.astype(jnp.float32)
    y = x32 * lax.rsqrt(jnp.mean(x32 * x32, axis=-1, keepdims=True) + RMS_EPS)
    return y.astype(x.dtype) * g

def token_shift(p, mu):
    prev = jnp.pad(p, ((0, 0), (1, 0), (0, 0)))[:, :-1]
    return p + mu * (prev - p)

def rwkv7_step(state, inp):
    r_t, w_t, k_t, v_t, a_t, b_t = inp
    sa = jnp.einsum('bhij,bhj->bhi', state, a_t)
    state = state * w_t[:, :, None, :] + sa[..., None] * b_t[:, :, None, :] + v_t[..., None] * k_t[:, :, None, :]
    y = jnp.einsum('bhij,bhj->bhi', state, r_t)
    return state, y

def rwkv7_mix(ps, w0, w2, a0, a2, k_k, k_a, r_k, lnx_g, lnx_b):
    b_, s_, _ = ps.shape
    f32 = jnp.float32
    r, k, v, g, wd, ad = jnp.split(ps, [D_RWKV, 2 * D_RWKV, 3 * D_RWKV, 4 * D_RWKV, 4 * D_RWKV + LORA_W], axis=-1)
    w_log = -jax.nn.softplus(-(w0 + jnp.tanh(wd) @ w2).astype(f32)) - 0.5
    decay = jnp.exp(-jnp.exp(w_log))
    a = jax.nn.sigmoid((a0 + ad @ a2).astype(f32))
    heads = lambda t: t.astype(f32).reshape(b_, s_, N_RWKV_HEADS, HEAD_DIM)
    r, k, v, decay, a = heads(r), heads(k), heads(v), heads(decay), heads(a)
    kk = k * k_k.astype(f32).reshape(N_RWKV_HEADS, HEAD_DIM)
    kk = kk / jnp.maximum(jnp.sqrt(jnp.sum(kk * kk, axis=-1, keepdims=True)), 1e-12)
    k = k * (1.0 + (a - 1.0) * k_a.astype(f32).reshape(N_RWKV_HEADS, HEAD_DIM))
    seq_first = lambda t: jnp.moveaxis(t, 1, 0)
    state0 = jnp.zeros((b_, N_RWKV_HEADS, HEAD_DIM, HEAD_DIM), f32)
    _, y = lax.scan(rwkv7_step, state0, (seq_first(r), seq_first(decay), seq_first(k), seq_first(v), seq_first(-kk), seq_first(kk * a)))
    y = jnp.moveaxis(y, 0, 1)
    mean = jnp.mean(y, axis=-1, keepdims=True)
    yc = y - mean
    y = yc * lax.rsqrt(jnp.mean(yc * yc, axis=-1, keepdims=True) + GN_EPS)
    y = y.reshape(b_, s_, D_RWKV) * lnx_g.astype(f32) + lnx_b.astype(f32)
    bonus = jnp.sum(r * k * r_k.astype(f32), axis=-1, keepdims=True) * v
    y = y + bonus.reshape(b_, s_, D_RWKV)
    return y.astype(ps.dtype), g

def chunk_band_attention(q, k, v, q_g, k_g, rel_bias):
    b_, s_, _ = q.shape
    nc = s_ // CHUNK
    pad = N_LEFT_CHUNKS * CHUNK
    def heads(t):
        return t.reshape(b_, s_, N_ATT_HEADS, HEAD_DIM).transpose(0, 2, 1, 3)
    q = heads(rms_norm(q.reshape(b_, s_, N_ATT_HEADS, HEAD_DIM), q_g).reshape(b_, s_, D_ATT))
    k = heads(rms_norm(k.reshape(b_, s_, N_ATT_HEADS, HEAD_DIM), k_g).reshape(b_, s_, D_ATT))
    v = heads(v)
    qc = q.reshape(b_, N_ATT_HEADS, nc, CHUNK, HEAD_DIM)
    def band(t):
        tp = jnp.pad(t, ((0, 0), (0, 0), (pad, 0), (0, 0))).reshape(b_, N_ATT_HEADS, nc + N_LEFT_CHUNKS, CHUNK, HEAD_DIM)
        return jnp.concatenate([tp[:, :, i:i + nc] for i in range(N_LEFT_CHUNKS + 1)], axis=3)
    kb, vb = band(k), band(v)
    s = jnp.einsum('bhnqd,bhnkd->bhnqk', qc, kb).astype(jnp.float32) * (HEAD_DIM ** -0.5)
    dist = jnp.arange(CHUNK)[:, None] + pad - jnp.arange(BAND)[None, :]
    rel_idx = jnp.clip(dist, -(CHUNK - 1), REL_CLIP) + (CHUNK - 1)
    bias = rel_bias[:, rel_idx].astype(jnp.float32)
    valid = (jnp.arange(nc)[:, None] * CHUNK + jnp.arange(BAND)[None, :] - pad) >= 0
    s = s + bias[None, :, None]
    s = jnp.where(valid[None, None, :, None, :], s, -1e30)
    p = jax.nn.softmax(s, axis=-1).astype(v.dtype)
    o = jnp.einsum('bhnqk,bhnkd->bhnqd', p, vb)
    return o.reshape(b_, N_ATT_HEADS, s_, HEAD_DIM).transpose(0, 2, 1, 3).reshape(b_, s_, D_ATT)

def second_inputs(seed: int = 0) -> dict:
    key = jax.random.key(seed)
    ks = jax.random.split(key, 22)
    n = lambda i, shape: jax.random.normal(ks[i], shape, jnp.float32)
    L = DEPTH_2
    return {
        'x': n(0, (BATCH, SEQ, D_MODEL)),
        'c': n(1, (BATCH, D_MODEL)),
        'norm_g': 1.0 + 0.1 * n(2, (L, D_MODEL)),
        'w_ada': n(3, (L, D_MODEL, 3 * D_MODEL)) * (0.5 * D_MODEL ** -0.5),
        'b_ada': 0.02 * n(4, (L, 3 * D_MODEL)),
        'w_in': n(5, (L, D_MODEL, D_IN)) * (D_MODEL ** -0.5),
        'mu_shift': jax.random.uniform(ks[6], (L, D_SHIFT), jnp.float32),
        'w0': -1.0 + 0.5 * n(7, (L, D_RWKV)),
        'w2': n(8, (L, LORA_W, D_RWKV)) * (0.5 * LORA_W ** -0.5),
        'a0': 0.5 * n(9, (L, D_RWKV)),
        'a2': n(10, (L, LORA_A, D_RWKV)) * (0.5 * LORA_A ** -0.5),
        'k_k': 0.85 + 0.05 * n(11, (L, D_RWKV)),
        'k_a': 1.0 + 0.05 * n(12, (L, D_RWKV)),
        'r_k': 0.1 * n(13, (L, N_RWKV_HEADS, HEAD_DIM)),
        'lnx_g': 1.0 + 0.1 * n(14, (L, D_RWKV)),
        'lnx_b': 0.02 * n(15, (L, D_RWKV)),
        'q_norm_g': 1.0 + 0.1 * n(16, (L, HEAD_DIM)),
        'k_norm_g': 1.0 + 0.1 * n(17, (L, HEAD_DIM)),
        'rel_bias': 0.5 * n(18, (L, N_ATT_HEADS, N_REL)),
        'w_out': n(19, (L, D_MIX, D_MODEL)) * (D_MIX ** -0.5),
    }

def second_block(x, c, norm_g, w_ada, b_ada, w_in, mu_shift, w0, w2, a0, a2, k_k, k_a, r_k, lnx_g, lnx_b, q_norm_g, k_norm_g, rel_bias, w_out):
    c_act = jax.nn.silu(c)
    for l in range(DEPTH_2):
        mod = c_act @ w_ada[l] + b_ada[l]
        shift, scale, gate = jnp.split(mod, 3, axis=-1)
        h = rms_norm(x, norm_g[l]) * (1.0 + scale[:, None, :]) + shift[:, None, :]
        proj = h @ w_in[l]
        ps = token_shift(proj[..., :D_SHIFT], mu_shift[l])
        pa = proj[..., D_SHIFT:]
        y_r, g_r = rwkv7_mix(ps, w0[l], w2[l], a0[l], a2[l], k_k[l], k_a[l], r_k[l], lnx_g[l], lnx_b[l])
        q, ka, va, g_a = jnp.split(pa, 4, axis=-1)
        y_a = chunk_band_attention(q, ka, va, q_norm_g[l], k_norm_g[l], rel_bias[l])
        y = jnp.concatenate([y_r * jax.nn.silu(g_r), y_a * jax.nn.silu(g_a)], axis=-1)
        x = x + gate[:, None, :] * (y @ w_out[l])
    return x


def setup_inputs(seed=0):
    out = dict(first_inputs(seed))
    for name, value in second_inputs(seed + 1).items():
        if name != "x":
            out[name + "_2"] = value
    return out


def reference(
    x, mem, ab_w_in, sgu_ln_g, sgu_ln_b, sgu_w, sgu_b, pool_w, pool_scale, ab_w_out, c_w_in,
    c_conv_w, c_w_out, ln_mix_g, ln_mix_b, xa_wq, xa_wkv, xa_wo, ln_xa_g, ln_xa_b, ffn_w_up,
    ffn_conv_w, ffn_conv_b, ffn_w_down, ln_ffn_g, ln_ffn_b, c_2, norm_g_2, w_ada_2, b_ada_2,
    w_in_2, mu_shift_2, w0_2, w2_2, a0_2, a2_2, k_k_2, k_a_2, r_k_2, lnx_g_2, lnx_b_2,
    q_norm_g_2, k_norm_g_2, rel_bias_2, w_out_2,
):
    x = first_block(
        x, mem, ab_w_in, sgu_ln_g, sgu_ln_b, sgu_w, sgu_b, pool_w, pool_scale, ab_w_out, c_w_in,
        c_conv_w, c_w_out, ln_mix_g, ln_mix_b, xa_wq, xa_wkv, xa_wo, ln_xa_g, ln_xa_b, ffn_w_up,
        ffn_conv_w, ffn_conv_b, ffn_w_down, ln_ffn_g, ln_ffn_b,
    )
    return second_block(
        x, c_2, norm_g_2, w_ada_2, b_ada_2, w_in_2, mu_shift_2, w0_2, w2_2, a0_2, a2_2, k_k_2,
        k_a_2, r_k_2, lnx_g_2, lnx_b_2, q_norm_g_2, k_norm_g_2, rel_bias_2, w_out_2,
    )


_drawn_inputs = setup_inputs


def setup_inputs(seed=0):
    import zlib

    import numpy as np

    out = dict(_drawn_inputs(seed))
    spreads = {}
    factors = {'sgu_ln_g': 7.416,
     'sgu_ln_b': 8.0,
     'sgu_b': 2.964,
     'ffn_conv_b': 8.0,
     'b_ada_2': 4.616,
     'w2_2': 5.457,
     'k_k_2': 39.01,
     'k_a_2': 6.187,
     'lnx_g_2': 4.535,
     'lnx_b_2': 26.996,
     'q_norm_g_2': 8.0,
     'k_norm_g_2': 8.0,
     'rel_bias_2': 6.832}
    for name, (base, spread) in spreads.items():
        noise = np.random.default_rng([zlib.crc32(name.encode()), seed]).standard_normal(out[name].shape)
        drawn = base * np.exp(spread * noise) if base else spread * noise
        out[name] = jnp.asarray(drawn.astype(out[name].dtype))
    for name, factor in factors.items():
        out[name] = (out[name] * factor).astype(out[name].dtype)
    return out
```

```python
from contextlib import ExitStack

import concourse.bass as bass
from concourse import mybir

F = mybir.dt.float32
FR = mybir.dt.float32r
ALU = mybir.AluOpType
ACT = mybir.ActivationFunctionType
AX = mybir.AxisListType

P = 128
D = 1024
T = 512
MEM = 256
DFF = 2816
ALPHA = 4.0 ** 0.25
NR = 4
NH = 5
EM5 = 0.6065306597126334


class Eng:

    def __init__(self, name, sem):
        self.name, self.sem, self.n, self.q, self.seen, self.last = name, sem, 0, [], {}, None

    def wait(self, *toks):
        for t in toks:
            if t is None:
                continue
            if isinstance(t, list):
                self.wait(*t)
                continue
            sem, v = t
            if self.seen.get(id(sem), 0) >= v:
                continue
            self.seen[id(sem)] = v
            self.q.append(lambda e, s=sem, k=v: e.wait_ge(s, k))

    def op(self, f, *toks, chain=True, inc=True):
        self.wait(*toks)
        if chain:
            self.wait(self.last)
        if not inc:
            self.q.append(f)
            return None
        self.n += 1
        self.q.append(lambda e, g=f, s=self.sem: g(e).then_inc(s, 1))
        self.last = (self.sem, self.n)
        return self.last

    def dma(self, dst, src, ds, *toks):
        self.wait(*toks)
        ds.n += 16
        self.q.append(lambda e: e.dma_start(dst, src).then_inc(ds.sem, 16))
        return (ds.sem, ds.n)


class Count:
    def __init__(self, sem):
        self.sem, self.n = sem, 0


class Bank:

    def __init__(self, t):
        self.t, self.free = t, None


VEC_ROWS = [("fcw0", 66), ("fcw1", 66), ("fcb0", 22), ("fcb1", 22), ("ccw", 24), ("psc", 4), ("mu", 17),
            ("w0", 4), ("a0", 4), ("kk", 4), ("ka", 4), ("rk", 4), ("lxg", 4), ("lxb", 4), ("ng", 8),
            ("c", 8), ("ba", 24), ("qg", 1), ("kg", 1)]


def build(nc, I, out, stop=None, dbg=None):
    ctx = ExitStack()
    with ctx:
        def sb(name, shape, dt=F):
            return ctx.enter_context(nc.sbuf_tensor(name, shape, dt))

        def sem(name):
            return ctx.enter_context(nc.semaphore(name))

        PE = Eng("tensor", sem("s_pe"))
        V = Eng("vector", sem("s_v"))
        A = Eng("scalar", sem("s_a"))
        G = Eng("gpsimd", sem("s_g"))
        S = Eng("sync", sem("s_s"))
        nds = [0]

        def dsem():
            nds[0] += 1
            return Count(sem(f"s_d{nds[0]}"))

        XR = sb("XR", [P, 4, D])
        XH = sb("XH", [P, 8, T], FR)
        XL = sb("XL", [P, 8, T], FR)
        RAW = [sb(f"RAW{i}", [P, 2, 512]) for i in range(NR)]
        WH = [sb(f"WH{i}", [P, 2, 512], FR) for i in range(NH)]
        WL = [sb(f"WL{i}", [P, 2, 512], FR) for i in range(NH)]
        GB = sb("GB", [P, 2048])
        BIG = sb("BIG", [P, 12288])
        LATE = sb("LATE", [P, 8192])
        SCR = sb("SCR", [P, 3136])
        CST = sb("CST", [P, 144])
        VEC = sb("VEC", [P, 384])
        SM = sb("SM", [P, 256])
        CH = sb("CH", [P, 8, 2], FR)
        CL = sb("CL", [P, 8, 2], FR)
        d_x = nc.dram_tensor("spill_x", (P, 4096), F, kind="Internal").ap()
        d_g = nc.dram_tensor("spill_g", (P, 2048), F, kind="Internal").ap()
        d_b = nc.dram_tensor("spill_b", (P, 2048), F, kind="Internal").ap()
        d_rel = nc.dram_tensor("rel_padded", (8, 384), F, kind="Internal").ap()
        ident = CST[:, 0:128]
        invc = CST[:, 128:144]
        banks = [Bank(ctx.enter_context(nc.psum_tensor(f"ps{i}", [P, 512], F))) for i in range(8)]
        nbk = [0]

        def bank():
            b = banks[nbk[0] % 8]
            nbk[0] += 1
            return b

        def big(off, n, a=None):
            v = BIG[:, off:off + n]
            return v if a is None else v.rearrange("p (a b) -> p a b", a=a)

        def late(off, n, a=None):
            v = LATE[:, off:off + n]
            return v if a is None else v.rearrange("p (a b) -> p a b", a=a)

        chunks = []

        def w_cols(w, k0, pieces):
            v = w[k0:k0 + 256, :].rearrange("(k p) n -> p k n", p=P)
            at, got = 0, []
            for c0, n in pieces:
                got.append((at, n, v[:, :, c0:c0 + n]))
                at += n
            chunks.append((got, at))

        def w_block(w, c0, n=512, rows=1024):
            for k in range(0, rows, 256):
                w_cols(w, k, [(c0, n)])

        for l in range(2):
            for b in range(4):
                w_block(I["xa_wkv"][l], 512 * b)
        for l in range(2):
            if l == 0:
                for c0 in (512, 0, 1024):
                    w_block(I["ab_w_in"][0], c0)
                for b in range(2):
                    w_block(I["ab_w_out"][0], 512 * b)
            else:
                for c0 in (1024, 2048, 1536, 2560, 0, 512):
                    w_block(I["c_w_in"][0], c0)
                for b in range(2):
                    w_block(I["c_w_out"][0], 512 * b)
            for w in ("xa_wq", "xa_wo"):
                for b in range(2):
                    w_block(I[w][l], 512 * b)
            for i in range(11):
                for k in range(0, 1024, 256):
                    w_cols(I["ffn_w_up"][l], k, [(256 * i, 256), (DFF + 256 * i, 256)])
            for b in range(2):
                w_block(I["ffn_w_down"][l], 512 * b, rows=DFF)
        for b in range(6):
            w_block(I["w_ada_2"][0], 512 * b)
        for c0, n in ((2176, 512), (2688, 512), (3200, 512), (3712, 512),
                      (0, 512), (512, 512), (1024, 512), (1536, 512), (2048, 128)):
            w_block(I["w_in_2"][0], c0, n)
        for b in range(2):
            w_block(I["w_out_2"][0], 512 * b)

        raw_ds = [dsem() for _ in range(NR)]
        conv_tok = {}
        dma_tok = {}
        rel_tok = {}
        wpos = [0]

        def w_dma(i):
            if i >= len(chunks):
                return
            for at, n, src in chunks[i][0]:
                dma_tok[i] = S.dma(RAW[i % NR][:, :, at:at + n], src, raw_ds[i % NR], conv_tok.get(i - NR))

        def w_conv(i):
            if i >= len(chunks):
                return
            n = chunks[i][1]
            raw, hi, lo = RAW[i % NR][:, :, 0:n], WH[i % NH][:, :, 0:n], WL[i % NH][:, :, 0:n]
            th = A.op(lambda e: e.activation(hi, raw, ACT.Copy), dma_tok[i], rel_tok.get(i - NH), chain=False)
            conv_tok[i] = V.op(lambda e: e.tensor_tensor(lo, raw, hi.bitcast(F), ALU.subtract), th, chain=False)
            w_dma(i + NR)

        def w_get():
            i = wpos[0]
            wpos[0] += 1
            return i, WH[i % NH], WL[i % NH], conv_tok[i]

        def w_release(i, tok):
            rel_tok[i] = tok
            w_conv(i + NH)

        def mm(o, l, r, start, stop, *toks, inc=False):
            return PE.op(lambda e: e.matmul(o, l, r, start=start, stop=stop), *toks, chain=False, inc=inc)

        def mm3(o, lh, ll, rh, rl, start, stop, *toks, inc=False):
            mm(o, lh, rh, start, False, *toks)
            mm(o, lh, rl, False, False)
            return mm(o, ll, rh, False, stop, inc=inc)

        def tr(o, i, *toks, inc=False, n=128):
            return PE.op(lambda e: e.transpose(o, i, ident[0:n, 0:n]), *toks, chain=False, inc=inc)

        def act(o, i, f, *toks, chain=True, **kw):
            return A.op(lambda e: e.activation(o, i, f, **kw), *toks, chain=chain)

        def tt(o, a, b, op, *toks, eng=None, chain=True):
            return (eng or V).op(lambda e: e.tensor_tensor(o, a, b, op), *toks, chain=chain)

        def ts(o, a, s1, s2, op0, op1, *toks, eng=None, chain=True):
            if s2 is None:
                return (eng or V).op(lambda e: e.tensor_scalar(o, a, s1, None, op0), *toks, chain=chain)
            return (eng or V).op(lambda e: e.tensor_scalar(o, a, s1, s2, op0, op1), *toks, chain=chain)

        def stt(o, a, s, b, op0, op1, *toks, chain=True):
            return V.op(lambda e: e.scalar_tensor_tensor(out=o, in0=a, scalar=s, in1=b, op0=op0, op1=op1),
                        *toks, chain=chain)

        def memset(eng, o, v, *toks):
            return eng.op(lambda e: e.memset(o, v), *toks)

        def split(hi, lo, src, *toks):
            th = act(hi, src, ACT.Copy, *toks, chain=False)
            return tt(lo, src, hi.bitcast(F), ALU.subtract, th, *toks, chain=False)

        def proj_t(xh, xl, nk2, ntok, nm, evac, *toks):
            bs = [bank() for _ in range(nm)]
            done = []
            for c in range(nk2):
                i, wh, wl, tok = w_get()
                for m in range(nm):
                    for k in range(2):
                        kt = 2 * c + k
                        last = c == nk2 - 1 and k == 1
                        t = mm3(bs[m].t[:, 0:ntok], wh[:, k, 128 * m:128 * m + 128], wl[:, k, 128 * m:128 * m + 128],
                                xh[:, kt, 0:ntok], xl[:, kt, 0:ntok], kt == 0, last, tok,
                                bs[m].free if kt == 0 else None, *toks, inc=last or (m == nm - 1 and k == 1))
                        if last:
                            done.append(t)
                w_release(i, t)
            for m in range(nm):
                evac(m, bs[m], done[m])

        def proj_n(xa, nk2, evac, final, *toks, nt=4, prep=None):
            bs = [bank() for _ in range(nt)]
            done = []
            cut = nk2 - 4 if final else nk2

            def part(c, got, t):
                i, wh, wl, tok = got
                for k in range(2):
                    kt = 2 * c + k
                    xh, xl = xa(kt, t)
                    last = c == nk2 - 1 and k == 1
                    r = mm3(bs[t].t[:, :], xh, xl, wh[:, k, :], wl[:, k, :], kt == 0, last, tok,
                            bs[t].free if kt == 0 else None, prep[kt] if prep else None, *toks,
                            inc=last or (t == nt - 1 and k == 1))
                return r

            for c in range(cut):
                got = w_get()
                if prep:
                    prep_k(prep, c)
                for t in range(nt):
                    r = part(c, got, t)
                    if c == nk2 - 1:
                        done.append(r)
                w_release(got[0], r)
                if prep:
                    prep_rel(prep, c, r)
            if not final:
                for t in range(nt):
                    evac(t, bs[t], done[t])
                return
            gots = [w_get() for _ in range(4)]
            if prep:
                for c in range(cut, nk2):
                    prep_k(prep, c)
            rels = {}
            for t in range(nt):
                for c in range(cut, nk2):
                    r = part(c, gots[c - cut], t)
                    rels[c] = r
                evac(t, bs[t], r)
            for c in range(cut, nk2):
                w_release(gots[c - cut][0], rels[c])
                if prep:
                    prep_rel(prep, c, rels[c])

        for i in range(NR):
            w_dma(i)
        tc = A.dma(CST[:, :], I["cst"], dsem())
        t_mem = A.dma(big(0, 2048, 2), I["mem"][0].rearrange("(a p) n -> p a n", p=P), dsem())
        xin = dsem()
        t_x = A.dma(XR[:, :, :], I["x"][0].rearrange("(a p) n -> p a n", p=P), xin)

        def rows(name):
            r = {
                "fcw0": I["ffn_conv_w"][0].rearrange("k (m c) -> (k m) c", c=P),
                "fcw1": I["ffn_conv_w"][1].rearrange("k (m c) -> (k m) c", c=P),
                "ccw": I["c_conv_w"][0].rearrange("k (m c) -> (k m) c", c=P),
            }
            if name in r:
                return [r[name]]
            if name in ("qg", "kg"):
                v = I["q_norm_g_2" if name == "qg" else "k_norm_g_2"]
                return [v, v]
            v = {
                "fcb0": I["ffn_conv_b"][0:1], "fcb1": I["ffn_conv_b"][1:2], "psc": I["pool_scale"],
                "mu": I["mu_shift_2"], "w0": I["w0_2"], "a0": I["a0_2"], "kk": I["k_k_2"], "ka": I["k_a_2"],
                "lxg": I["lnx_g_2"], "lxb": I["lnx_b_2"], "ng": I["norm_g_2"], "c": I["c_2"],
                "ba": I["b_ada_2"],
            }
            if name == "rk":
                return [I["r_k_2"][0].rearrange("(a b) c -> a (b c)", b=2)]
            return [v[name].rearrange("a (m c) -> (a m) c", c=P)]

        vcol = {}
        r0 = 0
        vds = dsem()
        stg = big(2048, 384, 3)
        t_vm = memset(V, stg, 0.0)
        for name, n in VEC_ROWS:
            vcol[name] = r0
            aps = rows(name)
            if len(aps) == 2:
                for h, a in enumerate(aps):
                    t_v = A.dma(stg[r0 % 128:r0 % 128 + 1, r0 // 128, 64 * h:64 * h + 64], a, vds, t_vm)
            else:
                a, at = aps[0], 0
                while at < n:
                    m = min(n - at, 128 - (r0 + at) % 128)
                    t_v = A.dma(stg[(r0 + at) % 128:(r0 + at) % 128 + m, (r0 + at) // 128, :], a[at:at + m, :], vds, t_vm)
                    at += m
            r0 += n
        assert r0 <= 384

        def vec(name, j=0):
            return VEC[:, vcol[name] + j:vcol[name] + j + 1]

        for i in range(NH):
            w_conv(i)
        nhalf = SM[:, 0:32]
        memset(V, nhalf, -0.5)
        t_nh = memset(V, SM[:, 32:64], 0.0)
        b = bank()
        for j in range(3):
            t = tr(b.t[:, 128 * j:128 * j + 128], stg[:, j, :], tc, t_v, t_vm, inc=j == 2)
        t_vec = b.free = V.op(lambda e, b=b: e.tensor_copy(VEC[:, :], b.t[:, 0:384]), t)

        def transposes(src, nt, n0=0, *toks):
            for t in range(n0, n0 + nt):
                for q in range(2):
                    b = bank()
                    for k in range(4):
                        r = tr(b.t[:, 128 * k:128 * k + 128], src(t, 4 * q + k), b.free, *toks, inc=k == 3)
                    b.free = split(XH[:, 4 * q:4 * q + 4, 128 * t:128 * t + 128],
                                   XL[:, 4 * q:4 * q + 4, 128 * t:128 * t + 128],
                                   b.t[:, :].rearrange("p (k n) -> p k n", k=4), r)
            return b.free

        memt = big(0, 2048, 2)
        tx = transposes(lambda t, k: memt[:, t, 128 * k:128 * k + 128], 2, 0, tc, t_mem)
        KT = [late(4096 * l, 2048, 8) for l in range(2)]
        VT = [late(4096 * l + 2048, 2048, 2) for l in range(2)]
        for l in range(2):
            for nb in range(2):
                def evk(m, b, tok, l=l, nb=nb):
                    b.free = act(KT[l][:, 4 * nb + m, :], b.t[:, 0:256], ACT.Copy, tok, chain=False)
                proj_t(XH, XL, 4, 256, 4, evk, tx)
            for nb in range(2):
                def evv(t, b, tok, l=l, nb=nb):
                    b.free = act(VT[l][:, t, 512 * nb:512 * nb + 512], b.t[:, :], ACT.Copy, tok, chain=False)
                proj_n(lambda kt, t: (XH[:, kt, 128 * t:128 * t + 128], XL[:, kt, 128 * t:128 * t + 128]), 4, evv,
                       False, tx, nt=2)
        t_kv = A.last

        def xa_x(kt, t):
            return XH[:, kt, 128 * t:128 * t + 128], XL[:, kt, 128 * t:128 * t + 128]

        def load_gb(g, b, tok, n=D):
            ds = dsem()
            G.dma(GB[:, 0:n], g.partition_broadcast(P), ds, tok)
            return G.dma(GB[:, 1024:1024 + n], b.partition_broadcast(P), ds, tok)

        stats = SM[:, 64:112].rearrange("p (t j s) -> p t j s", t=4, j=2)
        mv = SM[:, 112:120].rearrange("p (t s) -> p t s", s=2)
        vr = SM[:, 120:124]
        rs = SM[:, 124:128]
        nmr = SM[:, 128:132]

        def rstd(t, nstat, dst_rs):
            st = stats[:, t, 0:nstat, :]
            a = V.op(lambda e: e.bn_aggr(mv[:, t, :], st))
            ts(vr[:, t:t + 1], mv[:, t, 1:2], 1e-5, None, ALU.add, None, a, eng=G)
            r = tt(dst_rs, vr[:, t:t + 1], nhalf[:, 0:1], ALU.pow, t_nh, eng=G)
            return stt(nmr[:, t:t + 1], mv[:, t, 0:1], -1.0, dst_rs, ALU.mult, ALU.mult, r)

        def ln_in(j, t, b, tok):
            o = XR[:, t, 512 * j:512 * j + 512]
            b.free = stt(o, o, ALPHA, b.t[:, :], ALU.mult, ALU.add, tok)
            return V.op(lambda e: e.bn_stats(stats[:, t, j, :], o))

        def ln_out(t, tgb, turn=True):
            r = rstd(t, 2, rs[:, t:t + 1])
            x = XR[:, t, :]
            a = act(x, x, ACT.Identity, r, scale=rs[:, t:t + 1], bias=nmr[:, t:t + 1])
            tt(x, x, GB[:, 0:1024], ALU.mult, a, tgb)
            r = tt(x, x, GB[:, 1024:2048], ALU.add)
            return r

        def out_ln(xa, nk2, tgb, prep=None, turn=True, *toks):
            for j in range(2):
                def ev(t, b, tok, j=j):
                    ln_in(j, t, b, tok)
                    if j == 1:
                        r = ln_out(t, tgb)
                        lnr.append(r)
                        pend.append((t, r))
                lnr, pend = [], []
                proj_n(xa, nk2, ev, j == 1, *toks, prep=prep[j] if prep else None)
            last = lnr[-1]
            if not turn:
                return last, last
            for t, r in pend:
                tx = transposes(lambda t, k: XR[:, t, 128 * k:128 * k + 128], 1, t, r)
            return tx, last

        stopped = [False]

        def finish(src, n=4096):
            ds = dsem()
            o = out[0].rearrange("(a p) n -> p a n", p=P)
            t = S.dma(o, src, ds, PE.last, V.last, A.last, G.last)
            S.wait(t)
            stopped[0] = True

        t_gb = load_gb(I["ln_mix_g"][0], I["ln_mix_b"][0], None)
        tx = transposes(lambda t, k: XR[:, t, 128 * k:128 * k + 128], 4, 0, t_x)

        def mixer_ab():
            nonlocal tx
            uT = big(0, 2048, 4)
            vt = big(2048, 2048, 4)
            xb = big(4096, 2112, 4)
            pp = [big(6208 + 528 * i, 528) for i in range(2)]
            pooled = big(7264, 2048, 4)
            wraw = big(9312, 512, 4)
            wmT = big(9824, 512, 4)
            bs = big(10336, 512, 4)
            pw = big(10848, 512, 4)
            lg = SCR[:, 0:512]
            lb = SCR[:, 512:1024]
            ytmp = SCR[:, 1024:1536]
            ds = dsem()
            G.dma(wraw, I["sgu_w"][0].rearrange("g i j -> i g j"), ds, V.last, PE.last)
            G.dma(bs, I["sgu_b"][0].partition_broadcast(P), ds)
            G.dma(pw, I["pool_w"][0].rearrange("g c d -> c g d"), ds)
            G.dma(lg, I["sgu_ln_g"][0].partition_broadcast(P), ds)
            t_l = G.dma(lb, I["sgu_ln_b"][0].partition_broadcast(P), ds)
            tm = memset(G, xb[:, :, 0:16], 0.0, V.last, PE.last)
            memset(G, pp[0][:, 0:16], 0.0)
            tm = memset(G, pp[1][:, 0:16], 0.0)

            def ev_v(t, b, tok):
                o = vt[:, t, :]
                a = b.free = act(o, b.t[:, :], ACT.Gelu_apprx_tanh, tok)
                V.op(lambda e: e.bn_stats(stats[:, t, 0, :], o), a)
                r = rstd(t, 1, rs[:, t:t + 1])
                a = act(o, o, ACT.Identity, r, scale=rs[:, t:t + 1], bias=nmr[:, t:t + 1])
                tt(o, o, lg, ALU.mult, a, t_l)
                tt(o, o, lb, ALU.add)

            proj_n(xa_x, 4, ev_v, False, tx)
            t_vt = V.last
            b = bank()
            for g in range(4):
                r = tr(b.t[:, 128 * g:128 * g + 128], wraw[:, g, :], t_l, b.free, inc=g == 3)
            b.free = V.op(lambda e, b=b: e.tensor_copy(wmT, b.t[:, :].rearrange("p (g i) -> p g i", g=4)), r)
            t_wm = memset(V, wmT[64:128, :, 0:64], 0.0)

            def ev_u(m, b, tok):
                b.free = act(uT[:, m, :], b.t[:, :], ACT.Gelu_apprx_tanh, tok)

            proj_t(XH, XL, 4, 512, 4, ev_u, tx)
            t_u = A.last

            def ev_b(m, b, tok):
                b.free = act(xb[:, m, 16:528], b.t[:, :], ACT.Copy, tok, tm)

            proj_t(XH, XL, 4, 512, 4, ev_b, tx)
            t_xb = A.last
            ys = []
            for g in range(4):
                b = bank()
                for n in range(4):
                    r = mm(b.t[:, 128 * n:128 * n + 128], vt[:, n, 128 * g:128 * g + 128], wmT[:, g, :], True, True,
                           t_vt, t_wm, b.free, inc=n == 3)
                bb = bs[:, g, :].unsqueeze(1).broadcast_to([P, 4, 128])
                y3 = ytmp.rearrange("p (n i) -> p n i", n=4)
                b.free = tt(y3, b.t[:, :].rearrange("p (n i) -> p n i", n=4), bb, ALU.add, r, t_l)
                y = tt(uT[:, g, :], uT[:, g, :], ytmp, ALU.mult, t_u)
                split(XH[:, g, :], XL[:, g, :], uT[:, g, :], y, PE.last)
            for g in range(4):
                w = 2 << g
                src = xb[:, g, :]
                for s in range(g + 1):
                    dst = pp[s % 2]
                    tt(dst[:, 16:528], src[:, 16:528], src[:, 16 - (1 << s):528 - (1 << s)], ALU.add, t_xb, tm)
                    src = dst
                stt(pooled[:, g, :], src[:, 16:528], 1.0 / w, xb[:, g, 16:528], ALU.mult, ALU.subtract)
                tt(ytmp[:, 0:w], src[:, 16:16 + w], invc[:, 0:w], ALU.mult)
                r = tt(pooled[:, g, 0:w], ytmp[:, 0:w], xb[:, g, 16:16 + w], ALU.subtract)
                b = bank()
                r = mm(b.t[:, :], pw[:, g, :], pooled[:, g, :], True, True, r, t_l, b.free, inc=True)
                b.free = r = ts(pooled[:, g, :], b.t[:, :], vec("psc", g), None, ALU.mult, None, r, t_vec)
                ty = split(XH[:, 4 + g, :], XL[:, 4 + g, :], pooled[:, g, :], r, PE.last)
            return ty

        def mixer_c():
            ch = big(0, 4112, 8)
            cv = big(4112, 4096, 8)
            tm = memset(V, ch[:, :, 0:2], 0.0, PE.last)
            for hf in range(2):
                def ev_c(m, b, tok, hf=hf):
                    b.free = act(ch[:, 4 * hf + m, 2:514], b.t[:, :], ACT.Copy, tok, tm, V.last)

                def ev_h(m, b, tok, hf=hf):
                    j = 4 * hf + m
                    c, x = cv[:, j, :], ch[:, j, :]
                    b.free = tt(x[:, 2:514], x[:, 2:514], b.t[:, :], ALU.mult, tok, t_c)
                    ts(c, x[:, 2:514], vec("ccw", 16 + j), None, ALU.mult, None, t_vec)
                    stt(c, x[:, 1:513], vec("ccw", 8 + j), c, ALU.mult, ALU.add)
                    stt(c, x[:, 0:512], vec("ccw", j), c, ALU.mult, ALU.add)

                proj_t(XH, XL, 4, 512, 4, ev_c, tx)
                t_c = A.last
                proj_t(XH, XL, 4, 512, 4, ev_h, tx)
            for hf in range(2):
                def ev_g(m, b, tok, hf=hf):
                    c = cv[:, 4 * hf + m, :]
                    b.free = tt(c, c, b.t[:, :], ALU.mult, tok)

                proj_t(XH, XL, 4, 512, 4, ev_g, tx)
            r, pe = V.last, PE.last
            for j in range(8):
                ty = split(XH[:, j, :], XL[:, j, :], cv[:, j, :], r, pe)
            return ty

        def cross(l):
            qT = big(0, 4096, 8)
            Pm = [big(4096 + 1024 * i, 1024, 4) for i in range(2)]
            PT = [big(6144 + 1024 * i, 1024, 2) for i in range(2)]
            mx = SM[:, 132:140].rearrange("p (i t) -> p i t", i=2)
            sm = SM[:, 140:148].rearrange("p (i t) -> p i t", i=2)
            tp = [V.last, PE.last]
            for nb in range(2):
                def evq(m, b, tok, nb=nb):
                    b.free = act(qT[:, 4 * nb + m, :], b.t[:, :], ACT.Copy, tok, *tp, chain=False)
                proj_t(XH, XL, 4, 512, 4, evq, tx)
            tq, pq = A.last, PE.last
            pt_free = [None, None]
            state = {}

            def scores(h):
                i = h % 2
                toks = []
                for tp2 in range(2):
                    b = bank()
                    for t in range(2):
                        tt_ = 2 * tp2 + t
                        for k in range(2):
                            r = mm(b.t[:, 256 * t:256 * t + 256], qT[:, 2 * h + k, 128 * tt_:128 * tt_ + 128],
                                   KT[l][:, 2 * h + k, :], k == 0, k == 1, tq, t_kv, b.free, inc=t == 1 and k == 1)
                    v = b.t[:, :].rearrange("p (t m) -> p t m", t=2)
                    m2 = mx[:, i, 2 * tp2:2 * tp2 + 2]
                    V.op(lambda e, m2=m2, v=v: e.tensor_reduce(m2, v, AX.X, ALU.max), r, pt_free[i])
                    r = ts(m2, m2, -0.0625, None, ALU.mult, None)
                    for t in range(2):
                        tt_ = 2 * tp2 + t
                        a = act(Pm[i][:, tt_, :], v[:, t, :], ACT.Exp, r, pt_free[i], scale=0.0625,
                                bias=mx[:, i, tt_:tt_ + 1], accum_out=sm[:, i, tt_:tt_ + 1])
                    b.free = a
                V.op(lambda e: e.reciprocal(sm[:, i, :], sm[:, i, :]), a)
                for t in range(4):
                    r = ts(Pm[i][:, t, :], Pm[i][:, t, :], sm[:, i, t:t + 1], None, ALU.mult, None)
                state[h] = r

            def values(h):
                i = h % 2
                ts_ = []
                for mt in range(2):
                    b = bank()
                    for t in range(4):
                        r = tr(b.t[:, 128 * t:128 * t + 128], Pm[i][:, t, 128 * mt:128 * mt + 128], state[h], b.free,
                               inc=t == 3)
                    b.free = act(PT[i][:, mt, :], b.t[:, :], ACT.Copy, r)
                    ts_.append(b.free)
                pt_free[i] = r
                for d in range(2):
                    b = bank()
                    for mt in range(2):
                        r = mm(b.t[:, :], VT[l][:, mt, 256 * h + 128 * d:256 * h + 128 * d + 128], PT[i][:, mt, :],
                               mt == 0, mt == 1, ts_[mt], b.free, inc=mt == 1)
                    b.free = ty = split(XH[:, 2 * h + d, :], XL[:, 2 * h + d, :], b.t[:, :], r, pq)
                return ty

            scores(0)
            for h in range(4):
                if h < 3:
                    scores(h + 1)
                ty = values(h)
            return ty

        def ffn_up(l):
            hT = big(0, 11264, 22)
            gp = [SCR[:, 514 * i:514 * i + 514] for i in range(2)]
            cv = [SCR[:, 1028 + 512 * i:1540 + 512 * i] for i in range(2)]
            tm = V.last
            for i in range(2):
                tm = memset(V, gp[i][:, 0:2], 0.0, A.last)
            cvfree = [[None], [None]]
            tp = PE.last
            for nb in range(11):
                bk = {}

                def ev(m, b, tok, nb=nb, bk=bk):
                    bk[m] = (b, tok)
                    if m < 2:
                        return
                    i = m - 2
                    j = 2 * nb + i
                    g, c = gp[i], cv[i]
                    b.free = a = act(g[:, 2:514], b.t[:, :], ACT.Copy, tok, tm, cvfree[i][0], chain=False)
                    ts(c, g[:, 2:514], vec(f"fcw{l}", 44 + j), None, ALU.mult, None, a)
                    stt(c, g[:, 1:513], vec(f"fcw{l}", 22 + j), c, ALU.mult, ALU.add)
                    r = stt(c, g[:, 0:512], vec(f"fcw{l}", j), c, ALU.mult, ALU.add)
                    a = act(c, c, ACT.Gelu_apprx_tanh, r, bias=vec(f"fcb{l}", j))
                    ba, ta = bk[i]
                    ba.free = cvfree[i][0] = tt(hT[:, j, :], c, ba.t[:, :], ALU.mult, a, ta, tp)

                proj_t(XH, XL, 4, 512, 4, ev, tx, t_vec)
            return V.last, PE.last

        def prep_k(prep, c):
            for kt in (2 * c, 2 * c + 1):
                s = kt % 8
                src = big(0, 11264, 22)[:, kt, :]
                prep[kt] = split(XH[:, s, :], XL[:, s, :], src, prep["src"], prep["free"].get(s))

        def prep_rel(prep, c, tok):
            for kt in (2 * c, 2 * c + 1):
                prep["free"][kt % 8] = tok

        def ffn_down(l, th, tup, tgb):
            free = {s: tup for s in range(8)}
            preps = [{"src": th, "free": free}, {"src": th, "free": free}]
            for j in range(2):
                pass
            return out_ln(lambda kt, t: (XH[:, kt % 8, 128 * t:128 * t + 128], XL[:, kt % 8, 128 * t:128 * t + 128]),
                          11, tgb, preps, l == 0)

        def layers():
            nonlocal tx, t_gb
            for l in range(2):
                ty = mixer_ab() if l == 0 else mixer_c()
                tx, tl = out_ln(xa_x, 4, t_gb, None, True, ty)
                t_gb = load_gb(I["ln_xa_g"][l], I["ln_xa_b"][l], tl)
                if stop == f"mix{l}":
                    return
                ty = cross(l)
                tx, tl = out_ln(xa_x, 4, t_gb, None, True, ty)
                t_gb = load_gb(I["ln_ffn_g"][l], I["ln_ffn_b"][l], tl)
                if stop == f"xa{l}":
                    return
                th, tup = ffn_up(l)
                tx, tl = ffn_down(l, th, tup, t_gb)
                if l == 0:
                    t_gb = load_gb(I["ln_mix_g"][1], I["ln_mix_b"][1], tl)
                if stop == f"ffn{l}":
                    return


        def second():
            nonlocal tx
            B = [big(2048 * i, 2048) for i in range(6)]
            L = [late(2048 * i, 2048) for i in range(4)]

            def v4(x):
                return x.rearrange("p (a b) -> p a b", a=4)

            V.wait(t_rel)
            mod = SM[:, 148:172]

            for nb in range(6):
                def ev_mod(m, b, tok, nb=nb):
                    j = 4 * nb + m
                    b.free = tt(mod[:, j:j + 1], b.t[:, 0:1], vec("ba", j), ALU.add, tok)
                proj_t(CH, CL, 4, 2, 4, ev_mod, t_c)
            s1 = SM[:, 172:180]
            t_mod = stt(s1, mod[:, 8:16], 1.0, VEC[:, vcol["ng"]:vcol["ng"] + 8], ALU.add, ALU.mult)

            ss = SM[:, 180:184]
            rq = SM[:, 184:188]
            xn = big(0, 4096, 4)
            junk = SCR[:, 0:1024]
            for t in range(4):
                a = act(junk, XR[:, t, :], ACT.Square, t_xr, accum_out=ss[:, t:t + 1])
            ts(ss, ss, 1.0 / D, 1e-6, ALU.mult, ALU.add, a, eng=G)
            r = tt(rq, ss, nhalf[:, 0:4], ALU.pow, eng=G)
            for t in range(4):
                a = act(xn[:, t, :], XR[:, t, :], ACT.Copy, r, V.last, PE.last, scale=rq[:, t:t + 1])
            t_spx = A.dma(d_x, XR[:, :, :], dsem(), t_xr)
            for k in range(8):
                b = bank()
                for t in range(4):
                    r = tr(b.t[:, 128 * t:128 * t + 128], xn[:, t, 128 * k:128 * k + 128], a, b.free, inc=t == 3)
                h = SCR[:, 1024 + 512 * (k % 2):1536 + 512 * (k % 2)]
                b.free = r = ts(h, b.t[:, :], s1[:, k:k + 1], mod[:, k:k + 1], ALU.mult, ALU.add, r, t_mod, A.last)
                tx = split(XH[:, k, :], XL[:, k, :], h, r)

            qtok, ktok, va, sga = v4(B[0]), v4(B[1]), v4(B[2]), v4(B[3])
            R, K, Vt, Gt = v4(B[4]), v4(B[5]), v4(L[0]), v4(L[1])
            wd = L[2][:, 0:512]
            w2a2 = L[2][:, 512:1024]
            ds = dsem()
            G.dma(w2a2[0:64, :], I["w2_2"][0], ds, V.last, A.last)
            t_w2 = G.dma(w2a2[64:128, :], I["a2_2"][0], ds)
            bias = GB[:, :].rearrange("p (h k) -> p h k", h=8)
            rev, exch = L[3], SCR[:, 2600:2728]
            G.dma(rev.rearrange("p (h k) -> p h k", h=8),
                  bass.AP(tensor=d_rel.tensor, offset=0, ap=[[1, 128], [384, 8], [1, 256]]), ds, t_rel)
            t_bi = G.dma(exch, I["cstd"], ds)
            for j in range(4):
                b = bank()
                rr = mm(b.t[:, :], exch, rev[:, 512 * j:512 * j + 512], True, True, t_bi, b.free, inc=True)
                b.free = act(GB[:, 512 * j:512 * j + 512], b.t[:, :], ACT.Copy, rr, t_xr)
            t_bi = memset(G, bias[0:64, :, 192:256], -1e30, b.free)
            tpr = [V.last, A.last, PE.last]

            for dst in (qtok, ktok, va):
                def ev_n(t, b, tok, dst=dst):
                    b.free = act(dst[:, t, :], b.t[:, :], ACT.Copy, tok, *tpr, chain=False)
                proj_n(xa_x, 4, ev_n, False, tx)
            t_qkv = A.last

            def silu2(o, b, tok):
                a = act(o, b.t[:, :], ACT.Tanh, tok, *tpr, scale=0.5)
                b.free = stt(o, o, 1.0, b.t[:, :], ALU.add, ALU.mult, a)

            def ev_ga(m, b, tok):
                silu2(sga[:, m, :], b, tok)
            proj_t(XH, XL, 4, 512, 4, ev_ga, tx)
            sh = [SCR[:, 520 * i:520 * i + 513] for i in range(2)]
            tsh = [memset(V, sh[i][:, 0:1], 0.0, A.last) for i in range(2)]

            def shift(o, b, tok, j):
                i = j % 2
                a = b.free = act(sh[i][:, 1:513], b.t[:, :], ACT.Copy, tok, tsh[i], *tpr)
                tt(o, sh[i][:, 0:512], sh[i][:, 1:513], ALU.subtract, a)
                tsh[i] = stt(o, o, vec("mu", j), sh[i][:, 1:513], ALU.mult, ALU.add)
                return tsh[i]

            for n, dst in enumerate((R, K, Vt, Gt)):
                def ev_s(m, b, tok, n=n, dst=dst):
                    r = shift(dst[:, m, :], b, tok, 4 * n + m)
                    if n == 3:
                        th = SCR[:, 1040 + 512 * (m % 2):1552 + 512 * (m % 2)]
                        a = act(th, dst[:, m, :], ACT.Tanh, r, scale=0.5)
                        stt(dst[:, m, :], th, 1.0, dst[:, m, :], ALU.add, ALU.mult, a)
                proj_t(XH, XL, 4, 512, 4, ev_s, tx)
            t_g = V.last
            t_spg = A.dma(d_g, L[1], dsem(), t_g)

            def ev_w(m, b, tok):
                r = shift(wd, b, tok, 16)
                act(wd[0:64, :], wd[0:64, :], ACT.Tanh, r)
            proj_t(XH, XL, 4, 512, 1, ev_w, tx)
            t_wd = A.last
            t_xfree = PE.last

            sq = SCR[:, 1040:2064].rearrange("p (i n) -> p i n", i=2)
            ssq = SM[:, 188:252].rearrange("p (i n) -> p i n", i=2)
            for i, x in enumerate((qtok, ktok)):
                for t in range(4):
                    a = act(sq[:, t % 2, :], x[:, t, :], ACT.Square, t_qkv, V.last)
                    r = V.op(lambda e, i=i, t=t: e.tensor_reduce(
                        ssq[:, i, 8 * t:8 * t + 8], sq[:, t % 2, :].rearrange("p (h d) -> p h d", h=8), AX.X, ALU.add), a)
            r = ts(SM[:, 188:252], SM[:, 188:252], 1.0 / 64, 1e-6, ALU.mult, ALU.add)
            a = act(SM[:, 188:252], SM[:, 188:252], ACT.Sqrt, r)
            V.op(lambda e: e.reciprocal(SM[:, 188:252], SM[:, 188:252]), a)
            qT, kT = v4(L[3]), v4(B[0])
            for i, (x, dst, g) in enumerate(((qtok, qT, "qg"), (ktok, kT, "kg"))):
                for t in range(4):
                    x3 = x[:, t, :].rearrange("p (h d) -> p h d", h=8)
                    s3 = ssq[:, i, 8 * t:8 * t + 8].unsqueeze(2).broadcast_to([P, 8, 64])
                    r = tt(x3, x3, s3, ALU.mult)
                for t in range(4):
                    b = bank()
                    for m in range(4):
                        rr = tr(b.t[:, 128 * m:128 * m + 128], x[:, t, 128 * m:128 * m + 128], r, b.free, inc=m == 3)
                    b.free = t_qk = ts(dst[:, :, 128 * t:128 * t + 128], b.t[:, :].rearrange("p (m n) -> p m n", m=4),
                                       vec(g), None, ALU.mult, None, rr)
            PT = v4(B[1])
            Sb = [SCR[:, 512 * i:512 * i + 512] for i in range(4)]
            am = SM[:, 132:140]
            asum = SM[:, 140:148]
            sb_free = [None] * 4
            t_pt = None
            yb = None
            for h in range(8):
                hp, par = h // 2, h % 2
                ps = slice(64 * par, 64 * par + 64)
                tp = []
                for q in range(4):
                    nk = 128 * (q + 1)
                    b = bank()
                    r = mm(b.t[:, 0:nk], qT[ps, hp, 128 * q:128 * q + 128], kT[ps, hp, 0:nk], True, True, t_qk, b.free,
                           inc=True)
                    s = Sb[q]
                    lo = max(0, nk - 256)
                    if lo:
                        ts(s[:, 0:lo], b.t[:, 0:lo], 0.125, bias[:, h, 0:1], ALU.mult, ALU.add, r, t_bi, sb_free[q])
                    b.free = stt(s[:, lo:nk], b.t[:, lo:nk], 0.125, bias[:, h, 256 - (nk - lo):256], ALU.mult, ALU.add,
                                 r, t_bi, sb_free[q])
                    V.op(lambda e, s=s, nk=nk, q=q: e.tensor_reduce(am[:, q:q + 1], s[:, 0:nk], AX.X, ALU.max))
                    r = ts(am[:, q:q + 1], am[:, q:q + 1], -1.0, None, ALU.mult, None)
                    a = act(s[:, 0:nk], s[:, 0:nk], ACT.Exp, r, bias=am[:, q:q + 1], accum_out=asum[:, q:q + 1])
                    V.op(lambda e, q=q: e.reciprocal(asum[:, q:q + 1], asum[:, q:q + 1]), a)
                    r = ts(s[:, 0:nk], s[:, 0:nk], asum[:, q:q + 1], None, ALU.mult, None)
                    b = bank()
                    for m in range(q + 1):
                        rr = tr(b.t[:, 128 * m:128 * m + 128], s[:, 128 * m:128 * m + 128], r, b.free, inc=m == q)
                    sb_free[q] = rr
                    b.free = act(PT[:, 0:q + 1, 128 * q:128 * q + 128],
                                 b.t[:, 0:nk].rearrange("p (m n) -> p m n", n=128), ACT.Copy, rr, t_pt)
                yb = bank()
                for m in range(4):
                    r = mm(yb.t[ps, 128 * m:512], va[:, m, 64 * h:64 * h + 64], PT[:, m, 128 * m:512], m == 0, m == 3,
                           A.last, t_qkv, yb.free, inc=m == 3)
                t_pt = r
                yb.free = r = stt(sga[ps, hp, :], sga[ps, hp, :], 0.5, yb.t[ps, :], ALU.mult, ALU.mult, r)
                if par == 1:
                    t_ya = split(XH[:, 4 + hp, :], XL[:, 4 + hp, :], sga[:, hp, :], r, t_xfree)

            cb = GB
            t_cb = G.dma(GB[:, 0:1824], I["cstb"], dsem(), V.last)
            mSU, mU, mL1 = cb[:, 0:128], cb[:, 128:256], cb[:, 256:384]
            mLT = [cb[:, 384 + 128 * i:512 + 128 * i] for i in range(6)]
            bones = cb[:, 1152:1280]
            sel = cb[:, 1280:1312].rearrange("p (a b) -> p a b", a=4)
            selT = cb[0:8, 1312:1824]
            smask = SCR[:, 0:512]
            t_sm = G.dma(smask, I["cstc"].partition_broadcast(P), dsem(), V.last, PE.last, A.last)
            hv = SM[:, 132:140]
            r = ts(hv, VEC[:, vcol["w0"]:vcol["w0"] + 8], 0.5, None, ALU.mult, None)
            oka = SM[:, 140:144]
            ts(oka, VEC[:, vcol["ka"]:vcol["ka"] + 4], -1.0, 1.0, ALU.mult, ALU.add)
            LW, AA, C, Pp = v4(B[0]), v4(B[1]), v4(B[2]), v4(B[3])
            tp = [PE.last, V.last, A.last]
            for m in range(4):
                for half, dst in ((0, LW), (1, AA)):
                    b = bank()
                    p = slice(64 * half, 64 * half + 64)
                    rr = mm(b.t[:, :], w2a2[p, 128 * m:128 * m + 128], wd[p, :], True, True, t_wd, t_w2, b.free, inc=True)
                    a = b.free = act(dst[:, m, :], b.t[:, :], ACT.Tanh, rr, r, *tp, scale=0.5,
                                     bias=hv[:, 4 * half + m:4 * half + m + 1])
                    if half == 0:
                        ts(dst[:, m, :], dst[:, m, :], -EM5 / 2, -EM5 / 2, ALU.mult, ALU.add, a)
                        V.op(lambda e, m=m: e.tensor_tensor_scan(C[:, m, :], smask, LW[:, m, :], 0.0, ALU.mult, ALU.add),
                             t_sm)
                    else:
                        ts(dst[:, m, :], dst[:, m, :], 0.5, 0.5, ALU.mult, ALU.add, a)
            r = tt(B[0], B[2], B[0], ALU.subtract)
            act(B[0], B[0], ACT.Exp, r)
            act(B[3], B[2], ACT.Exp)
            t_exp = act(B[2], B[2], ACT.Exp, scale=-1.0)
            Pm1, Pinv = v4(B[0]), v4(B[2])
            pC = SM[:, 188:220].rearrange("p (a c) -> p a c", a=4)
            V.op(lambda e: e.tensor_copy(pC, B[3].rearrange("p (a c k) -> p a c k", a=4, k=64)[:, :, :, 63]), t_exp)
            KK = v4(L[3])
            for m in range(4):
                ts(KK[:, m, :], K[:, m, :], vec("kk", m), None, ALU.mult, None)
            X = [XR[:, 0:2, :].rearrange("p a b -> p (a b)"), XR[:, 2:4, :].rearrange("p a b -> p (a b)")]
            r = tt(X[0], L[3], L[3], ALU.mult, t_spx)
            b = bank()
            for m in range(4):
                rr = mm(b.t[0:8, :], sel[:, m, :], v4(X[0])[:, m, :], m == 0, m == 3, r, t_cb, b.free, inc=m == 3)
            rs8 = SCR[0:8, 512:1024]
            b.free = r = ts(rs8, b.t[0:8, :], 1e-24, None, ALU.max, None, rr)
            a = act(rs8, rs8, ACT.Sqrt, r)
            r = V.op(lambda e: e.reciprocal(rs8, rs8), a)
            for m in range(4):
                b = bank()
                rr = mm(b.t[:, :], selT[:, 128 * m:128 * m + 128], rs8, True, True, r, b.free, inc=True)
                b.free = tt(KK[:, m, :], KK[:, m, :], b.t[:, :], ALU.mult, rr)
            for m in range(4):
                ts(v4(X[0])[:, m, :], AA[:, m, :], vec("ka", m), oka[:, m:m + 1], ALU.mult, ALU.add)
            tt(B[5], B[5], X[0], ALU.mult)
            ar = XR[:, :, :].rearrange("p a b -> p (a b)").rearrange("p (x s j) -> p x s j", s=2, j=64)
            k32 = "p (x j) -> p x j"
            stt(ar[:, :, 0, :], L[3].rearrange(k32, j=64), -1.0, B[0].rearrange(k32, j=64), ALU.mult, ALU.mult)
            tt(ar[:, :, 1, :], B[4].rearrange(k32, j=64), B[3].rearrange(k32, j=64), ALU.mult)
            tt(B[1], B[1], L[3], ALU.mult)
            tt(B[1], B[1], B[2], ALU.mult)
            tt(L[3], B[4], B[5], ALU.mult)
            rkb = v4(B[0][:, 0:512])
            for m in range(4):
                r = ts(rkb[:, m, :], bones, vec("rk", m), None, ALU.mult, None, t_cb)
            for m in range(4):
                b = bank()
                rr = mm(b.t[:, :], rkb[:, m, :], v4(L[3])[:, m, :], True, True, r, b.free, inc=True)
                b.free = r2 = tt(v4(B[3])[:, m, :], Vt[:, m, :], b.t[:, :], ALU.mult, rr)
            t_spb = A.dma(d_b, B[3], dsem(), r2)
            r = tt(B[5], B[5], B[2], ALU.mult)
            KtT, BtT = K, AA
            toks = {}
            for n, (src, dst) in enumerate(((Vt, v4(B[0])), (BtT, v4(B[2])), (KtT, v4(B[4])))):
                for t in range(4):
                    b = bank()
                    for m in range(4):
                        rr = tr(b.t[:, 128 * m:128 * m + 128], src[:, m, 128 * t:128 * t + 128], r, b.free, inc=m == 3)
                    b.free = act(dst[:, t, :], b.t[:, :], ACT.Copy, rr, r, r2)
            t_tok = A.last
            Vk, Bk, Kk = v4(B[0]), v4(B[2]), v4(B[4])
            ar5 = ar.rearrange("p (a c) s j -> p a c s j", a=4)

            TTc, RBc, NV, Y0 = v4(L[0]), v4(L[1]), v4(L[2]), v4(L[3])

            def tmp(x, par):
                return x[:, 512 * par:512 * par + 512].rearrange("p (m n) -> p m n", m=4)

            MTt, Tt = B[3][:, 0:1024], B[3][:, 1024:2048]
            TTt, Xt, Mk = SCR[:, 0:1024], SCR[:, 1024:2048], SCR[:, 2048:3072]

            def bc(m):
                return m.unsqueeze(1).broadcast_to([P, 4, 128])

            def b3(b):
                return b.t[:, :].rearrange("p (m n) -> p m n", m=4)

            t0 = [t_spb, t_spg, t_tok, PE.last, A.last, V.last]
            for t in range(4):
                for par in range(2):
                    ps = slice(64 * par, 64 * par + 64)
                    sl = slice(128 * t, 128 * t + 128)

                    def atok(s, m):
                        return ar5[ps, m, 2 * t:2 * t + 2, s, :]

                    def gram(l, r):
                        b = bank()
                        for m in range(4):
                            o = b.t[:, 128 * m:128 * m + 128]
                            rr = mm(o, l(m), r(m), True, True, b.free, *t0, inc=m == 3)
                        return b, rr

                    def bt(m):
                        return BtT[ps, m, sl]

                    def kt(m):
                        return KtT[ps, m, sl]

                    b, rr = gram(kt, lambda m: atok(0, m))
                    b.free = r = tt(tmp(Xt, par), b3(b), bc(mSU), ALU.mult, rr, PE.last)
                    bn, rr = gram(kt, lambda m: atok(1, m))
                    bn.free = r = tt(tmp(Mk, par), b3(bn), bc(mU), ALU.mult, rr, G.last)
                    b, rr = gram(bt, lambda m: atok(0, m))
                    b.free = tt(tmp(MTt, par), b3(b), bc(mSU), ALU.mult, rr, G.last)
                    b = bank()
                    for m in range(4):
                        for cp in range(2):
                            rr = mm(b.t[64 * cp:64 * cp + 64, 128 * m:128 * m + 128], ar5[ps, m, 2 * t + cp, 0, :], bt(m),
                                    True, True, b.free, inc=m == 3 and cp == 1)
                    b.free = tt(tmp(Tt, par), b3(b), bc(mL1), ALU.mult, rr)
                    tt(tmp(Tt, par), tmp(Tt, par), bc(ident), ALU.add)
                    tt(tmp(TTt, par), tmp(MTt, par), bc(mLT[0]), ALU.mult)
                    r2 = tt(tmp(TTt, par), tmp(TTt, par), bc(ident), ALU.add)
                    b, rr = gram(bt, lambda m: atok(1, m))
                    rb = RBc[:, t, :].rearrange("p (m q n) -> p m q n", q=2, n=64)
                    for cp in range(2):
                        pp = slice(64 * cp, 64 * cp + 64)
                        b.free = tt(rb[pp, :, par, :], b3(b)[pp, :, pp], mU[pp, pp].unsqueeze(1).broadcast_to([64, 4, 64]),
                                    ALU.mult, rr)
                    for src, dst in ((Xt, NV), (Mk, Y0)):
                        b = bank()
                        for m in range(4):
                            rr = mm(b.t[:, 64 * m:64 * m + 64], tmp(src, par)[:, m, :],
                                    Vk[:, t, 128 * m + 64 * par:128 * m + 64 * par + 64], True, True, r, b.free, inc=m == 3)
                        b.free = act(dst[:, t, :].rearrange("p (m q n) -> p m q n", q=2, n=64)[:, :, par, :],
                                     b.t[:, 0:256].rearrange("p (m n) -> p m n", m=4), ACT.Copy, rr)
                tpar = [V.last, V.last]
                for lv in range(1, 6):
                    for par in range(2):
                        g = tt(tmp(Mk, par), tmp(MTt, par), bc(mLT[lv]), ALU.mult, V.last, PE.last, eng=G)
                        b = bank()
                        for m in range(4):
                            rr = mm(b.t[:, 128 * m:128 * m + 128], tmp(Mk, par)[:, m, :], tmp(Tt, par)[:, m, :], True, True,
                                    g, tpar[par], b.free, inc=m == 3)
                        b.free = a = act(tmp(Xt, par), b3(b), ACT.Copy, rr)
                        b2 = bank()
                        for m in range(4):
                            rr = mm(b2.t[:, 128 * m:128 * m + 128], tmp(Xt, par)[:, m, :], tmp(TTt, par)[:, m, :],
                                    True, True, a, b2.free, inc=m == 3)
                        if lv < 5:
                            b = bank()
                            for m in range(4):
                                r1 = mm(b.t[:, 128 * m:128 * m + 128], tmp(TTt, par)[:, m, :], tmp(Xt, par)[:, m, :],
                                        True, True, a, b.free, inc=m == 3)
                            b.free = tt(tmp(Tt, par), tmp(Tt, par), b3(b), ALU.add, r1)
                            b2.free = tpar[par] = tt(tmp(TTt, par), tmp(TTt, par), b3(b2), ALU.add, rr)
                        else:
                            tc4 = TTc[:, t, :].rearrange("p (m q n) -> p m q n", q=2, n=64)
                            for cp in range(2):
                                pp = slice(64 * cp, 64 * cp + 64)
                                b2.free = tt(tc4[pp, :, par, :], tmp(TTt, par)[pp, :, pp], b3(b2)[pp, :, pp], ALU.add, rr)

            St = v4(B[3][:, 0:256])
            Us = [B[3][:, 512 + 512 * i:1024 + 512 * i] for i in range(2)]
            t_s = memset(V, B[3][:, 0:256], 0.0, PE.last)
            for c in range(8):
                t, cp = c // 2, c % 2
                pp = slice(64 * cp, 64 * cp + 64)
                nv = NV[pp, t, :].rearrange("p (m q n) -> p m q n", q=2, n=64)
                y0 = Y0[pp, t, :].rearrange("p (m q n) -> p m q n", q=2, n=64)
                wb = []
                for par in range(2):
                    b = bank()
                    ps = slice(64 * par, 64 * par + 64)
                    for m in range(4):
                        rr = mm(b.t[:, 64 * m:64 * m + 64], ar5[ps, m, c, :, :].rearrange("p s j -> p (s j)"), St[ps, m, :],
                                True, True, t_s, b.free, A.last, inc=m == 3)
                    w3 = b.t[:, 0:256].rearrange("p (m n) -> p m n", m=4)
                    r = tt(nv[:, :, par, :], nv[:, :, par, :], w3[0:64], ALU.add, rr)
                    wb.append((b, w3))
                b = bank()
                for h in range(8):
                    hs = slice(64 * h, 64 * h + 64)
                    rr = mm(b.t[pp, hs], TTc[pp, t, hs], NV[pp, t, hs], True, True, r, b.free, inc=h == 7)
                U = Us[c % 2]
                b.free = a = act(U[pp, :], b.t[pp, :], ACT.Copy, rr)
                bd = bank()
                for m in range(4):
                    hs = slice(128 * m, 128 * m + 128)
                    mm(bd.t[:, hs], Kk[pp, t, hs], Vk[pp, t, hs], True, False, a, bd.free)
                    rr = mm(bd.t[:, hs], Bk[pp, t, hs], U[pp, hs], False, True, inc=m == 3)
                by = bank()
                for h in range(8):
                    hs = slice(64 * h, 64 * h + 64)
                    ry = mm(by.t[pp, hs], RBc[pp, t, hs], U[pp, hs], True, True, a, by.free, inc=h == 7)
                d3 = b3(bd)
                for par in range(2):
                    ps = slice(64 * par, 64 * par + 64)
                    bd.free = tt(St[ps, :, :], St[ps, :, :], d3[ps, :, ps], ALU.add, rr)
                t_s = tt(St, St, pC[:, :, c].unsqueeze(2).broadcast_to([P, 4, 64]), ALU.mult)
                for par in range(2):
                    wb[par][0].free = tt(y0[:, :, par, :], y0[:, :, par, :], wb[par][1][64:128], ALU.add)
                by.free = tt(Y0[pp, t, :], Y0[pp, t, :], by.t[pp, :], ALU.add, ry)

            t_g = A.dma(B[1], d_g, dsem(), t_spg, PE.last)
            t_b = A.dma(B[5], d_b, dsem(), t_spb, PE.last)
            t_x = A.dma(XR[:, :, :], d_x, dsem(), t_spx, PE.last)
            y32 = L[3].rearrange("p (x j) -> p x j", j=64)
            gs, gm = SM[:, 188:220], SM[:, 220:252]
            V.op(lambda e: e.tensor_reduce(gm, y32, AX.X, ALU.add))
            ts(gm, gm, 1.0 / 64, None, ALU.mult, None)
            r = tt(y32, y32, gm.unsqueeze(2).broadcast_to([P, 32, 64]), ALU.subtract)
            a = act(L[2], L[3], ACT.Square, r)
            V.op(lambda e: e.tensor_reduce(gs, L[2].rearrange("p (x j) -> p x j", j=64), AX.X, ALU.add), a)
            r = ts(gs, gs, 1.0 / 64, 64e-5, ALU.mult, ALU.add)
            a = act(gs, gs, ACT.Sqrt, r)
            V.op(lambda e: e.reciprocal(gs, gs), a)
            r = tt(y32, y32, gs.unsqueeze(2).broadcast_to([P, 32, 64]), ALU.mult)
            yT = v4(B[2])
            for m in range(4):
                b = bank()
                for t in range(4):
                    rr = tr(b.t[:, 128 * t:128 * t + 128], Y0[:, t, 128 * m:128 * m + 128], r, b.free, inc=t == 3)
                y = yT[:, m, :]
                b.free = ts(y, b.t[:, :], vec("lxg", m), vec("lxb", m), ALU.mult, ALU.add, rr)
                tt(y, y, v4(B[5])[:, m, :], ALU.add, t_b)
                ry = stt(y, y, 0.5, v4(B[1])[:, m, :], ALU.mult, ALU.mult, t_g)
                ty = split(XH[:, m, :], XL[:, m, :], y, ry, t_xfree)

            ones = SCR[:, 0:128]
            dg = SCR[:, 1024:2048].rearrange("p (k n) -> p k n", k=8)
            gate = B[0][:, 0:1024]
            memset(V, ones, 1.0, PE.last)
            for k in range(8):
                r = ts(dg[:, k, :], ident, mod[:, 16 + k:17 + k], None, ALU.mult, None)
            for j in range(2):
                b = bank()
                for k in range(4):
                    rr = mm(b.t[:, 128 * k:128 * k + 128], ones, dg[:, 4 * j + k, :], True, True, r, b.free, inc=k == 3)
                b.free = act(gate[:, 512 * j:512 * j + 512], b.t[:, :], ACT.Copy, rr, r)
            t_gt = A.last
            o = out[0].rearrange("(a p) n -> p a n", p=P)
            ods = dsem()
            fin = []
            for j in range(2):
                def ev_o(t, b, tok, j=j):
                    cs = slice(512 * j, 512 * j + 512)
                    x = B[4 + (t % 2)][:, 1024:1536] if False else GB[:, 512 * (t % 4):512 * (t % 4) + 512]
                    b.free = tt(x, b.t[:, :], gate[:, cs], ALU.mult, tok, t_gt)
                    r = tt(XR[:, t, cs], XR[:, t, cs], x, ALU.add, t_x)
                    fin.append(A.dma(o[:, t, cs], XR[:, t, cs], ods, r))
                proj_n(xa_x, 4, ev_o, True, ty, t_ya)
            A.wait(fin[-1])

        cc = VEC[:, vcol["c"]:vcol["c"] + 8]
        cs1 = SM[:, 148:156]
        a = act(cs1, cc, ACT.Tanh, t_vec, scale=0.5)
        ts(cs1, cs1, 0.5, 0.5, ALU.mult, ALU.add, a)
        tt(cs1, cs1, cc, ALU.mult)
        r = V.op(lambda e: e.tensor_copy(CH[:, :, :], cs1.unsqueeze(2).broadcast_to([P, 8, 2])))
        t_c = tt(CL[:, :, :], cs1.unsqueeze(2).broadcast_to([P, 8, 2]), CH[:, :, :].bitcast(F), ALU.subtract)
        rp = big(11500, 384)[0:8, :]
        r = A.dma(rp[:, 127:319], I["rel_rev"], dsem())
        V.op(lambda e: e.tensor_copy(rp[:, 0:127], rp[:, 127:128].broadcast_to([8, 127])), r)
        r = V.op(lambda e: e.tensor_copy(rp[:, 319:384], rp[:, 318:319].broadcast_to([8, 65])))
        t_rel = A.dma(d_rel, rp, dsem(), r)
        layers()
        t_xr = V.last
        if stop:
            finish(XR[:, :, :])
        else:
            second()

        block = ctx.enter_context(nc.Block())

        def play(eng):
            def f(e):
                for g in eng.q:
                    g(e)
            return f

        block.tensor(play(PE))
        block.vector(play(V))
        block.scalar(play(A))
        block.gpsimd(play(G))
        block.sync(play(S))


_INS = ["x", "mem", "ab_w_in", "sgu_ln_g", "sgu_ln_b", "sgu_w", "sgu_b", "pool_w", "pool_scale", "ab_w_out",
        "c_w_in", "c_conv_w", "c_w_out", "ln_mix_g", "ln_mix_b", "xa_wq", "xa_wkv", "xa_wo", "ln_xa_g", "ln_xa_b",
        "ffn_w_up", "ffn_conv_w", "ffn_conv_b", "ffn_w_down", "ln_ffn_g", "ln_ffn_b", "c_2", "norm_g_2", "w_ada_2",
        "b_ada_2", "w_in_2", "mu_shift_2", "w0_2", "w2_2", "a0_2", "a2_2", "k_k_2", "k_a_2", "r_k_2", "lnx_g_2",
        "lnx_b_2", "q_norm_g_2", "k_norm_g_2", "rel_bias_2", "w_out_2"]


def constants():
    import numpy as np
    cst = np.zeros((128, 144), np.float32)
    cst[:, 0:128] = np.eye(128)
    cst[:, 128:144] = 1.0 / np.arange(1, 17)
    t = np.arange(128)
    s, q = t[:, None], t[None, :]
    same = s // 64 == q // 64

    def level(row, col, n):
        return (row // (2 * n) == col // (2 * n)) & (row // n % 2 == 1) & (col // n % 2 == 0)

    cb = np.zeros((128, 1824), np.float32)
    cb[:, 0:128] = same & (s < q)
    cb[:, 128:256] = same & (s <= q)
    cb[:, 256:384] = level(s, q, 1)
    for i in range(6):
        cb[:, 384 + 128 * i:512 + 128 * i] = level(q, s, 1 << i)
    cb[:, 1152:1280] = same
    for m in range(4):
        for p in range(2):
            cb[64 * p:64 * p + 64, 1280 + 8 * m + 2 * m + p] = 1
            cb[2 * m + p, 1312 + 128 * m + 64 * p:1312 + 128 * m + 64 * p + 64] = 1
    cc = np.ones(512, np.float32)
    cc[0::64] = 0
    return {"cst": cst, "cstb": cb, "cstc": cc, "cstd": np.ascontiguousarray(np.eye(128, dtype=np.float32)[::-1])}


def kernel(**inputs):
    import numpy as _np
    import concourse.bacc as _bacc
    from concourse import mybir as _mybir
    from concourse.bass_utils import run_bass_kernel_spmd as _run

    nc = _bacc.Bacc("TRN2", target_bir_lowering=False, num_devices=1)
    arrays, I = {}, {}
    for name in _INS:
        arrays[name] = _np.ascontiguousarray(inputs[name])
    arrays["rel_rev"] = _np.ascontiguousarray(inputs["rel_bias_2"][0, :, ::-1])
    arrays.update(constants())
    for name, a in arrays.items():
        I[name] = nc.dram_tensor(name, a.shape, _mybir.dt.from_np(a.dtype), kind="ExternalInput").ap()
    o = nc.dram_tensor("out0", (1, 512, 1024), F, kind="ExternalOutput").ap()
    build(nc, I, o)
    r = _run(nc, [arrays], core_ids=[0])
    return r.results[0]["out0"]
```

```python
from contextlib import ExitStack

import concourse.bass as bass
from concourse import mybir

F = mybir.dt.float32
FR = mybir.dt.float32r
ALU = mybir.AluOpType
ACT = mybir.ActivationFunctionType
AX = mybir.AxisListType

P = 128
D = 1024
T = 512
MEM = 256
DFF = 2816
ALPHA = 4.0 ** 0.25
NR = 4
NH = 5
EM5 = 0.6065306597126334


class Eng:

    def __init__(self, name, sem):
        self.name, self.sem, self.n, self.q, self.seen, self.last = name, sem, 0, [], {}, None

    def wait(self, *toks):
        for t in toks:
            if t is None:
                continue
            if isinstance(t, list):
                self.wait(*t)
                continue
            sem, v = t
            if self.seen.get(id(sem), 0) >= v:
                continue
            self.seen[id(sem)] = v
            self.q.append(lambda e, s=sem, k=v: e.wait_ge(s, k))

    def op(self, f, *toks, chain=True, inc=True):
        self.wait(*toks)
        if chain:
            self.wait(self.last)
        if not inc:
            self.q.append(f)
            return None
        self.n += 1
        self.q.append(lambda e, g=f, s=self.sem: g(e).then_inc(s, 1))
        self.last = (self.sem, self.n)
        return self.last

    def dma(self, dst, src, ds, *toks):
        self.wait(*toks)
        ds.n += 16
        self.q.append(lambda e: e.dma_start(dst, src).then_inc(ds.sem, 16))
        return (ds.sem, ds.n)


class Count:
    def __init__(self, sem):
        self.sem, self.n = sem, 0


class Bank:

    def __init__(self, t):
        self.t, self.held, self.tok = t, False, None

    @property
    def free(self):
        return self.tok

    @free.setter
    def free(self, tok):
        self.tok, self.held = tok, False



VEC_ROWS = [("fcw0", 66), ("fcw1", 66), ("fcb0", 22), ("fcb1", 22), ("ccw", 24), ("psc", 4), ("mu", 17),
            ("w0", 4), ("a0", 4), ("kk", 4), ("ka", 4), ("rk", 4), ("lxg", 4), ("lxb", 4), ("ng", 8),
            ("c", 8), ("ba", 24), ("qg", 1), ("kg", 1)]


def build(nc, I, out, stop=None, dbg=None):
    ctx = ExitStack()
    with ctx:
        def sb(name, shape, dt=F):
            return ctx.enter_context(nc.sbuf_tensor(name, shape, dt))

        def sem(name):
            return ctx.enter_context(nc.semaphore(name))

        PE = Eng("tensor", sem("s_pe"))
        V = Eng("vector", sem("s_v"))
        A = Eng("scalar", sem("s_a"))
        G = Eng("gpsimd", sem("s_g"))
        S = Eng("sync", sem("s_s"))
        nds = [0]

        def dsem():
            nds[0] += 1
            return Count(sem(f"s_d{nds[0]}"))

        XR = sb("XR", [P, 4, D])
        XH = sb("XH", [P, 8, T], FR)
        XL = sb("XL", [P, 8, T], FR)
        RAW = [sb(f"RAW{i}", [P, 2, 512]) for i in range(NR)]
        WH = [sb(f"WH{i}", [P, 2, 512], FR) for i in range(NH)]
        WL = [sb(f"WL{i}", [P, 2, 512], FR) for i in range(NH)]
        GB = sb("GB", [P, 2048])
        BIG = sb("BIG", [P, 12288])
        LATE = sb("LATE", [P, 8192])
        SCR = sb("SCR", [P, 3136])
        CST = sb("CST", [P, 144])
        VEC = sb("VEC", [P, 384])
        SM = sb("SM", [P, 256])
        d_x = nc.dram_tensor("spill_x", (P, 4096), F, kind="Internal").ap()
        d_g = nc.dram_tensor("spill_g", (P, 2048), F, kind="Internal").ap()
        d_b = nc.dram_tensor("spill_b", (P, 2048), F, kind="Internal").ap()
        d_rel = nc.dram_tensor("rel_padded", (8, 384), F, kind="Internal").ap()
        ident = CST[:, 0:128]
        invc = CST[:, 128:144]
        banks = [Bank(ctx.enter_context(nc.psum_tensor(f"ps{i}", [P, 512], F))) for i in range(8)]
        nbk = [0]

        def bank():
            for _ in range(8):
                b = banks[nbk[0] % 8]
                nbk[0] += 1
                if not b.held:
                    b.held = True
                    return b
            raise RuntimeError("all PSUM banks are held")

        def big(off, n, a=None):
            v = BIG[:, off:off + n]
            return v if a is None else v.rearrange("p (a b) -> p a b", a=a)

        def late(off, n, a=None):
            v = LATE[:, off:off + n]
            return v if a is None else v.rearrange("p (a b) -> p a b", a=a)

        chunks = []

        def w_cols(w, k0, pieces, whole=False):
            v = w[k0:k0 + 256, :].rearrange("(k p) n -> p k n", p=P)
            at, got = 0, []
            for c0, n in pieces:
                got.append((at, n, v[:, :, c0:c0 + n]))
                at += n
            chunks.append((got, at, whole))

        def w_block(w, c0, n=512, rows=1024, whole=False):
            for k in range(0, rows, 256):
                w_cols(w, k, [(c0, n)], whole)

        for l in range(2):
            for b in range(4):
                w_block(I["xa_wkv"][l], 512 * b)
        for l in range(2):
            if l == 0:
                for c0 in (512, 0, 1024):
                    w_block(I["ab_w_in"][0], c0)
                for b in range(2):
                    w_block(I["ab_w_out"][0], 512 * b)
            else:
                for c0 in (1024, 2048, 1536, 2560, 0, 512):
                    w_block(I["c_w_in"][0], c0)
                for b in range(2):
                    w_block(I["c_w_out"][0], 512 * b)
            for w in ("xa_wq", "xa_wo"):
                for b in range(2):
                    w_block(I[w][l], 512 * b)
            for i in range(11):
                for k in range(0, 1024, 256):
                    w_cols(I["ffn_w_up"][l], k, [(256 * i, 256), (DFF + 256 * i, 256)])
            for b in range(2):
                w_block(I["ffn_w_down"][l], 512 * b, rows=DFF)
        for b in range(6):
            w_block(I["w_ada_2"][0], 512 * b, whole=True)
        for c0, n in ((2176, 512), (2688, 512), (3200, 512), (3712, 512),
                      (0, 512), (512, 512), (1024, 512), (1536, 512), (2048, 128)):
            w_block(I["w_in_2"][0], c0, n)
        for b in range(2):
            w_block(I["w_out_2"][0], 512 * b)

        raw_ds = [dsem() for _ in range(NR)]
        split_no = []
        for i, c in enumerate(chunks):
            if not c[2]:
                split_no.append(i)
        slot_of = {i: n for n, i in enumerate(split_no)}
        dma_tok, conv_tok, rel_tok = {}, {}, {}
        pos = {"dma": 0, "conv": 0, "get": 0}

        def w_pump():
            while True:
                moved = False
                i = pos["dma"]
                old = i - NR
                free = None if old < 0 else (rel_tok if chunks[old][2] else conv_tok).get(old)
                if i < len(chunks) and (old < 0 or free):
                    for at, n, src in chunks[i][0]:
                        dma_tok[i] = S.dma(RAW[i % NR][:, :, at:at + n], src, raw_ds[i % NR], free)
                    pos["dma"] += 1
                    moved = True
                h = pos["conv"]
                if h < len(split_no) and split_no[h] in dma_tok and (h < NH or split_no[h - NH] in rel_tok):
                    i = split_no[h]
                    n = chunks[i][1]
                    raw, hi, lo = RAW[i % NR][:, :, 0:n], WH[h % NH][:, :, 0:n], WL[h % NH][:, :, 0:n]
                    rel = rel_tok[split_no[h - NH]] if h >= NH else None
                    th = A.op(lambda e, hi=hi, raw=raw: e.activation(hi, raw, ACT.Copy), dma_tok[i], rel, chain=False)
                    conv_tok[i] = V.op(lambda e, hi=hi, lo=lo, raw=raw: e.tensor_tensor(lo, raw, hi.bitcast(F), ALU.subtract),
                                       th, chain=False)
                    pos["conv"] += 1
                    moved = True
                if not moved:
                    return

        def w_get():
            i = pos["get"]
            pos["get"] += 1
            if chunks[i][2]:
                return i, RAW[i % NR], None, dma_tok[i]
            h = slot_of[i]
            return i, WH[h % NH], WL[h % NH], conv_tok[i]

        def w_release(i, tok, pump=True):
            rel_tok[i] = tok
            if pump:
                w_pump()

        npe = [0]

        def mark(name):
            pass

        def mm(o, l, r, start, stop, *toks, inc=False):
            npe[0] += 1
            return PE.op(lambda e: e.matmul(o, l, r, start=start, stop=stop), *toks, chain=False, inc=inc)

        def mm3(o, lh, ll, rh, rl, start, stop, *toks, inc=False):
            mm(o, lh, rh, start, False, *toks)
            mm(o, lh, rl, False, False)
            return mm(o, ll, rh, False, stop, inc=inc)

        def tr(o, i, *toks, inc=False, n=128):
            npe[0] += 1
            return PE.op(lambda e: e.transpose(o, i, ident[0:n, 0:n]), *toks, chain=False, inc=inc)

        def act(o, i, f, *toks, chain=True, **kw):
            return A.op(lambda e: e.activation(o, i, f, **kw), *toks, chain=chain)

        def tt(o, a, b, op, *toks, eng=None, chain=True):
            return (eng or V).op(lambda e: e.tensor_tensor(o, a, b, op), *toks, chain=chain)

        def ts(o, a, s1, s2, op0, op1, *toks, eng=None, chain=True):
            if s2 is None:
                return (eng or V).op(lambda e: e.tensor_scalar(o, a, s1, None, op0), *toks, chain=chain)
            return (eng or V).op(lambda e: e.tensor_scalar(o, a, s1, s2, op0, op1), *toks, chain=chain)

        def stt(o, a, s, b, op0, op1, *toks, chain=True):
            return V.op(lambda e: e.scalar_tensor_tensor(out=o, in0=a, scalar=s, in1=b, op0=op0, op1=op1),
                        *toks, chain=chain)

        def memset(eng, o, v, *toks):
            return eng.op(lambda e: e.memset(o, v), *toks)

        def split(hi, lo, src, *toks):
            th = act(hi, src, ACT.Copy, *toks, chain=False)
            return tt(lo, src, hi.bitcast(F), ALU.subtract, th, *toks, chain=False)

        def proj_t(xh, xl, nk2, ntok, nm, evac, *toks, late=None):
            if late:
                for t in (0, 1):
                    t_h = late(t)
                bs = [bank() for _ in range(nm)]
                gots = [w_get() for _ in range(nk2)]
                for half in range(2):
                    if half:
                        for t in (2, 3):
                            t_h = late(t)
                    cs = slice(256 * half, 256 * half + 256)
                    done = []
                    for c, (i, wh, wl, tok) in enumerate(gots):
                        for m in range(nm):
                            for k in range(2):
                                kt = 2 * c + k
                                last = c == nk2 - 1 and k == 1
                                t = mm3(bs[m].t[:, cs], wh[:, k, 128 * m:128 * m + 128], wl[:, k, 128 * m:128 * m + 128],
                                        xh[:, kt, cs], xl[:, kt, cs], kt == 0, last, tok, t_h,
                                        bs[m].free if kt == 0 else None, *toks,
                                        inc=last or (m == nm - 1 and k == 1))
                                if last:
                                    done.append(t)
                        if half:
                            w_release(i, t)
                for m in range(nm):
                    evac(m, bs[m], done[m])
                return t_h
            bs = [bank() for _ in range(nm)]
            done = []
            for c in range(nk2):
                i, wh, wl, tok = w_get()
                for m in range(nm):
                    for k in range(2):
                        kt = 2 * c + k
                        last = c == nk2 - 1 and k == 1
                        t = mm3(bs[m].t[:, 0:ntok], wh[:, k, 128 * m:128 * m + 128], wl[:, k, 128 * m:128 * m + 128],
                                xh[:, kt, 0:ntok], xl[:, kt, 0:ntok], kt == 0, last, tok,
                                bs[m].free if kt == 0 else None, *toks, inc=last or (m == nm - 1 and k == 1))
                        if last:
                            done.append(t)
                w_release(i, t)
            for m in range(nm):
                evac(m, bs[m], done[m])

        def proj_n(xa, nk2, evac, final, *toks, nt=4, kt_tok=None, ahead=None, done_k=None):
            bs = [bank() for _ in range(nt)]
            done = []
            cut = nk2 - 4 if final else nk2

            def part(c, got, t):
                i, wh, wl, tok = got
                for k in range(2):
                    kt = 2 * c + k
                    xh, xl = xa(kt, t)
                    last = c == nk2 - 1 and k == 1
                    r = mm3(bs[t].t[:, :], xh, xl, wh[:, k, :], wl[:, k, :], kt == 0, last, tok,
                            bs[t].free if kt == 0 else None, kt_tok[kt] if kt_tok else None, *toks,
                            inc=last or (t == nt - 1 and k == 1))
                return r

            for c in range(cut):
                got = w_get()
                for t in range(nt):
                    r = part(c, got, t)
                    if c == nk2 - 1:
                        done.append(r)
                if done_k:
                    done_k(c, r)
                w_release(got[0], r)
                if ahead:
                    ahead(c + 3)
            if not final:
                for t in range(nt):
                    evac(t, bs[t], done[t])
                return
            gots = [w_get() for _ in range(4)]
            if ahead:
                ahead(nk2 - 1)
            rels = {}
            for t in range(nt):
                for c in range(cut, nk2):
                    r = part(c, gots[c - cut], t)
                    rels[c] = r
                if t == nt - 1:
                    for c in range(cut, nk2):
                        if done_k:
                            done_k(c, rels[c])
                        w_release(gots[c - cut][0], rels[c])
                evac(t, bs[t], r)

        tc = A.dma(CST[:, :], I["cst"], dsem())
        t_mem = A.dma(big(0, 2048, 2), I["mem"][0].rearrange("(a p) n -> p a n", p=P), dsem())
        xin = dsem()
        t_x = A.dma(XR[:, :, :], I["x"][0].rearrange("(a p) n -> p a n", p=P), xin)

        def rows(name):
            r = {
                "fcw0": I["ffn_conv_w"][0].rearrange("k (m c) -> (k m) c", c=P),
                "fcw1": I["ffn_conv_w"][1].rearrange("k (m c) -> (k m) c", c=P),
                "ccw": I["c_conv_w"][0].rearrange("k (m c) -> (k m) c", c=P),
            }
            if name in r:
                return [r[name]]
            if name in ("qg", "kg"):
                v = I["q_norm_g_2" if name == "qg" else "k_norm_g_2"]
                return [v, v]
            v = {
                "fcb0": I["ffn_conv_b"][0:1], "fcb1": I["ffn_conv_b"][1:2], "psc": I["pool_scale"],
                "mu": I["mu_shift_2"], "w0": I["w0_2"], "a0": I["a0_2"], "kk": I["k_k_2"], "ka": I["k_a_2"],
                "lxg": I["lnx_g_2"], "lxb": I["lnx_b_2"], "ng": I["norm_g_2"], "c": I["c_2"],
                "ba": I["b_ada_2"],
            }
            if name == "rk":
                return [I["r_k_2"][0].rearrange("(a b) c -> a (b c)", b=2)]
            return [v[name].rearrange("a (m c) -> (a m) c", c=P)]

        vcol = {}
        r0 = 0
        vds = dsem()
        stg = big(2048, 384, 3)
        t_vm = memset(V, stg, 0.0)
        for name, n in VEC_ROWS:
            vcol[name] = r0
            aps = rows(name)
            if len(aps) == 2:
                for h, a in enumerate(aps):
                    t_v = A.dma(stg[r0 % 128:r0 % 128 + 1, r0 // 128, 64 * h:64 * h + 64], a, vds, t_vm)
            else:
                a, at = aps[0], 0
                while at < n:
                    m = min(n - at, 128 - (r0 + at) % 128)
                    t_v = A.dma(stg[(r0 + at) % 128:(r0 + at) % 128 + m, (r0 + at) // 128, :], a[at:at + m, :], vds, t_vm)
                    at += m
            r0 += n
        assert r0 <= 384

        def vec(name, j=0):
            return VEC[:, vcol[name] + j:vcol[name] + j + 1]

        w_pump()
        nhalf = SM[:, 0:32]
        memset(V, nhalf, -0.5)
        t_nh = memset(V, SM[:, 32:64], 0.0)
        b = bank()
        for j in range(3):
            t = tr(b.t[:, 128 * j:128 * j + 128], stg[:, j, :], tc, t_v, t_vm, inc=j == 2)
        t_vec = b.free = V.op(lambda e, b=b: e.tensor_copy(VEC[:, :], b.t[:, 0:384]), t)

        def transposes(src, nt, n0=0, *toks):
            for t in range(n0, n0 + nt):
                for q in range(2):
                    b = bank()
                    for k in range(4):
                        r = tr(b.t[:, 128 * k:128 * k + 128], src(t, 4 * q + k), b.free, *toks, inc=k == 3)
                    b.free = split(XH[:, 4 * q:4 * q + 4, 128 * t:128 * t + 128],
                                   XL[:, 4 * q:4 * q + 4, 128 * t:128 * t + 128],
                                   b.t[:, :].rearrange("p (k n) -> p k n", k=4), r)
            return b.free

        memt = big(0, 2048, 2)
        tx = transposes(lambda t, k: memt[:, t, 128 * k:128 * k + 128], 2, 0, tc, t_mem)
        KT = [late(4096 * l, 2048, 8) for l in range(2)]
        VT = [late(4096 * l + 2048, 2048, 2) for l in range(2)]
        for l in range(2):
            for nb in range(2):
                def evk(m, b, tok, l=l, nb=nb):
                    b.free = act(KT[l][:, 4 * nb + m, :], b.t[:, 0:256], ACT.Copy, tok, chain=False)
                proj_t(XH, XL, 4, 256, 4, evk, tx)
            for nb in range(2):
                def evv(t, b, tok, l=l, nb=nb):
                    b.free = act(VT[l][:, t, 512 * nb:512 * nb + 512], b.t[:, :], ACT.Copy, tok, chain=False)
                proj_n(lambda kt, t: (XH[:, kt, 128 * t:128 * t + 128], XL[:, kt, 128 * t:128 * t + 128]), 4, evv,
                       False, tx, nt=2)
        t_kv = A.last

        def xa_x(kt, t):
            return XH[:, kt, 128 * t:128 * t + 128], XL[:, kt, 128 * t:128 * t + 128]

        def load_gb(g, b, tok, n=D):
            ds = dsem()
            G.dma(GB[:, 0:n], g.partition_broadcast(P), ds, tok)
            return G.dma(GB[:, 1024:1024 + n], b.partition_broadcast(P), ds, tok)

        stats = SM[:, 64:112].rearrange("p (t j s) -> p t j s", t=4, j=2)
        mv = SM[:, 112:120].rearrange("p (t s) -> p t s", s=2)
        vr = SM[:, 120:124]
        rs = SM[:, 124:128]
        nmr = SM[:, 128:132]

        def rstd(t, nstat, dst_rs):
            st = stats[:, t, 0:nstat, :]
            a = V.op(lambda e: e.bn_aggr(mv[:, t, :], st))
            ts(vr[:, t:t + 1], mv[:, t, 1:2], 1e-5, None, ALU.add, None, a, eng=G)
            r = tt(dst_rs, vr[:, t:t + 1], nhalf[:, 0:1], ALU.pow, t_nh, eng=G)
            return stt(nmr[:, t:t + 1], mv[:, t, 0:1], -1.0, dst_rs, ALU.mult, ALU.mult, r)

        def ln_in(j, t, b, tok):
            o = XR[:, t, 512 * j:512 * j + 512]
            b.free = stt(o, o, ALPHA, b.t[:, :], ALU.mult, ALU.add, tok)
            return V.op(lambda e: e.bn_stats(stats[:, t, j, :], o))

        def ln_out(t, tgb, turn=True):
            r = rstd(t, 2, rs[:, t:t + 1])
            x = XR[:, t, :]
            a = act(x, x, ACT.Identity, r, scale=rs[:, t:t + 1], bias=nmr[:, t:t + 1])
            tt(x, x, GB[:, 0:1024], ALU.mult, a, tgb)
            r = tt(x, x, GB[:, 1024:2048], ALU.add)
            return r

        def turn(t):
            return transposes(lambda t, k: XR[:, t, 128 * k:128 * k + 128], 1, t, lnr[t])

        lnr = {}

        def out_ln(xa, nk2, tgb, kt_tok=None, prep=None):
            for j in range(2):
                def ev(t, b, tok, j=j):
                    ln_in(j, t, b, tok)
                    if j == 1:
                        lnr[t] = ln_out(t, tgb)
                p = prep[j] if prep else {}
                if prep and j == 0:
                    for c in range(3):
                        prep[0]["ahead"](c)
                if prep and j == 1:
                    for c in range(3):
                        prep[1]["ahead"](c)
                proj_n(xa, nk2, ev, j == 1, kt_tok=p.get("tok", kt_tok), ahead=p.get("ahead"), done_k=p.get("done"))
            return lnr[3]

        stopped = [False]

        def finish(src, n=4096):
            ds = dsem()
            o = out[0].rearrange("(a p) n -> p a n", p=P)
            t = S.dma(o, src, ds, PE.last, V.last, A.last, G.last)
            S.wait(t)
            stopped[0] = True

        mark("kv")
        t_gb = load_gb(I["ln_mix_g"][0], I["ln_mix_b"][0], None)
        tx = transposes(lambda t, k: XR[:, t, 128 * k:128 * k + 128], 4, 0, t_x)

        def mixer_ab():
            nonlocal tx
            uT = big(0, 2048, 4)
            vt = big(2048, 2048, 4)
            xb = big(4096, 2112, 4)
            pp = [big(6208 + 528 * i, 528) for i in range(2)]
            pooled = big(7264, 2048, 4)
            wraw = big(9312, 512, 4)
            wmT = big(9824, 512, 4)
            bs = big(10336, 512, 4)
            pw = big(10848, 512, 4)
            lg = SCR[:, 0:512]
            lb = SCR[:, 512:1024]
            ytmp = SCR[:, 1024:1536]
            ds = dsem()
            G.dma(wraw, I["sgu_w"][0].rearrange("g i j -> i g j"), ds, V.last, PE.last)
            G.dma(bs, I["sgu_b"][0].partition_broadcast(P), ds)
            G.dma(pw, I["pool_w"][0].rearrange("g c d -> c g d"), ds)
            G.dma(lg, I["sgu_ln_g"][0].partition_broadcast(P), ds)
            t_l = G.dma(lb, I["sgu_ln_b"][0].partition_broadcast(P), ds)
            tm = memset(G, xb[:, :, 0:16], 0.0, V.last, PE.last)
            memset(G, pp[0][:, 0:16], 0.0)
            tm = memset(G, pp[1][:, 0:16], 0.0)

            def ev_v(t, b, tok):
                o = vt[:, t, :]
                a = b.free = act(o, b.t[:, :], ACT.Gelu_apprx_tanh, tok)
                V.op(lambda e: e.bn_stats(stats[:, t, 0, :], o), a)
                r = rstd(t, 1, rs[:, t:t + 1])
                a = act(o, o, ACT.Identity, r, scale=rs[:, t:t + 1], bias=nmr[:, t:t + 1])
                tt(o, o, lg, ALU.mult, a, t_l)
                tt(o, o, lb, ALU.add)

            proj_n(xa_x, 4, ev_v, False, tx)
            t_vt = V.last
            b = bank()
            for g in range(4):
                r = tr(b.t[:, 128 * g:128 * g + 128], wraw[:, g, :], t_l, b.free, inc=g == 3)
            b.free = V.op(lambda e, b=b: e.tensor_copy(wmT, b.t[:, :].rearrange("p (g i) -> p g i", g=4)), r)
            t_wm = memset(V, wmT[64:128, :, 0:64], 0.0)

            def ev_u(m, b, tok):
                b.free = act(uT[:, m, :], b.t[:, :], ACT.Gelu_apprx_tanh, tok)

            proj_t(XH, XL, 4, 512, 4, ev_u, tx)
            t_u = A.last
            for g in range(4):
                b = bank()
                for n in range(4):
                    r = mm(b.t[:, 128 * n:128 * n + 128], vt[:, n, 128 * g:128 * g + 128], wmT[:, g, :], True, True,
                           t_vt, t_wm, b.free, inc=n == 3)
                bb = bs[:, g, :].unsqueeze(1).broadcast_to([P, 4, 128])
                y3 = ytmp.rearrange("p (n i) -> p n i", n=4)
                b.free = tt(y3, b.t[:, :].rearrange("p (n i) -> p n i", n=4), bb, ALU.add, r, t_l)
                t_y = tt(uT[:, g, :], uT[:, g, :], ytmp, ALU.mult, t_u)

            def ev_b(m, b, tok):
                b.free = act(xb[:, m, 16:528], b.t[:, :], ACT.Copy, tok, tm)

            proj_t(XH, XL, 4, 512, 4, ev_b, tx)
            t_xb = A.last
            toks = []
            pe = PE.last
            for g in range(4):
                toks.append(split(XH[:, g, :], XL[:, g, :], uT[:, g, :], t_y, pe))
            for g in range(4):
                w = 2 << g
                src = xb[:, g, :]
                for s in range(g + 1):
                    dst = pp[s % 2]
                    tt(dst[:, 16:528], src[:, 16:528], src[:, 16 - (1 << s):528 - (1 << s)], ALU.add, t_xb, tm)
                    src = dst
                stt(pooled[:, g, :], src[:, 16:528], 1.0 / w, xb[:, g, 16:528], ALU.mult, ALU.subtract)
                tt(ytmp[:, 0:w], src[:, 16:16 + w], invc[:, 0:w], ALU.mult)
                r = tt(pooled[:, g, 0:w], ytmp[:, 0:w], xb[:, g, 16:16 + w], ALU.subtract)
                b = bank()
                r = mm(b.t[:, :], pw[:, g, :], pooled[:, g, :], True, True, r, t_l, b.free, inc=True)
                b.free = r = ts(pooled[:, g, :], b.t[:, :], vec("psc", g), None, ALU.mult, None, r, t_vec)
                toks.append(split(XH[:, 4 + g, :], XL[:, 4 + g, :], pooled[:, g, :], r, pe))
            return toks

        def mixer_c():
            nonlocal tx
            ch = big(0, 4112, 8)
            cv = big(4112, 4096, 8)
            tm = memset(V, ch[:, :, 0:2], 0.0, PE.last)
            for hf in range(2):
                def ev_c(m, b, tok, hf=hf):
                    b.free = act(ch[:, 4 * hf + m, 2:514], b.t[:, :], ACT.Copy, tok, tm, V.last)

                def ev_h(m, b, tok, hf=hf):
                    j = 4 * hf + m
                    c, x = cv[:, j, :], ch[:, j, :]
                    b.free = tt(x[:, 2:514], x[:, 2:514], b.t[:, :], ALU.mult, tok, t_c)
                    ts(c, x[:, 2:514], vec("ccw", 16 + j), None, ALU.mult, None, t_vec)
                    stt(c, x[:, 1:513], vec("ccw", 8 + j), c, ALU.mult, ALU.add)
                    stt(c, x[:, 0:512], vec("ccw", j), c, ALU.mult, ALU.add)

                if hf == 0:
                    tx = proj_t(XH, XL, 4, 512, 4, ev_c, late=turn)
                else:
                    proj_t(XH, XL, 4, 512, 4, ev_c, tx)
                t_c = A.last
                proj_t(XH, XL, 4, 512, 4, ev_h, tx)
            t_cv = []
            for hf in range(2):
                def ev_g(m, b, tok, hf=hf):
                    c = cv[:, 4 * hf + m, :]
                    b.free = tt(c, c, b.t[:, :], ALU.mult, tok)
                    t_cv.append(b.free)

                proj_t(XH, XL, 4, 512, 4, ev_g, tx)
            pe = PE.last
            return [split(XH[:, j, :], XL[:, j, :], cv[:, j, :], t_cv[j], pe) for j in range(8)]

        def cross(l):
            nonlocal tx
            qT = big(0, 4096, 8)
            Pm = [big(4096 + 1024 * i, 1024, 4) for i in range(2)]
            PT = [big(6144 + 1024 * i, 1024, 2) for i in range(2)]
            mx = SM[:, 132:140].rearrange("p (i t) -> p i t", i=2)
            sm = SM[:, 140:148].rearrange("p (i t) -> p i t", i=2)
            tp = [V.last, PE.last]
            for nb in range(2):
                def evq(m, b, tok, nb=nb):
                    b.free = act(qT[:, 4 * nb + m, :], b.t[:, :], ACT.Copy, tok, *tp, chain=False)
                if nb == 0:
                    tx = proj_t(XH, XL, 4, 512, 4, evq, late=turn)
                else:
                    proj_t(XH, XL, 4, 512, 4, evq, tx)
            tq, pq = A.last, PE.last
            pt_free = [None, None]
            state = {}

            def scores(h):
                i = h % 2
                toks = []
                for tp2 in range(2):
                    b = bank()
                    for t in range(2):
                        tt_ = 2 * tp2 + t
                        for k in range(2):
                            r = mm(b.t[:, 256 * t:256 * t + 256], qT[:, 2 * h + k, 128 * tt_:128 * tt_ + 128],
                                   KT[l][:, 2 * h + k, :], k == 0, k == 1, tq, t_kv, b.free, inc=t == 1 and k == 1)
                    v = b.t[:, :].rearrange("p (t m) -> p t m", t=2)
                    m2 = mx[:, i, 2 * tp2:2 * tp2 + 2]
                    V.op(lambda e, m2=m2, v=v: e.tensor_reduce(m2, v, AX.X, ALU.max), r, pt_free[i])
                    r = ts(m2, m2, -0.0625, None, ALU.mult, None)
                    for t in range(2):
                        tt_ = 2 * tp2 + t
                        a = act(Pm[i][:, tt_, :], v[:, t, :], ACT.Exp, r, pt_free[i], scale=0.0625,
                                bias=mx[:, i, tt_:tt_ + 1], accum_out=sm[:, i, tt_:tt_ + 1])
                    b.free = a
                V.op(lambda e: e.reciprocal(sm[:, i, :], sm[:, i, :]), a)
                for t in range(4):
                    r = ts(Pm[i][:, t, :], Pm[i][:, t, :], sm[:, i, t:t + 1], None, ALU.mult, None)
                state[h] = r

            def values(h):
                i = h % 2
                ts_ = []
                for mt in range(2):
                    b = bank()
                    for t in range(4):
                        r = tr(b.t[:, 128 * t:128 * t + 128], Pm[i][:, t, 128 * mt:128 * mt + 128], state[h], b.free,
                               inc=t == 3)
                    b.free = act(PT[i][:, mt, :], b.t[:, :], ACT.Copy, r)
                    ts_.append(b.free)
                pt_free[i] = r
                for d in range(2):
                    b = bank()
                    for mt in range(2):
                        r = mm(b.t[:, :], VT[l][:, mt, 256 * h + 128 * d:256 * h + 128 * d + 128], PT[i][:, mt, :],
                               mt == 0, mt == 1, ts_[mt], b.free, inc=mt == 1)
                    b.free = split(XH[:, 2 * h + d, :], XL[:, 2 * h + d, :], b.t[:, :], r, pq)
                    ty.append(b.free)

            ty = []
            scores(0)
            for h in range(4):
                if h < 3:
                    scores(h + 1)
                values(h)
            return ty

        def ffn_up(l):
            nonlocal tx
            hT = big(0, 11264, 22)
            gp = [SCR[:, 514 * i:514 * i + 514] for i in range(2)]
            cv = [SCR[:, 1028 + 512 * i:1540 + 512 * i] for i in range(2)]
            tm = V.last
            for i in range(2):
                tm = memset(V, gp[i][:, 0:2], 0.0, A.last)
            cvfree = [[None], [None]]
            tp = PE.last
            for nb in range(11):
                bk = {}

                def ev(m, b, tok, nb=nb, bk=bk):
                    bk[m] = (b, tok)
                    if m < 2:
                        return
                    i = m - 2
                    j = 2 * nb + i
                    g, c = gp[i], cv[i]
                    b.free = a = act(g[:, 2:514], b.t[:, :], ACT.Copy, tok, tm, cvfree[i][0], chain=False)
                    ts(c, g[:, 2:514], vec(f"fcw{l}", 44 + j), None, ALU.mult, None, a)
                    stt(c, g[:, 1:513], vec(f"fcw{l}", 22 + j), c, ALU.mult, ALU.add)
                    r = stt(c, g[:, 0:512], vec(f"fcw{l}", j), c, ALU.mult, ALU.add)
                    a = act(c, c, ACT.Gelu_apprx_tanh, r, bias=vec(f"fcb{l}", j))
                    ba, ta = bk[i]
                    ba.free = cvfree[i][0] = tt(hT[:, j, :], c, ba.t[:, :], ALU.mult, a, ta, tp)

                if nb == 0:
                    tx = proj_t(XH, XL, 4, 512, 4, ev, t_vec, late=turn)
                else:
                    proj_t(XH, XL, 4, 512, 4, ev, tx, t_vec)
            return V.last, PE.last

        def ffn_down(l, th, tup, tgb):
            hT = big(0, 11264, 22)
            free = {s: tup for s in range(8)}

            def prep():
                tok = {}

                def ahead(c):
                    if c > 10:
                        return
                    for kt in (2 * c, 2 * c + 1):
                        tok[kt] = split(XH[:, kt % 8, :], XL[:, kt % 8, :], hT[:, kt, :], th, free[kt % 8])

                def done(c, r):
                    for kt in (2 * c, 2 * c + 1):
                        free[kt % 8] = r

                return {"tok": tok, "ahead": ahead, "done": done}

            return out_ln(lambda kt, t: (XH[:, kt % 8, 128 * t:128 * t + 128], XL[:, kt % 8, 128 * t:128 * t + 128]),
                          11, tgb, None, [prep(), prep()])

        def layers():
            nonlocal t_gb
            for l in range(2):
                ty = mixer_ab() if l == 0 else mixer_c()
                mark(f"mixin{l}")
                tl = out_ln(xa_x, 4, t_gb, ty)
                t_gb = load_gb(I["ln_xa_g"][l], I["ln_xa_b"][l], tl)
                mark(f"mixout{l}")
                if stop == f"mix{l}":
                    return
                ty = cross(l)
                mark(f"cross{l}")
                tl = out_ln(xa_x, 4, t_gb, ty)
                t_gb = load_gb(I["ln_ffn_g"][l], I["ln_ffn_b"][l], tl)
                mark(f"wo{l}")
                if stop == f"xa{l}":
                    return
                th, tup = ffn_up(l)
                mark(f"up{l}")
                tl = ffn_down(l, th, tup, t_gb)
                if l == 0:
                    t_gb = load_gb(I["ln_mix_g"][1], I["ln_mix_b"][1], tl)
                mark(f"down{l}")
                if stop == f"ffn{l}":
                    return


        def second():
            nonlocal tx
            B = [big(2048 * i, 2048) for i in range(6)]
            L = [late(2048 * i, 2048) for i in range(4)]

            def v4(x):
                return x.rearrange("p (a b) -> p a b", a=4)

            V.wait(t_rel)
            mod = SM[:, 148:172]

            for nb in range(6):
                def ev_mod(m, b, tok, nb=nb):
                    j = 4 * nb + m
                    b.free = tt(mod[:, j:j + 1], b.t[:, 0:1], vec("ba", j), ALU.add, tok)
                bs = [bank() for _ in range(4)]
                for c in range(4):
                    i, raw, _, tok = w_get()
                    for m in range(4):
                        for k in range(2):
                            last = c == 3 and k == 1
                            r = mm(bs[m].t[:, 0:1], raw[:, k, 128 * m:128 * m + 128], ca[:, 2 * c + k:2 * c + k + 1],
                                   c == 0 and k == 0, last, tok, t_c, bs[m].free, inc=last or (m == 3 and k == 1))
                        if last:
                            ev_mod(m, bs[m], r)
                    w_release(i, r)
            s1 = SM[:, 172:180]
            t_mod = stt(s1, mod[:, 8:16], 1.0, VEC[:, vcol["ng"]:vcol["ng"] + 8], ALU.add, ALU.mult)

            ss = SM[:, 180:184]
            rq = SM[:, 184:188]
            xn = big(0, 4096, 4)
            junk = SCR[:, 0:1024]
            for t in range(4):
                a = act(junk, XR[:, t, :], ACT.Square, t_xr, accum_out=ss[:, t:t + 1])
            ts(ss, ss, 1.0 / D, 1e-6, ALU.mult, ALU.add, a, eng=G)
            r = tt(rq, ss, nhalf[:, 0:4], ALU.pow, eng=G)
            for t in range(4):
                a = act(xn[:, t, :], XR[:, t, :], ACT.Copy, r, V.last, PE.last, scale=rq[:, t:t + 1])
            t_spx = A.dma(d_x, XR[:, :, :], dsem(), t_xr)
            for k in range(8):
                b = bank()
                for t in range(4):
                    r = tr(b.t[:, 128 * t:128 * t + 128], xn[:, t, 128 * k:128 * k + 128], a, b.free, inc=t == 3)
                h = SCR[:, 1024 + 512 * (k % 2):1536 + 512 * (k % 2)]
                b.free = r = ts(h, b.t[:, :], s1[:, k:k + 1], mod[:, k:k + 1], ALU.mult, ALU.add, r, t_mod, A.last)
                tx = split(XH[:, k, :], XL[:, k, :], h, r)

            mark("ada+rms")
            qtok, ktok, va, sga = v4(B[0]), v4(B[1]), v4(B[2]), v4(B[3])
            R, K, Vt, Gt = v4(B[4]), v4(B[5]), v4(L[0]), v4(L[1])
            wd = L[2][:, 0:512]
            w2a2 = L[2][:, 512:1024]
            ds = dsem()
            G.dma(w2a2[0:64, :], I["w2_2"][0], ds, V.last, A.last)
            t_w2 = G.dma(w2a2[64:128, :], I["a2_2"][0], ds)
            bias = GB[:, :].rearrange("p (h k) -> p h k", h=8)
            rev, exch = L[3], SCR[:, 2600:2728]
            G.dma(rev.rearrange("p (h k) -> p h k", h=8),
                  bass.AP(tensor=d_rel.tensor, offset=0, ap=[[1, 128], [384, 8], [1, 256]]), ds, t_rel)
            t_bi = G.dma(exch, I["cstd"], ds)
            for j in range(4):
                b = bank()
                rr = mm(b.t[:, :], exch, rev[:, 512 * j:512 * j + 512], True, True, t_bi, b.free, inc=True)
                b.free = act(GB[:, 512 * j:512 * j + 512], b.t[:, :], ACT.Copy, rr, t_xr)
            t_bi = memset(G, bias[0:64, :, 192:256], -1e30, b.free)
            tpr = [V.last, A.last, PE.last]

            for dst in (qtok, ktok, va):
                def ev_n(t, b, tok, dst=dst):
                    b.free = act(dst[:, t, :], b.t[:, :], ACT.Copy, tok, *tpr, chain=False)
                proj_n(xa_x, 4, ev_n, False, tx)
            t_qkv = A.last

            def silu2(o, b, tok):
                a = act(o, b.t[:, :], ACT.Tanh, tok, *tpr, scale=0.5)
                b.free = stt(o, o, 1.0, b.t[:, :], ALU.add, ALU.mult, a)

            def ev_ga(m, b, tok):
                silu2(sga[:, m, :], b, tok)
            proj_t(XH, XL, 4, 512, 4, ev_ga, tx)
            sh = [SCR[:, 520 * i:520 * i + 513] for i in range(2)]
            tsh = [memset(V, sh[i][:, 0:1], 0.0, A.last) for i in range(2)]

            def shift(o, b, tok, j):
                i = j % 2
                a = b.free = act(sh[i][:, 1:513], b.t[:, :], ACT.Copy, tok, tsh[i], *tpr)
                tt(o, sh[i][:, 0:512], sh[i][:, 1:513], ALU.subtract, a)
                tsh[i] = stt(o, o, vec("mu", j), sh[i][:, 1:513], ALU.mult, ALU.add)
                return tsh[i]

            for n, dst in enumerate((R, K, Vt, Gt)):
                def ev_s(m, b, tok, n=n, dst=dst):
                    r = shift(dst[:, m, :], b, tok, 4 * n + m)
                    if n == 3:
                        th = SCR[:, 1040 + 512 * (m % 2):1552 + 512 * (m % 2)]
                        a = act(th, dst[:, m, :], ACT.Tanh, r, scale=0.5)
                        stt(dst[:, m, :], th, 1.0, dst[:, m, :], ALU.add, ALU.mult, a)
                proj_t(XH, XL, 4, 512, 4, ev_s, tx)
            t_g = V.last
            t_spg = A.dma(d_g, L[1], dsem(), t_g)

            def ev_w(m, b, tok):
                r = shift(wd, b, tok, 16)
                act(wd[0:64, :], wd[0:64, :], ACT.Tanh, r)
            proj_t(XH, XL, 4, 512, 1, ev_w, tx)
            t_wd = A.last
            t_xfree = PE.last

            mark("w_in")
            sq = SCR[:, 1040:2064].rearrange("p (i n) -> p i n", i=2)
            ssq = SM[:, 188:252].rearrange("p (i n) -> p i n", i=2)
            for i, x in enumerate((qtok, ktok)):
                for t in range(4):
                    a = act(sq[:, t % 2, :], x[:, t, :], ACT.Square, t_qkv, V.last)
                    r = V.op(lambda e, i=i, t=t: e.tensor_reduce(
                        ssq[:, i, 8 * t:8 * t + 8], sq[:, t % 2, :].rearrange("p (h d) -> p h d", h=8), AX.X, ALU.add), a)
            r = ts(SM[:, 188:252], SM[:, 188:252], 1.0 / 64, 1e-6, ALU.mult, ALU.add)
            a = act(SM[:, 188:252], SM[:, 188:252], ACT.Sqrt, r)
            V.op(lambda e: e.reciprocal(SM[:, 188:252], SM[:, 188:252]), a)
            qT, kT = v4(L[3]), v4(B[0])
            for i, (x, dst, g) in enumerate(((qtok, qT, "qg"), (ktok, kT, "kg"))):
                for t in range(4):
                    x3 = x[:, t, :].rearrange("p (h d) -> p h d", h=8)
                    s3 = ssq[:, i, 8 * t:8 * t + 8].unsqueeze(2).broadcast_to([P, 8, 64])
                    r = tt(x3, x3, s3, ALU.mult)
                for t in range(4):
                    b = bank()
                    for m in range(4):
                        rr = tr(b.t[:, 128 * m:128 * m + 128], x[:, t, 128 * m:128 * m + 128], r, b.free, inc=m == 3)
                    b.free = t_qk = ts(dst[:, :, 128 * t:128 * t + 128], b.t[:, :].rearrange("p (m n) -> p m n", m=4),
                                       vec(g), None, ALU.mult, None, rr)
            PT = v4(B[1])
            Sb = [SCR[:, 512 * i:512 * i + 512] for i in range(4)]
            am = SM[:, 132:140]
            asum = SM[:, 140:148]
            sb_free = [None] * 4
            t_pt = None
            yb = None
            for h in range(8):
                hp, par = h // 2, h % 2
                ps = slice(64 * par, 64 * par + 64)
                tp = []
                for q in range(4):
                    nk = 128 * (q + 1)
                    b = bank()
                    r = mm(b.t[:, 0:nk], qT[ps, hp, 128 * q:128 * q + 128], kT[ps, hp, 0:nk], True, True, t_qk, b.free,
                           inc=True)
                    s = Sb[q]
                    lo = max(0, nk - 256)
                    if lo:
                        ts(s[:, 0:lo], b.t[:, 0:lo], 0.125, bias[:, h, 0:1], ALU.mult, ALU.add, r, t_bi, sb_free[q])
                    b.free = stt(s[:, lo:nk], b.t[:, lo:nk], 0.125, bias[:, h, 256 - (nk - lo):256], ALU.mult, ALU.add,
                                 r, t_bi, sb_free[q])
                    V.op(lambda e, s=s, nk=nk, q=q: e.tensor_reduce(am[:, q:q + 1], s[:, 0:nk], AX.X, ALU.max))
                    r = ts(am[:, q:q + 1], am[:, q:q + 1], -1.0, None, ALU.mult, None)
                    a = act(s[:, 0:nk], s[:, 0:nk], ACT.Exp, r, bias=am[:, q:q + 1], accum_out=asum[:, q:q + 1])
                    V.op(lambda e, q=q: e.reciprocal(asum[:, q:q + 1], asum[:, q:q + 1]), a)
                    r = ts(s[:, 0:nk], s[:, 0:nk], asum[:, q:q + 1], None, ALU.mult, None)
                    b = bank()
                    for m in range(q + 1):
                        rr = tr(b.t[:, 128 * m:128 * m + 128], s[:, 128 * m:128 * m + 128], r, b.free, inc=m == q)
                    sb_free[q] = rr
                    b.free = act(PT[:, 0:q + 1, 128 * q:128 * q + 128],
                                 b.t[:, 0:nk].rearrange("p (m n) -> p m n", n=128), ACT.Copy, rr, t_pt)
                yb = bank()
                for m in range(4):
                    r = mm(yb.t[ps, 128 * m:512], va[:, m, 64 * h:64 * h + 64], PT[:, m, 128 * m:512], m == 0, m == 3,
                           A.last, t_qkv, yb.free, inc=m == 3)
                t_pt = r
                yb.free = r = stt(sga[ps, hp, :], sga[ps, hp, :], 0.5, yb.t[ps, :], ALU.mult, ALU.mult, r)
                if par == 1:
                    t_ya = split(XH[:, 4 + hp, :], XL[:, 4 + hp, :], sga[:, hp, :], r, t_xfree)

            mark("attn")
            cb = GB
            t_cb = G.dma(GB[:, 0:1312], I["cstb"], dsem(), V.last)
            mSU2, mL1 = cb[:, 0:128], cb[:, 128:192]
            mLT = [cb[:, 192 + 64 * i:256 + 64 * i] for i in range(6)]
            id64, bones = cb[:, 576:640], cb[:, 640:768]
            sel = cb[:, 768:800].rearrange("p (a b) -> p a b", a=4)
            selT = cb[0:8, 800:1312]
            smask = SCR[:, 0:512]
            t_sm = G.dma(smask, I["cstc"].partition_broadcast(P), dsem(), V.last, PE.last, A.last)
            hv = SM[:, 132:140]
            r = ts(hv, VEC[:, vcol["w0"]:vcol["w0"] + 8], 0.5, None, ALU.mult, None)
            oka = SM[:, 140:144]
            ts(oka, VEC[:, vcol["ka"]:vcol["ka"] + 4], -1.0, 1.0, ALU.mult, ALU.add)
            LW, AA, C, Pp = v4(B[0]), v4(B[1]), v4(B[2]), v4(B[3])
            tp = [PE.last, V.last, A.last]
            for m in range(4):
                for half, dst in ((0, LW), (1, AA)):
                    b = bank()
                    p = slice(64 * half, 64 * half + 64)
                    rr = mm(b.t[:, :], w2a2[p, 128 * m:128 * m + 128], wd[p, :], True, True, t_wd, t_w2, b.free, inc=True)
                    a = b.free = act(dst[:, m, :], b.t[:, :], ACT.Tanh, rr, r, *tp, scale=0.5,
                                     bias=hv[:, 4 * half + m:4 * half + m + 1])
                    if half == 0:
                        ts(dst[:, m, :], dst[:, m, :], -EM5 / 2, -EM5 / 2, ALU.mult, ALU.add, a)
                        V.op(lambda e, m=m: e.tensor_tensor_scan(C[:, m, :], smask, LW[:, m, :], 0.0, ALU.mult, ALU.add),
                             t_sm)
                    else:
                        ts(dst[:, m, :], dst[:, m, :], 0.5, 0.5, ALU.mult, ALU.add, a)
            r = tt(B[0], B[2], B[0], ALU.subtract)
            act(B[0], B[0], ACT.Exp, r)
            act(B[3], B[2], ACT.Exp)
            t_exp = act(B[2], B[2], ACT.Exp, scale=-1.0)
            Pm1, Pinv = v4(B[0]), v4(B[2])
            pC = SM[:, 188:220].rearrange("p (a c) -> p a c", a=4)
            V.op(lambda e: e.tensor_copy(pC, B[3].rearrange("p (a c k) -> p a c k", a=4, k=64)[:, :, :, 63]), t_exp)
            KK = v4(L[3])
            for m in range(4):
                ts(KK[:, m, :], K[:, m, :], vec("kk", m), None, ALU.mult, None)
            X = [XR[:, 0:2, :].rearrange("p a b -> p (a b)"), XR[:, 2:4, :].rearrange("p a b -> p (a b)")]
            r = tt(X[0], L[3], L[3], ALU.mult, t_spx)
            b = bank()
            for m in range(4):
                rr = mm(b.t[0:8, :], sel[:, m, :], v4(X[0])[:, m, :], m == 0, m == 3, r, t_cb, b.free, inc=m == 3)
            rs8 = SCR[0:8, 512:1024]
            b.free = r = ts(rs8, b.t[0:8, :], 1e-24, None, ALU.max, None, rr)
            a = act(rs8, rs8, ACT.Sqrt, r)
            r = V.op(lambda e: e.reciprocal(rs8, rs8), a)
            for m in range(4):
                b = bank()
                rr = mm(b.t[:, :], selT[:, 128 * m:128 * m + 128], rs8, True, True, r, b.free, inc=True)
                b.free = tt(KK[:, m, :], KK[:, m, :], b.t[:, :], ALU.mult, rr)
            for m in range(4):
                ts(v4(X[0])[:, m, :], AA[:, m, :], vec("ka", m), oka[:, m:m + 1], ALU.mult, ALU.add)
            tt(B[5], B[5], X[0], ALU.mult)
            ar = XR[:, :, :].rearrange("p a b -> p (a b)").rearrange("p (x s j) -> p x s j", s=2, j=64)
            k32 = "p (x j) -> p x j"
            stt(ar[:, :, 0, :], L[3].rearrange(k32, j=64), -1.0, B[0].rearrange(k32, j=64), ALU.mult, ALU.mult)
            tt(ar[:, :, 1, :], B[4].rearrange(k32, j=64), B[3].rearrange(k32, j=64), ALU.mult)
            tt(B[1], B[1], L[3], ALU.mult)
            tt(B[1], B[1], B[2], ALU.mult)
            tt(L[3], B[4], B[5], ALU.mult)
            rkb = v4(B[0][:, 0:512])
            for m in range(4):
                r = ts(rkb[:, m, :], bones, vec("rk", m), None, ALU.mult, None, t_cb)
            for m in range(4):
                b = bank()
                rr = mm(b.t[:, :], rkb[:, m, :], v4(L[3])[:, m, :], True, True, r, b.free, inc=True)
                b.free = r2 = tt(v4(B[3])[:, m, :], Vt[:, m, :], b.t[:, :], ALU.mult, rr)
            t_spb = A.dma(d_b, B[3], dsem(), r2)
            r = tt(B[5], B[5], B[2], ALU.mult)
            KtT, BtT = K, AA
            toks = {}
            for n, (src, dst) in enumerate(((Vt, v4(B[0])), (BtT, v4(B[2])), (KtT, v4(B[4])))):
                for t in range(4):
                    b = bank()
                    for m in range(4):
                        rr = tr(b.t[:, 128 * m:128 * m + 128], src[:, m, 128 * t:128 * t + 128], r, b.free, inc=m == 3)
                    b.free = act(dst[:, t, :], b.t[:, :], ACT.Copy, rr, r, r2)
            t_tok = A.last
            Vk, Bk, Kk = v4(B[0]), v4(B[2]), v4(B[4])
            ar5 = ar.rearrange("p (a c) s j -> p a c s j", a=4)

            mark("rwkv ops")
            NV, Y0 = v4(L[2]), v4(L[3])
            TTc = [L[0][:, 512 * i:512 * i + 512] for i in range(2)]
            KA = L[0][:, 1024:2048].rearrange("p (h s n) -> p h s n", s=2, n=64)
            BAs = [L[1][:, 1024 * i:1024 * i + 1024].rearrange("p (h s n) -> p h s n", s=2, n=64) for i in range(2)]
            Tt, TTt, Xt, Mk0, Mk1 = [SCR[:, 512 * i:512 * i + 512].rearrange("p (h n) -> p h n", n=64) for i in range(5)]
            Mks = [Mk0, Mk1]
            St = B[3][:, 0:256].rearrange("p (m n) -> p m n", m=4)
            Us = [B[3][:, 512 + 512 * i:1024 + 512 * i] for i in range(2)]
            NG = 2
            HG = 8 // NG
            pps = [slice(0, 64), slice(64, 128)]
            t0 = [t_spb, t_spg, t_tok, PE.last, A.last, V.last]
            sfree = {}

            def bc(m, n=8):
                return m.unsqueeze(1).broadcast_to([P, n, 64])

            def b3(b, n=8):
                return b.t[:, 0:64 * n].rearrange("p (h n) -> p h n", n=64)

            def inverse(t):
                BA = BAs[t % 2]
                cols = [slice(128 * t + 64 * cp, 128 * t + 64 * cp + 64) for cp in range(2)]
                mask2 = mSU2.unsqueeze(1).broadcast_to([P, 4, 128])
                t_ka = []
                for src, dst, ba in ((KtT, KA, 0), (BtT, BA, 1)):
                    for par, ps in enumerate(pps):
                        b = bank()
                        for m in range(4):
                            for cp in range(2):
                                rr = mm(b.t[pps[cp], 128 * m:128 * m + 128], src[ps, m, cols[cp]],
                                        ar5[ps, m, 2 * t + cp, :, :].rearrange("p s j -> p (s j)"), True, True,
                                        b.free, *t0, inc=m == 3 and cp == 1)
                        b.free = r = tt(dst[:, par::2, :, :].rearrange("p h s n -> p h (s n)"),
                                        b.t[:, :].rearrange("p (h n) -> p h n", h=4), mask2, ALU.mult, rr,
                                        sfree.get(("ba", t - 2)) if ba else sfree.get(("ka", t - 1)),
                                        sfree.get(("tt", t - 1)))
                        if not ba:
                            t_ka.append(r)
                    yield
                t_ba = r
                for par, ps in enumerate(pps):
                    b = bank()
                    for m in range(4):
                        for cp in range(2):
                            rr = mm(b.t[pps[cp], 64 * m:64 * m + 64], ar5[ps, m, 2 * t + cp, 0, :],
                                    BtT[ps, m, cols[cp]], True, True, b.free, inc=m == 3 and cp == 1)
                    b.free = tt(Tt[:, par::2, :], b3(b, 4), bc(mL1, 4), ALU.mult, rr)
                tt(TTt, BA[:, :, 0, :], bc(mLT[0]), ALU.mult)
                tt(Tt, Tt, bc(id64), ALU.add)
                r = tt(TTt, TTt, bc(id64), ALU.add)
                mk = [None, tt(Mks[1], BA[:, :, 0, :], bc(mLT[1]), ALU.mult, t_ba, sfree.get(("mk", 1)), eng=G)]
                yield
                for s, dst in ((0, NV), (1, Y0)):
                    b = bank()
                    for h in range(8):
                        for cp in range(2):
                            rr = mm(b.t[pps[cp], 64 * h:64 * h + 64], KA[pps[cp], h, s, :],
                                    Vk[pps[cp], t, 64 * h:64 * h + 64], True, True, t_ka[-1], b.free,
                                    inc=h == 7 and cp == 1)
                    b.free = act(dst[:, t, :], b.t[:, :], ACT.Copy, rr)
                sfree["nv", t] = b.free
                sfree["ka", t] = rr
                yield
                tg = [r] * NG
                for lv in range(1, 6):
                    if lv < 5:
                        mk.append(tt(Mks[(lv + 1) % 2], BA[:, :, 0, :], bc(mLT[lv + 1]), ALU.mult,
                                     sfree.get(("mk", (lv + 1) % 2)), eng=G))
                    M = Mks[lv % 2]
                    xa = []
                    for g in range(NG):
                        hs = slice(HG * g, HG * g + HG)
                        b = bank()
                        for h in range(HG * g, HG * g + HG):
                            for cp in range(2):
                                rr = mm(b.t[pps[cp], 64 * (h % HG):64 * (h % HG) + 64], M[pps[cp], h, :], Tt[pps[cp], h, :],
                                        True, True, mk[lv], tg[g], b.free, inc=h % HG == HG - 1 and cp == 1)
                        b.free = a = act(Xt[:, hs, :], b3(b, HG), ACT.Copy, rr, sfree.get(("x", g)))
                        xa.append(a)
                    sfree["mk", lv % 2] = rr
                    yield
                    for g in range(NG):
                        hs = slice(HG * g, HG * g + HG)
                        prods = [(Xt, TTt)] if lv == 5 else [(TTt, Xt), (Xt, TTt)]
                        bs = []
                        for l, rg in prods:
                            b = bank()
                            for h in range(HG * g, HG * g + HG):
                                for cp in range(2):
                                    rr = mm(b.t[pps[cp], 64 * (h % HG):64 * (h % HG) + 64], l[pps[cp], h, :],
                                            rg[pps[cp], h, :], True, True, xa[g], b.free,
                                            inc=h % HG == HG - 1 and cp == 1)
                            bs.append((b, rr))
                        sfree["x", g] = rr
                        if lv < 5:
                            bs[0][0].free = tg[g] = tt(Tt[:, hs, :], Tt[:, hs, :], b3(bs[0][0], HG), ALU.add, bs[0][1],
                                                       bs[1][1])
                            bs[1][0].free = tg[g] = tt(TTt[:, hs, :], TTt[:, hs, :], b3(bs[1][0], HG), ALU.add, bs[1][1])
                        else:
                            bs[0][0].free = r = tt(TTc[t % 2].rearrange("p (h n) -> p h n", n=64)[:, hs, :],
                                                   TTt[:, hs, :], b3(bs[0][0], HG), ALU.add, bs[0][1],
                                                   sfree.get(("s", t - 2)))
                    yield
                sfree["tt", t] = r

            s_tok = [memset(V, B[3][:, 0:256], 0.0, *t0)]
            u_free = [None, None]

            def state(t):
                RB = BAs[t % 2]
                for cp in range(2):
                    c = 2 * t + cp
                    pp = pps[cp]
                    nv = NV[pp, t, :].rearrange("p (m q n) -> p m q n", q=2, n=64)
                    y0 = Y0[pp, t, :].rearrange("p (m q n) -> p m q n", q=2, n=64)
                    ws = []
                    for par, ps in enumerate(pps):
                        w = bank()
                        for m in range(4):
                            rr = mm(w.t[:, 64 * m:64 * m + 64], ar5[ps, m, c, :, :].rearrange("p s j -> p (s j)"),
                                    St[ps, m, :], True, True, s_tok[0], w.free, inc=m == 3)
                        r = tt(nv[:, :, par, :], nv[:, :, par, :], b3(w, 4)[0:64], ALU.add, rr, sfree["nv", t])
                        ws.append(w)
                    yield
                    b = bank()
                    for h in range(8):
                        hs = slice(64 * h, 64 * h + 64)
                        rr = mm(b.t[pp, hs], TTc[t % 2][pp, hs], NV[pp, t, hs], True, True, r, sfree["tt", t], b.free,
                                inc=h == 7)
                    U = Us[c % 2]
                    b.free = a = act(U[pp, :], b.t[pp, :], ACT.Copy, rr, u_free[c % 2])
                    yield
                    bd = bank()
                    for h in range(8):
                        hs = slice(64 * h, 64 * h + 64)
                        o = bd.t[pps[h % 2], 64 * (h // 2):64 * (h // 2) + 64]
                        mm(o, Kk[pp, t, hs], Vk[pp, t, hs], True, False, a, bd.free)
                        rd = mm(o, Bk[pp, t, hs], U[pp, hs], False, True, inc=h == 7)
                    by = bank()
                    for h in range(8):
                        hs = slice(64 * h, 64 * h + 64)
                        ry = mm(by.t[pp, hs], RB[pp, h, 1, :], U[pp, hs], True, True, by.free, inc=h == 7)
                    u_free[c % 2] = ry
                    bd.free = tt(St, St, b3(bd, 4), ALU.add, rd)
                    s_tok[0] = tt(St, St, pC[:, :, c].unsqueeze(2).broadcast_to([P, 4, 64]), ALU.mult)
                    for par in range(2):
                        ws[par].free = tt(y0[:, :, par, :], y0[:, :, par, :], b3(ws[par], 4)[64:128], ALU.add)
                    by.free = tt(Y0[pp, t, :], Y0[pp, t, :], by.t[pp, :], ALU.add, ry)
                    yield
                sfree["s", t] = sfree["ba", t] = ry

            for t in range(5):
                gens = ([inverse(t)] if t < 4 else []) + ([state(t - 1)] if t > 0 else [])
                while gens:
                    for g in list(gens):
                        if next(g, "end") == "end":
                            gens.remove(g)

            mark("rwkv state")
            t_g = A.dma(B[1], d_g, dsem(), t_spg, PE.last)
            t_b = A.dma(B[5], d_b, dsem(), t_spb, PE.last)
            t_x = A.dma(XR[:, :, :], d_x, dsem(), t_spx, PE.last)
            y32 = L[3].rearrange("p (x j) -> p x j", j=64)
            gs, gm = SM[:, 188:220], SM[:, 220:252]
            V.op(lambda e: e.tensor_reduce(gm, y32, AX.X, ALU.add))
            ts(gm, gm, 1.0 / 64, None, ALU.mult, None)
            r = tt(y32, y32, gm.unsqueeze(2).broadcast_to([P, 32, 64]), ALU.subtract)
            a = act(L[2], L[3], ACT.Square, r)
            V.op(lambda e: e.tensor_reduce(gs, L[2].rearrange("p (x j) -> p x j", j=64), AX.X, ALU.add), a)
            r = ts(gs, gs, 1.0 / 64, 64e-5, ALU.mult, ALU.add)
            a = act(gs, gs, ACT.Sqrt, r)
            V.op(lambda e: e.reciprocal(gs, gs), a)
            r = tt(y32, y32, gs.unsqueeze(2).broadcast_to([P, 32, 64]), ALU.mult)
            yT = v4(B[2])
            for m in range(4):
                b = bank()
                for t in range(4):
                    rr = tr(b.t[:, 128 * t:128 * t + 128], Y0[:, t, 128 * m:128 * m + 128], r, b.free, inc=t == 3)
                y = yT[:, m, :]
                b.free = ts(y, b.t[:, :], vec("lxg", m), vec("lxb", m), ALU.mult, ALU.add, rr)
                tt(y, y, v4(B[5])[:, m, :], ALU.add, t_b)
                ry = stt(y, y, 0.5, v4(B[1])[:, m, :], ALU.mult, ALU.mult, t_g)
                ty = split(XH[:, m, :], XL[:, m, :], y, ry, t_xfree)

            mark("gn")
            ones = SCR[:, 0:128]
            dg = SCR[:, 1024:2048].rearrange("p (k n) -> p k n", k=8)
            gate = B[0][:, 0:1024]
            memset(V, ones, 1.0, PE.last)
            for k in range(8):
                r = ts(dg[:, k, :], ident, mod[:, 16 + k:17 + k], None, ALU.mult, None)
            for j in range(2):
                b = bank()
                for k in range(4):
                    rr = mm(b.t[:, 128 * k:128 * k + 128], ones, dg[:, 4 * j + k, :], True, True, r, b.free, inc=k == 3)
                b.free = act(gate[:, 512 * j:512 * j + 512], b.t[:, :], ACT.Copy, rr, r)
            t_gt = A.last
            o = out[0].rearrange("(a p) n -> p a n", p=P)
            ods = dsem()
            fin = []
            for j in range(2):
                def ev_o(t, b, tok, j=j):
                    cs = slice(512 * j, 512 * j + 512)
                    x = B[4 + (t % 2)][:, 1024:1536] if False else GB[:, 512 * (t % 4):512 * (t % 4) + 512]
                    b.free = tt(x, b.t[:, :], gate[:, cs], ALU.mult, tok, t_gt)
                    r = tt(XR[:, t, cs], XR[:, t, cs], x, ALU.add, t_x)
                    fin.append(A.dma(o[:, t, cs], XR[:, t, cs], ods, r))
                proj_n(xa_x, 4, ev_o, True, ty, t_ya)
            mark("out")
            A.wait(fin[-1])

        cc = VEC[:, vcol["c"]:vcol["c"] + 8]
        cs1 = ca = SM[:, 188:196]
        a = act(cs1, cc, ACT.Tanh, t_vec, scale=0.5)
        ts(cs1, cs1, 0.5, 0.5, ALU.mult, ALU.add, a)
        t_c = tt(cs1, cs1, cc, ALU.mult)
        rp = big(11500, 384)[0:8, :]
        r = A.dma(rp[:, 127:319], I["rel_rev"], dsem())
        V.op(lambda e: e.tensor_copy(rp[:, 0:127], rp[:, 127:128].broadcast_to([8, 127])), r)
        r = V.op(lambda e: e.tensor_copy(rp[:, 319:384], rp[:, 318:319].broadcast_to([8, 65])))
        t_rel = A.dma(d_rel, rp, dsem(), r)
        layers()
        t_xr = V.last
        if stop:
            finish(XR[:, :, :])
        else:
            second()

        block = ctx.enter_context(nc.Block())

        def play(eng):
            def f(e):
                for g in eng.q:
                    g(e)
            return f

        block.tensor(play(PE))
        block.vector(play(V))
        block.scalar(play(A))
        block.gpsimd(play(G))
        block.sync(play(S))


_INS = ["x", "mem", "ab_w_in", "sgu_ln_g", "sgu_ln_b", "sgu_w", "sgu_b", "pool_w", "pool_scale", "ab_w_out",
        "c_w_in", "c_conv_w", "c_w_out", "ln_mix_g", "ln_mix_b", "xa_wq", "xa_wkv", "xa_wo", "ln_xa_g", "ln_xa_b",
        "ffn_w_up", "ffn_conv_w", "ffn_conv_b", "ffn_w_down", "ln_ffn_g", "ln_ffn_b", "c_2", "norm_g_2", "w_ada_2",
        "b_ada_2", "w_in_2", "mu_shift_2", "w0_2", "w2_2", "a0_2", "a2_2", "k_k_2", "k_a_2", "r_k_2", "lnx_g_2",
        "lnx_b_2", "q_norm_g_2", "k_norm_g_2", "rel_bias_2", "w_out_2"]


def constants():
    import numpy as np
    cst = np.zeros((128, 144), np.float32)
    cst[:, 0:128] = np.eye(128)
    cst[:, 128:144] = 1.0 / np.arange(1, 17)
    t = np.arange(128)
    s, q = t[:, None] % 64, t[None, 0:64]

    def level(row, col, n):
        return (row // (2 * n) == col // (2 * n)) & (row // n % 2 == 1) & (col // n % 2 == 0)

    cb = np.zeros((128, 1312), np.float32)
    cb[:, 0:64] = s < q
    cb[:, 64:128] = s <= q
    cb[:, 128:192] = level(s, q, 1)
    for i in range(6):
        cb[:, 192 + 64 * i:256 + 64 * i] = level(q, s, 1 << i)
    cb[:, 576:640] = s == q
    cb[:, 640:768] = t[:, None] // 64 == t[None, :] // 64
    for m in range(4):
        for p in range(2):
            cb[64 * p:64 * p + 64, 768 + 8 * m + 2 * m + p] = 1
            cb[2 * m + p, 800 + 128 * m + 64 * p:800 + 128 * m + 64 * p + 64] = 1
    cc = np.ones(512, np.float32)
    cc[0::64] = 0
    return {"cst": cst, "cstb": cb, "cstc": cc, "cstd": np.ascontiguousarray(np.eye(128, dtype=np.float32)[::-1])}


def kernel(**inputs):
    import numpy as _np
    import concourse.bacc as _bacc
    from concourse import mybir as _mybir
    from concourse.bass_utils import run_bass_kernel_spmd as _run

    nc = _bacc.Bacc("TRN2", target_bir_lowering=False, num_devices=1)
    arrays, I = {}, {}
    for name in _INS:
        arrays[name] = _np.ascontiguousarray(inputs[name])
    arrays["rel_rev"] = _np.ascontiguousarray(inputs["rel_bias_2"][0, :, ::-1])
    arrays.update(constants())
    for name, a in arrays.items():
        I[name] = nc.dram_tensor(name, a.shape, _mybir.dt.from_np(a.dtype), kind="ExternalInput").ap()
    o = nc.dram_tensor("out0", (1, 512, 1024), F, kind="ExternalOutput").ap()
    build(nc, I, o)
    r = _run(nc, [arrays], core_ids=[0])
    return r.results[0]["out0"]
```

```python
from contextlib import ExitStack

import concourse.bass as bass
from concourse import mybir

F = mybir.dt.float32
FR = mybir.dt.float32r
ALU = mybir.AluOpType
ACT = mybir.ActivationFunctionType
AX = mybir.AxisListType

P = 128
D = 1024
T = 512
MEM = 256
DFF = 2816
ALPHA = 4.0 ** 0.25
NR = 4
NH = 5
EM5 = 0.6065306597126334


class Eng:

    def __init__(self, name, sem):
        self.name, self.sem, self.n, self.q, self.seen, self.last = name, sem, 0, [], {}, None

    def wait(self, *toks):
        for t in toks:
            if t is None:
                continue
            if isinstance(t, list):
                self.wait(*t)
                continue
            sem, v = t
            if self.seen.get(id(sem), 0) >= v:
                continue
            self.seen[id(sem)] = v
            self.q.append(lambda e, s=sem, k=v: e.wait_ge(s, k))

    def op(self, f, *toks, chain=True, inc=True):
        self.wait(*toks)
        if chain:
            self.wait(self.last)
        if not inc:
            self.q.append(f)
            return None
        self.n += 1
        self.q.append(lambda e, g=f, s=self.sem: g(e).then_inc(s, 1))
        self.last = (self.sem, self.n)
        return self.last

    def dma(self, dst, src, ds, *toks):
        self.wait(*toks)
        ds.n += 16
        self.q.append(lambda e: e.dma_start(dst, src).then_inc(ds.sem, 16))
        return (ds.sem, ds.n)


class Count:
    def __init__(self, sem):
        self.sem, self.n = sem, 0


class Bank:

    def __init__(self, t, idle):
        self.t, self.tok, self.idle = t, None, idle
        idle.append(self)

    @property
    def free(self):
        return self.tok

    @free.setter
    def free(self, tok):
        self.tok = tok
        if self in self.idle:
            self.idle.remove(self)
        self.idle.append(self)



VEC_ROWS = [("fcw0", 66), ("fcw1", 66), ("fcb0", 22), ("fcb1", 22), ("ccw", 24), ("psc", 4), ("mu", 17),
            ("w0", 4), ("a0", 4), ("kk", 4), ("ka", 4), ("rk", 4), ("lxg", 4), ("lxb", 4), ("ng", 8),
            ("c", 8), ("ba", 24), ("qg", 1), ("kg", 1)]


def build(nc, I, out):
    ctx = ExitStack()
    with ctx:
        def sb(name, shape, dt=F):
            return ctx.enter_context(nc.sbuf_tensor(name, shape, dt))

        def sem(name):
            return ctx.enter_context(nc.semaphore(name))

        PE = Eng("tensor", sem("s_pe"))
        V = Eng("vector", sem("s_v"))
        A = Eng("scalar", sem("s_a"))
        G = Eng("gpsimd", sem("s_g"))
        S = Eng("sync", sem("s_s"))
        nds = [0]

        def dsem():
            nds[0] += 1
            return Count(sem(f"s_d{nds[0]}"))

        XR = sb("XR", [P, 4, D])
        XH = sb("XH", [P, 8, T], FR)
        XL = sb("XL", [P, 8, T], FR)
        RAW = [sb(f"RAW{i}", [P, 2, 512]) for i in range(NR)]
        WH = [sb(f"WH{i}", [P, 2, 512], FR) for i in range(NH)]
        WL = [sb(f"WL{i}", [P, 2, 512], FR) for i in range(NH)]
        GB = sb("GB", [P, 2048])
        BIG = sb("BIG", [P, 12288])
        LATE = sb("LATE", [P, 8192])
        SCR = sb("SCR", [P, 3136])
        CST = sb("CST", [P, 144])
        VEC = sb("VEC", [P, 384])
        SM = sb("SM", [P, 256])
        d_x = nc.dram_tensor("spill_x", (P, 4096), F, kind="Internal").ap()
        d_g = nc.dram_tensor("spill_g", (P, 2048), F, kind="Internal").ap()
        d_b = nc.dram_tensor("spill_b", (P, 2048), F, kind="Internal").ap()
        d_rel = nc.dram_tensor("rel_padded", (8, 384), F, kind="Internal").ap()
        ident = CST[:, 0:128]
        invc = CST[:, 128:144]
        idle = []
        for i in range(8):
            Bank(ctx.enter_context(nc.psum_tensor(f"ps{i}", [P, 512], F)), idle)

        def bank():
            return idle.pop(0)

        def big(off, n, a=None):
            v = BIG[:, off:off + n]
            return v if a is None else v.rearrange("p (a b) -> p a b", a=a)

        def late(off, n, a=None):
            v = LATE[:, off:off + n]
            return v if a is None else v.rearrange("p (a b) -> p a b", a=a)

        chunks = []

        def w_cols(w, k0, pieces):
            v = w[k0:k0 + 256, :].rearrange("(k p) n -> p k n", p=P)
            at, got = 0, []
            for c0, n in pieces:
                got.append((at, n, v[:, :, c0:c0 + n]))
                at += n
            chunks.append((got, at))

        def w_block(w, c0, n=512, rows=1024):
            for k in range(0, rows, 256):
                w_cols(w, k, [(c0, n)])

        for l in range(2):
            for b in range(4):
                w_block(I["xa_wkv"][l], 512 * b)
        for l in range(2):
            if l == 0:
                for c0 in (512, 1024, 0):
                    w_block(I["ab_w_in"][0], c0)
                for b in range(2):
                    w_block(I["ab_w_out"][0], 512 * b)
            else:
                for c0 in (1024, 2048, 1536, 2560, 0, 512):
                    w_block(I["c_w_in"][0], c0)
                for b in range(2):
                    w_block(I["c_w_out"][0], 512 * b)
            for w in ("xa_wq", "xa_wo"):
                for b in range(2):
                    w_block(I[w][l], 512 * b)
            for i in range(11):
                for k in range(4):
                    w_cols(I["ffn_w_up"][l], 256 * k, [(256 * i, 256), (DFF + 256 * i, 256)])
            for b in range(2):
                w_block(I["ffn_w_down"][l], 512 * b, rows=DFF)
        for c0, n in ((2176, 512), (2688, 512), (3200, 512), (3712, 512),
                      (0, 512), (512, 512), (1024, 512), (1536, 512), (2048, 128)):
            w_block(I["w_in_2"][0], c0, n)
        for b in range(2):
            w_block(I["w_out_2"][0], 512 * b)

        raw_ds = [dsem() for _ in range(NR)]
        dma_tok, conv_tok, rel_tok = {}, {}, {}
        pos = {"dma": 0, "conv": 0, "get": 0}

        def w_pump():
            while True:
                moved = False
                i = pos["dma"]
                old = i - NR
                free = conv_tok.get(old)
                if i < len(chunks) and (old < 0 or free):
                    for at, n, src in chunks[i][0]:
                        dma_tok[i] = S.dma(RAW[i % NR][:, :, at:at + n], src, raw_ds[i % NR], free)
                    pos["dma"] += 1
                    moved = True
                i = pos["conv"]
                if i < len(chunks) and i in dma_tok and (i < NH or i - NH in rel_tok):
                    n = chunks[i][1]
                    raw, hi, lo = RAW[i % NR][:, :, 0:n], WH[i % NH][:, :, 0:n], WL[i % NH][:, :, 0:n]
                    th = A.op(lambda e, hi=hi, raw=raw: e.activation(hi, raw, ACT.Copy), dma_tok[i], rel_tok.get(i - NH),
                              chain=False)
                    conv_tok[i] = V.op(lambda e, hi=hi, lo=lo, raw=raw: e.tensor_tensor(lo, raw, hi.bitcast(F), ALU.subtract),
                                       th, chain=False)
                    pos["conv"] += 1
                    moved = True
                if not moved:
                    return

        def w_get():
            i = pos["get"]
            pos["get"] += 1
            return i, WH[i % NH], WL[i % NH], conv_tok[i]

        def w_release(i, tok, pump=True):
            rel_tok[i] = tok
            if pump:
                w_pump()

        def mm(o, l, r, start, stop, *toks, inc=False):
            return PE.op(lambda e: e.matmul(o, l, r, start=start, stop=stop), *toks, chain=False, inc=inc)

        def mm3(o, lh, ll, rh, rl, start, stop, *toks, inc=False):
            mm(o, lh, rh, start, False, *toks)
            mm(o, lh, rl, False, False)
            return mm(o, ll, rh, False, stop, inc=inc)

        def tr(o, i, *toks, inc=False, n=128):
            return PE.op(lambda e: e.transpose(o, i, ident[0:n, 0:n]), *toks, chain=False, inc=inc)

        def act(o, i, f, *toks, chain=True, **kw):
            return A.op(lambda e: e.activation(o, i, f, **kw), *toks, chain=chain)

        def tt(o, a, b, op, *toks, eng=None, chain=True):
            return (eng or V).op(lambda e: e.tensor_tensor(o, a, b, op), *toks, chain=chain)

        def ts(o, a, s1, s2, op0, op1, *toks, eng=None, chain=True):
            if s2 is None:
                return (eng or V).op(lambda e: e.tensor_scalar(o, a, s1, None, op0), *toks, chain=chain)
            return (eng or V).op(lambda e: e.tensor_scalar(o, a, s1, s2, op0, op1), *toks, chain=chain)

        def stt(o, a, s, b, op0, op1, *toks, chain=True):
            return V.op(lambda e: e.scalar_tensor_tensor(out=o, in0=a, scalar=s, in1=b, op0=op0, op1=op1),
                        *toks, chain=chain)

        def memset(eng, o, v, *toks):
            return eng.op(lambda e: e.memset(o, v), *toks)

        def split(hi, lo, src, *toks):
            th = act(hi, src, ACT.Copy, *toks, chain=False)
            return tt(lo, src, hi.bitcast(F), ALU.subtract, th, *toks, chain=False)

        def proj_t(xh, xl, nk2, ntok, nm, evac, *toks, late=None, side=None):
            if late:
                for t in (0, 1):
                    t_h = turned.pop(t) if t in turned else late(t)
                bs = [bank() for _ in range(nm)]
                gots = [w_get() for _ in range(nk2)]
                for half in range(2):
                    if half:
                        for t in (2, 3):
                            t_h = late(t)
                    cs = slice(256 * half, 256 * half + 256)
                    done = []
                    for c, (i, wh, wl, tok) in enumerate(gots):
                        for m in range(nm):
                            for k in range(2):
                                kt = 2 * c + k
                                last = c == nk2 - 1 and k == 1
                                t = mm3(bs[m].t[:, cs], wh[:, k, 128 * m:128 * m + 128], wl[:, k, 128 * m:128 * m + 128],
                                        xh[:, kt, cs], xl[:, kt, cs], kt == 0, last, tok, t_h,
                                        bs[m].free if kt == 0 else None, *toks,
                                        inc=last or (m == nm - 1 and k == 1))
                                if last:
                                    done.append(t)
                        if half:
                            w_release(i, t)
                for m in range(nm):
                    evac(m, bs[m], done[m])
                return t_h
            bs = [bank() for _ in range(nm)]
            done = []
            for c in range(nk2):
                i, wh, wl, tok = w_get()
                for m in range(nm):
                    for k in range(2):
                        kt = 2 * c + k
                        last = c == nk2 - 1 and k == 1
                        t = mm3(bs[m].t[:, 0:ntok], wh[:, k, 128 * m:128 * m + 128], wl[:, k, 128 * m:128 * m + 128],
                                xh[:, kt, 0:ntok], xl[:, kt, 0:ntok], kt == 0, last, tok,
                                bs[m].free if kt == 0 else None, *toks, inc=last or (m == nm - 1 and k == 1))
                        if last:
                            done.append(t)
                    if side and m == 1:
                        side()
                w_release(i, t)
                if side:
                    side()
            for m in range(nm):
                evac(m, bs[m], done[m])

        def proj_n(xa, nk2, evac, final, *toks, nt=4, kt_tok=None, ahead=None, done_k=None, between=None):
            bs = [bank() for _ in range(nt)]
            done = []
            cut = nk2 - 4 if final else nk2

            def part(c, got, t):
                i, wh, wl, tok = got
                for k in range(2):
                    kt = 2 * c + k
                    xh, xl = xa(kt, t)
                    last = c == nk2 - 1 and k == 1
                    r = mm3(bs[t].t[:, :], xh, xl, wh[:, k, :], wl[:, k, :], kt == 0, last, tok,
                            bs[t].free if kt == 0 else None, kt_tok[kt] if kt_tok else None, *toks,
                            inc=last or (t == nt - 1 and k == 1))
                return r

            for c in range(cut):
                got = w_get()
                for t in range(nt):
                    r = part(c, got, t)
                    if c == nk2 - 1:
                        done.append(r)
                if done_k:
                    done_k(c, r)
                w_release(got[0], r)
                if ahead:
                    ahead(c + 3)
            if not final:
                for t in range(nt):
                    evac(t, bs[t], done[t])
                return
            gots = [w_get() for _ in range(4)]
            if ahead:
                ahead(nk2 - 1)
            rels = {}
            for t in range(nt):
                for c in range(cut, nk2):
                    r = part(c, gots[c - cut], t)
                    rels[c] = r
                if t >= 2 and between:
                    between(t - 2)
                if t == nt - 1 and not between:
                    evac(t, bs[t], r)
                if t == nt - 1:
                    for c in range(cut, nk2):
                        if done_k:
                            done_k(c, rels[c])
                        w_release(gots[c - cut][0], rels[c], c < nk2 - 1)
                if t < nt - 1 or between:
                    evac(t, bs[t], r)
            w_pump()

        tc = A.dma(CST[:, :], I["cst"], dsem())
        t_mem = A.dma(big(0, 2048, 2), I["mem"][0].rearrange("(a p) n -> p a n", p=P), dsem())
        xin = dsem()
        t_x = A.dma(XR[:, :, :], I["x"][0].rearrange("(a p) n -> p a n", p=P), xin)

        def rows(name):
            r = {
                "fcw0": I["ffn_conv_w"][0].rearrange("k (m c) -> (k m) c", c=P),
                "fcw1": I["ffn_conv_w"][1].rearrange("k (m c) -> (k m) c", c=P),
                "ccw": I["c_conv_w"][0].rearrange("k (m c) -> (k m) c", c=P),
            }
            if name in r:
                return [r[name]]
            if name in ("qg", "kg"):
                v = I["q_norm_g_2" if name == "qg" else "k_norm_g_2"]
                return [v, v]
            v = {
                "fcb0": I["ffn_conv_b"][0:1], "fcb1": I["ffn_conv_b"][1:2], "psc": I["pool_scale"],
                "mu": I["mu_shift_2"], "w0": I["w0_2"], "a0": I["a0_2"], "kk": I["k_k_2"], "ka": I["k_a_2"],
                "lxg": I["lnx_g_2"], "lxb": I["lnx_b_2"], "ng": I["norm_g_2"], "c": I["c_2"],
                "ba": I["b_ada_2"],
            }
            if name == "rk":
                return [I["r_k_2"][0].rearrange("(a b) c -> a (b c)", b=2)]
            return [v[name].rearrange("a (m c) -> (a m) c", c=P)]

        vcol = {}
        r0 = 0
        vds = dsem()
        stg = big(2048, 384, 3)
        t_vm = memset(V, stg, 0.0)
        for name, n in VEC_ROWS:
            vcol[name] = r0
            aps = rows(name)
            if len(aps) == 2:
                for h, a in enumerate(aps):
                    t_v = G.dma(stg[r0 % 128:r0 % 128 + 1, r0 // 128, 64 * h:64 * h + 64], a, vds, t_vm)
            else:
                a, at = aps[0], 0
                while at < n:
                    m = min(n - at, 128 - (r0 + at) % 128)
                    t_v = G.dma(stg[(r0 + at) % 128:(r0 + at) % 128 + m, (r0 + at) // 128, :], a[at:at + m, :], vds, t_vm)
                    at += m
            r0 += n
        assert r0 <= 384

        def vec(name, j=0):
            return VEC[:, vcol[name] + j:vcol[name] + j + 1]

        w_pump()
        nhalf = SM[:, 0:32]
        t_nh = memset(V, nhalf, -0.5)

        def transposes(src, nt, n0=0, *toks):
            for t in range(n0, n0 + nt):
                for q in range(2):
                    b = bank()
                    for k in range(4):
                        r = tr(b.t[:, 128 * k:128 * k + 128], src(t, 4 * q + k), b.free, *toks, inc=k == 3)
                    b.free = split(XH[:, 4 * q:4 * q + 4, 128 * t:128 * t + 128],
                                   XL[:, 4 * q:4 * q + 4, 128 * t:128 * t + 128],
                                   b.t[:, :].rearrange("p (k n) -> p k n", k=4), r)
            return b.free

        memt = big(0, 2048, 2)
        tx = transposes(lambda t, k: memt[:, t, 128 * k:128 * k + 128], 2, 0, tc, t_mem)
        KT = [late(4096 * l, 2048, 8) for l in range(2)]
        VT = [late(4096 * l + 2048, 2048, 2) for l in range(2)]
        for l in range(2):
            for nb in range(2):
                def evk(m, b, tok, l=l, nb=nb):
                    b.free = act(KT[l][:, 4 * nb + m, :], b.t[:, 0:256], ACT.Copy, tok, chain=False)
                proj_t(XH, XL, 4, 256, 4, evk, tx)
            for nb in range(2):
                def evv(t, b, tok, l=l, nb=nb):
                    b.free = act(VT[l][:, t, 512 * nb:512 * nb + 512], b.t[:, :], ACT.Copy, tok, chain=False)
                proj_n(lambda kt, t: (XH[:, kt, 128 * t:128 * t + 128], XL[:, kt, 128 * t:128 * t + 128]), 4, evv,
                       False, tx, nt=2)
        t_kv = A.last
        b = bank()
        for j in range(3):
            t = tr(b.t[:, 128 * j:128 * j + 128], stg[:, j, :], tc, t_v, t_vm, b.free, inc=j == 2)
        t_vec = b.free = V.op(lambda e, b=b: e.tensor_copy(VEC[:, :], b.t[:, 0:384]), t)

        def xa_x(kt, t):
            return XH[:, kt, 128 * t:128 * t + 128], XL[:, kt, 128 * t:128 * t + 128]

        def load_gb(g, b, tok, n=D):
            ds = dsem()
            G.dma(GB[:, 0:n], g.partition_broadcast(P), ds, tok)
            return G.dma(GB[:, 1024:1024 + n], b.partition_broadcast(P), ds, tok)

        stats = SM[:, 64:112].rearrange("p (t j s) -> p t j s", t=4, j=2)
        mv = SM[:, 112:120].rearrange("p (t s) -> p t s", s=2)
        vr = SM[:, 120:124]
        rs = SM[:, 124:128]

        def norm(x, t, nstat, g, b, tgb):
            a = V.op(lambda e: e.bn_aggr(mv[:, t, :], stats[:, t, 0:nstat, :]))
            ts(vr[:, t:t + 1], mv[:, t, 1:2], 1e-5, None, ALU.add, None, a, eng=G)
            r = tt(rs[:, t:t + 1], vr[:, t:t + 1], nhalf[:, 0:1], ALU.pow, t_nh, eng=G)
            stt(x, x, mv[:, t, 0:1], g, ALU.subtract, ALU.mult, tgb)
            return stt(x, x, rs[:, t:t + 1], b, ALU.mult, ALU.add, r)

        def ln_in(j, t, b, tok):
            o = XR[:, t, 512 * j:512 * j + 512]
            b.free = stt(o, o, ALPHA, b.t[:, :], ALU.mult, ALU.add, tok)
            return V.op(lambda e: e.bn_stats(stats[:, t, j, :], o))

        def turn(t):
            return transposes(lambda t, k: XR[:, t, 128 * k:128 * k + 128], 1, t, lnr[t])

        lnr, turned = {}, {}

        def turn_early(t):
            turned[t] = turn(t)

        def out_ln(xa, nk2, tgb, kt_tok=None, prep=None, more=True, after=None):
            for j in range(2):
                def ev(t, b, tok, j=j):
                    ln_in(j, t, b, tok)
                    if j == 1:
                        lnr[t] = norm(XR[:, t, :], t, 2, GB[:, 0:1024], GB[:, 1024:2048], tgb)
                        if after:
                            after(t)
                p = prep[j] if prep else {}
                proj_n(xa, nk2, ev, j == 1, kt_tok=p.get("tok", kt_tok), ahead=p.get("ahead"), done_k=p.get("done"),
                       between=turn_early if j == 1 and more else None)
            return lnr[3]

        t_gb = load_gb(I["ln_mix_g"][0], I["ln_mix_b"][0], None)
        tx = transposes(lambda t, k: XR[:, t, 128 * k:128 * k + 128], 4, 0, t_x)

        def mixer_ab():
            nonlocal tx
            uT = big(0, 2048, 4)
            vt = big(2048, 2048, 4)
            xb = big(4096, 2112, 4)
            pp = [big(6208 + 528 * i, 528) for i in range(2)]
            pooled = big(7264, 2048, 4)
            wraw = big(9312, 512, 4)
            wmT = big(9824, 512, 4)
            bs = big(10336, 512, 4)
            pw = big(10848, 512, 4)
            lg = SCR[:, 0:512]
            lb = SCR[:, 512:1024]
            sp = SCR[:, 1024:3072].rearrange("p (g n) -> p g n", g=4)
            edge = SCR[:, 3072:3088]
            ds = dsem()
            G.dma(wraw, I["sgu_w"][0].rearrange("g i j -> i g j"), ds, V.last, PE.last)
            G.dma(bs, I["sgu_b"][0].partition_broadcast(P), ds)
            G.dma(pw, I["pool_w"][0].rearrange("g c d -> c g d"), ds)
            G.dma(lg, I["sgu_ln_g"][0].partition_broadcast(P), ds)
            t_l = G.dma(lb, I["sgu_ln_b"][0].partition_broadcast(P), ds)
            tm = memset(G, xb[:, :, 0:16], 0.0, V.last, PE.last)
            memset(G, pp[0][:, 0:16], 0.0)
            tm = memset(G, pp[1][:, 0:16], 0.0)

            def ev_v(t, b, tok):
                o = vt[:, t, :]
                a = b.free = act(o, b.t[:, :], ACT.Gelu_apprx_tanh, tok)
                V.op(lambda e: e.bn_stats(stats[:, t, 0, :], o), a)
                norm(o, t, 1, lg, lb, t_l)

            proj_n(xa_x, 4, ev_v, False, tx)
            t_vt = V.last
            b = bank()
            for g in range(4):
                r = tr(b.t[:, 128 * g:128 * g + 128], wraw[:, g, :], t_l, b.free, inc=g == 3)
            b.free = V.op(lambda e, b=b: e.tensor_copy(wmT, b.t[:, :].rearrange("p (g i) -> p g i", g=4)), r)
            t_wm = memset(V, wmT[64:128, :, 0:64], 0.0)

            def ev_b(m, b, tok):
                b.free = act(xb[:, m, 16:528], b.t[:, :], ACT.Copy, tok, tm)

            proj_t(XH, XL, 4, 512, 4, ev_b, tx)
            t_xb = A.last
            for g in range(4):
                b = bank()
                for n in range(4):
                    r = mm(b.t[:, 128 * n:128 * n + 128], vt[:, n, 128 * g:128 * g + 128], wmT[:, g, :], True, True,
                           t_vt, t_wm, b.free, inc=n == 3)
                bb = bs[:, g, :].unsqueeze(1).broadcast_to([P, 4, 128])
                b.free = tt(sp[:, g, :].rearrange("p (n i) -> p n i", n=4),
                            b.t[:, :].rearrange("p (n i) -> p n i", n=4), bb, ALU.add, r, t_l)
            t_pool, calls = [], [0]

            def pool():
                calls[0] += 1
                if calls[0] % 2:
                    return
                g = len(t_pool)
                w = 2 << g
                src = xb[:, g, :]
                for s in range(g + 1):
                    dst = pp[s % 2]
                    tt(dst[:, 16:528], src[:, 16:528], src[:, 16 - (1 << s):528 - (1 << s)], ALU.add, t_xb, tm)
                    src = dst
                stt(pooled[:, g, :], src[:, 16:528], 1.0 / w, xb[:, g, 16:528], ALU.mult, ALU.subtract)
                tt(edge[:, 0:w], src[:, 16:16 + w], invc[:, 0:w], ALU.mult)
                t_pool.append(tt(pooled[:, g, 0:w], edge[:, 0:w], xb[:, g, 16:16 + w], ALU.subtract))

            toks = []

            def ev_u(m, b, tok):
                b.free = a = act(uT[:, m, :], b.t[:, :], ACT.Gelu_apprx_tanh, tok)
                r = tt(uT[:, m, :], uT[:, m, :], sp[:, m, :], ALU.mult, a)
                toks.append(split(XH[:, m, :], XL[:, m, :], uT[:, m, :], r, PE.last))

            proj_t(XH, XL, 4, 512, 4, ev_u, tx, side=pool)
            pe = PE.last
            for g in range(4):
                b = bank()
                r = mm(b.t[:, :], pw[:, g, :], pooled[:, g, :], True, True, t_pool[g], t_l, b.free, inc=True)
                b.free = r = ts(pooled[:, g, :], b.t[:, :], vec("psc", g), None, ALU.mult, None, r, t_vec)
                toks.append(split(XH[:, 4 + g, :], XL[:, 4 + g, :], pooled[:, g, :], r, pe))
            return toks

        def mixer_c():
            nonlocal tx
            ch = big(0, 4112, 8)
            cv = big(4112, 4096, 8)
            tm = memset(V, ch[:, :, 0:2], 0.0, PE.last)
            for hf in range(2):
                def ev_c(m, b, tok, hf=hf):
                    b.free = act(ch[:, 4 * hf + m, 2:514], b.t[:, :], ACT.Copy, tok, tm, V.last)

                def ev_h(m, b, tok, hf=hf):
                    j = 4 * hf + m
                    c, x = cv[:, j, :], ch[:, j, :]
                    b.free = tt(x[:, 2:514], x[:, 2:514], b.t[:, :], ALU.mult, tok, t_c)
                    ts(c, x[:, 2:514], vec("ccw", 16 + j), None, ALU.mult, None, t_vec)
                    stt(c, x[:, 1:513], vec("ccw", 8 + j), c, ALU.mult, ALU.add)
                    stt(c, x[:, 0:512], vec("ccw", j), c, ALU.mult, ALU.add)

                if hf == 0:
                    tx = proj_t(XH, XL, 4, 512, 4, ev_c, late=turn)
                else:
                    proj_t(XH, XL, 4, 512, 4, ev_c, tx)
                t_c = A.last
                proj_t(XH, XL, 4, 512, 4, ev_h, tx)
            t_cv = []
            for hf in range(2):
                def ev_g(m, b, tok, hf=hf):
                    c = cv[:, 4 * hf + m, :]
                    b.free = tt(c, c, b.t[:, :], ALU.mult, tok)
                    t_cv.append(b.free)

                proj_t(XH, XL, 4, 512, 4, ev_g, tx)
            pe = PE.last
            return [split(XH[:, j, :], XL[:, j, :], cv[:, j, :], t_cv[j], pe) for j in range(8)]

        def cross(l):
            nonlocal tx
            qT = big(0, 4096, 8)
            Pm = [big(4096 + 1024 * i, 1024, 4) for i in range(3)]
            PT = [big(7168 + 1024 * i, 1024, 2) for i in range(2)]
            mx = SM[:, 32:44].rearrange("p (i t) -> p i t", i=3)
            sm = SM[:, 44:56].rearrange("p (i t) -> p i t", i=3)
            tp = [V.last, PE.last]
            for nb in range(2):
                def evq(m, b, tok, nb=nb):
                    b.free = act(qT[:, 4 * nb + m, :], b.t[:, :], ACT.Copy, tok, *tp, chain=False)
                if nb == 0:
                    tx = proj_t(XH, XL, 4, 512, 4, evq, late=turn)
                else:
                    proj_t(XH, XL, 4, 512, 4, evq, tx)
            tq, pq = A.last, PE.last
            pt_free = [None] * 3
            state = {}

            def scores(h):
                i = h % 3
                banks2 = []
                for tp2 in range(2):
                    b = bank()
                    for t in range(2):
                        tt_ = 2 * tp2 + t
                        for k in range(2):
                            r = mm(b.t[:, 256 * t:256 * t + 256], qT[:, 2 * h + k, 128 * tt_:128 * tt_ + 128],
                                   KT[l][:, 2 * h + k, :], k == 0, k == 1, tq, t_kv, b.free, inc=t == 1 and k == 1)
                    banks2.append((b, r))
                for tp2, (b, r) in enumerate(banks2):
                    v = b.t[:, :].rearrange("p (t m) -> p t m", t=2)
                    m2 = mx[:, i, 2 * tp2:2 * tp2 + 2]
                    r = V.op(lambda e, m2=m2, v=v: e.tensor_reduce(m2, v, AX.X, ALU.max), r, pt_free[i])
                    r = ts(m2, m2, -0.0625, None, ALU.mult, None)
                    for t in range(2):
                        tt_ = 2 * tp2 + t
                        a = act(Pm[i][:, tt_, :], v[:, t, :], ACT.Exp, r, pt_free[i], scale=0.0625,
                                bias=mx[:, i, tt_:tt_ + 1], accum_out=sm[:, i, tt_:tt_ + 1], chain=False)
                    b.free = a
                r = V.op(lambda e: e.reciprocal(sm[:, i, :], sm[:, i, :]), a)
                state[h] = [ts(Pm[i][:, t, :], Pm[i][:, t, :], sm[:, i, t:t + 1], None, ALU.mult, None, r, chain=False)
                            for t in range(4)]

            def values(h):
                i = h % 3
                pt = PT[h % 2]
                ts_ = []
                for mt in range(2):
                    b = bank()
                    for t in range(4):
                        r = tr(b.t[:, 128 * t:128 * t + 128], Pm[i][:, t, 128 * mt:128 * mt + 128], state[h], b.free,
                               inc=t == 3)
                    b.free = act(pt[:, mt, :], b.t[:, :], ACT.Copy, r, pv_done.get(h - 2), chain=False)
                    ts_.append(b.free)
                pt_free[i] = r
                for d in range(2):
                    b = bank()
                    for mt in range(2):
                        r = mm(b.t[:, :], VT[l][:, mt, 256 * h + 128 * d:256 * h + 128 * d + 128], pt[:, mt, :],
                               mt == 0, mt == 1, ts_[mt], b.free, inc=mt == 1)
                    b.free = split(XH[:, 2 * h + d, :], XL[:, 2 * h + d, :], b.t[:, :], r, pq)
                    ty.append(b.free)
                pv_done[h] = r

            ty, pv_done = [], {}
            scores(0)
            scores(1)
            for h in range(4):
                if h < 2:
                    scores(h + 2)
                values(h)
            return ty

        mod = SM[:, 148:172]
        n_ada = [0, 0]
        s1, ss, rq = SM[:, 172:180], SM[:, 180:184], SM[:, 184:188]
        xn = big(0, 4096, 4)
        t_n, t_mod = [], []

        def rms(t):
            if t == 0:
                t_mod.append(stt(s1, mod[:, 8:16], 1.0, VEC[:, vcol["ng"]:vcol["ng"] + 8], ALU.add, ALU.mult))
            a = act(SCR[:, 0:1024], XR[:, t, :], ACT.Square, lnr[t], accum_out=ss[:, t:t + 1])
            ts(ss[:, t:t + 1], ss[:, t:t + 1], 1.0 / D, 1e-6, ALU.mult, ALU.add, a, eng=G)
            r = tt(rq[:, t:t + 1], ss[:, t:t + 1], nhalf[:, 0:1], ALU.pow, eng=G)
            t_n.append(act(xn[:, t, :], XR[:, t, :], ACT.Copy, r, scale=rq[:, t:t + 1]))


        ada = [late(1024 * i, 1024, 2) for i in range(4)]
        ada_ds = [dsem() for _ in range(4)]
        ada_tok = {}

        def ada_load(a, *toks):
            if a < 24:
                k, c = 256 * (a % 4), 512 * (a // 4)
                src = I["w_ada_2"][0][k:k + 256, c:c + 512].rearrange("(k p) n -> p k n", p=P)
                ada_tok[a] = S.dma(ada[a % 4], src, ada_ds[a % 4], *toks)

        acc, one = SCR[:, 2056:2568], SM[:, 56:57]

        def ada_steps():
            t_one = memset(G, one, 1.0)
            r_pe = None
            for nb in range(6):
                for k in range(8):
                    a = 4 * nb + k // 2
                    raw = ada[a % 4][:, k % 2, :]
                    if k == 0:
                        r = ts(acc, raw, ca[:, 0:1], None, ALU.mult, None, ada_tok[a], t_c, r_pe, A.last)
                    else:
                        r = stt(acc, raw, ca[:, k:k + 1], acc, ALU.mult, ALU.add, ada_tok[a], t_c)
                    if k % 2:
                        ada_load(a + 4, r)
                    yield
                b = bank()
                for m in range(4):
                    r_pe = mm(b.t[:, m:m + 1], acc[:, 128 * m:128 * m + 128], one, True, True, r, t_one, b.free, inc=m == 3)
                yield
                b.free = tt(mod[:, 4 * nb:4 * nb + 4], VEC[:, vcol["ba"] + 4 * nb:vcol["ba"] + 4 * nb + 4], b.t[:, 0:4],
                            ALU.add, r_pe, t_vec)
                yield

        ada_run = ada_steps()

        def modulation():
            n_ada[0] += 1
            if n_ada[0] * 62 // 160 > n_ada[1]:
                n_ada[1] += 1
                next(ada_run, None)

        def ffn_up(l, h_tok, before_last):
            nonlocal tx
            hT = big(0, 11264, 22)
            gp = [SCR[:, 514 * i:514 * i + 514] for i in range(2)]
            cv = [SCR[:, 1028 + 512 * i:1540 + 512 * i] for i in range(2)]
            tm = V.last
            for i in range(2):
                tm = memset(V, gp[i][:, 0:2], 0.0, A.last)
            cvfree = [[None], [None]]
            tp = PE.last
            for nb in range(11):
                bk = {}

                def ev(m, b, tok, nb=nb, bk=bk):
                    bk[m] = (b, tok)
                    if m < 2:
                        return
                    i = m - 2
                    j = 2 * nb + i
                    g, c = gp[i], cv[i]
                    b.free = a = act(g[:, 2:514], b.t[:, :], ACT.Copy, tok, tm, cvfree[i][0], chain=False)
                    ts(c, g[:, 2:514], vec(f"fcw{l}", 44 + j), None, ALU.mult, None, a)
                    stt(c, g[:, 1:513], vec(f"fcw{l}", 22 + j), c, ALU.mult, ALU.add)
                    r = stt(c, g[:, 0:512], vec(f"fcw{l}", j), c, ALU.mult, ALU.add)
                    a = act(c, c, ACT.Gelu_apprx_tanh, r, bias=vec(f"fcb{l}", j))
                    ba, ta = bk[i]
                    ba.free = cvfree[i][0] = h_tok[j] = tt(hT[:, j, :], c, ba.t[:, :], ALU.mult, a, ta, tp)

                def ev_last(m, b, tok, ev=ev):
                    if m == 0:
                        before_last()
                    ev(m, b, tok)

                if nb == 0:
                    tx = proj_t(XH, XL, 4, 512, 4, ev, t_vec, late=turn)
                else:
                    proj_t(XH, XL, 4, 512, 4, ev_last if nb == 10 else ev, tx, t_vec, side=modulation)

        def ffn(l, tgb):
            hT = big(0, 11264, 22)
            free, h_tok = {}, {}
            toks = [{}, {}]

            def ahead(j, c):
                if c > 10:
                    j, c = j + 1, c - 11
                if j > 1:
                    return
                for kt in (2 * c, 2 * c + 1):
                    toks[j][kt] = split(XH[:, kt % 8, :], XL[:, kt % 8, :], hT[:, kt, :], h_tok[kt], free[kt % 8])

            def done(c, r):
                for kt in (2 * c, 2 * c + 1):
                    free[kt % 8] = r

            def before_last():
                for i in range(8):
                    free[i] = PE.last
                for c in range(3):
                    ahead(0, c)

            ffn_up(l, h_tok, before_last)
            prep = [{"tok": toks[j], "ahead": lambda c, j=j: ahead(j, c), "done": done} for j in range(2)]
            return out_ln(lambda kt, t: (XH[:, kt % 8, 128 * t:128 * t + 128], XL[:, kt % 8, 128 * t:128 * t + 128]),
                          11, tgb, None, prep, more=l == 0, after=rms if l == 1 else None)

        t_early = []

        def early_loads():
            ds = dsem()
            G.dma(late(4096, 2048)[0:64, 512:1024], I["w2_2"][0], ds, V.last, A.last, PE.last)
            G.dma(late(4096, 2048)[64:128, 512:1024], I["a2_2"][0], ds)
            G.dma(late(6144, 2048).rearrange("p (h k) -> p h k", h=8),
                  bass.AP(tensor=d_rel.tensor, offset=0, ap=[[1, 128], [384, 8], [1, 256]]), ds, t_rel)
            t_early.append(G.dma(SCR[:, 2600:2728], I["cstd"], ds))

        def layers():
            nonlocal t_gb
            for l in range(2):
                ty = mixer_ab() if l == 0 else mixer_c()
                tl = out_ln(xa_x, 4, t_gb, ty)
                t_gb = load_gb(I["ln_xa_g"][l], I["ln_xa_b"][l], tl)
                ty = cross(l)
                tl = out_ln(xa_x, 4, t_gb, ty)
                t_gb = load_gb(I["ln_ffn_g"][l], I["ln_ffn_b"][l], tl)
                if l == 0:
                    for a in range(4):
                        ada_load(a, PE.last)
                else:
                    early_loads()
                tl = ffn(l, t_gb)
                if l == 0:
                    t_gb = load_gb(I["ln_mix_g"][1], I["ln_mix_b"][1], tl)


        def second():
            nonlocal tx
            B = [big(2048 * i, 2048) for i in range(6)]
            L = [late(2048 * i, 2048) for i in range(4)]

            def v4(x):
                return x.rearrange("p (a b) -> p a b", a=4)

            V.wait(t_rel)
            t_spx = A.dma(d_x, XR[:, :, :], dsem(), t_xr)
            hs = [SCR[:, 512 * i:512 * i + 512] for i in range(4)]
            hfree = [t_n] * 4
            made, t_kt = [], {}

            def low(k, h, th):
                t_kt[k] = hfree[k % 4] = tt(XL[:, k, :], h, XH[:, k, :].bitcast(F), ALU.subtract, th, chain=False)

            for k in range(8):
                b = bank()
                for t in range(4):
                    r = tr(b.t[:, 128 * t:128 * t + 128], xn[:, t, 128 * k:128 * k + 128], *t_n, b.free, inc=t == 3)
                h = hs[k % 4]
                if k % 2:
                    b.free = r = act(h, b.t[:, :], ACT.Identity, r, *t_mod, hfree[k % 4], scale=s1[:, k:k + 1],
                                     bias=mod[:, k:k + 1], chain=False)
                else:
                    b.free = r = ts(h, b.t[:, :], s1[:, k:k + 1], mod[:, k:k + 1], ALU.mult, ALU.add, r, *t_mod,
                                    hfree[k % 4], chain=False)
                made.append((k, h, act(XH[:, k, :], h, ACT.Copy, r, chain=False)))
                if k:
                    low(*made[k - 1])
            low(*made[7])
            tx = V.last

            qtok, ktok, va, sga = v4(B[0]), v4(B[1]), v4(B[2]), v4(B[3])
            R, K, Vt, Gt = v4(B[4]), v4(B[5]), v4(L[0]), v4(L[1])
            wd = L[2][:, 0:512]
            w2a2 = L[2][:, 512:1024]
            bias = GB[:, :].rearrange("p (h k) -> p h k", h=8)
            rev, exch = L[3], SCR[:, 2600:2728]
            t_w2 = t_early[0]
            tpr = [V.last, A.last, PE.last]

            t_ga, t_att = [], []

            def attention(t_qkv, t_bi, t_first):
                sq = SCR[:, 1040:2064].rearrange("p (i n) -> p i n", i=2)
                ssq = SM[:, 188:252].rearrange("p (i n) -> p i n", i=2)
                for i, x in enumerate((qtok, ktok)):
                    for t in range(4):
                        a = act(sq[:, t % 2, :], x[:, t, :], ACT.Square, t_qkv, V.last)
                        r = V.op(lambda e, i=i, t=t: e.tensor_reduce(
                            ssq[:, i, 8 * t:8 * t + 8], sq[:, t % 2, :].rearrange("p (h d) -> p h d", h=8), AX.X, ALU.add),
                            a)
                    yield
                    yield
                r = ts(SM[:, 188:252], SM[:, 188:252], 1.0 / 64, 1e-6, ALU.mult, ALU.add)
                a = act(SM[:, 188:252], SM[:, 188:252], ACT.Sqrt, r)
                r = V.op(lambda e: e.reciprocal(SM[:, 188:252], SM[:, 188:252]), a)
                t_n = []
                for i, x in enumerate((qtok, ktok)):
                    for t in range(4):
                        x3 = x[:, t, :].rearrange("p (h d) -> p h d", h=8)
                        s3 = ssq[:, i, 8 * t:8 * t + 8].unsqueeze(2).broadcast_to([P, 8, 64])
                        t_n.append(tt(x3, x3, s3, ALU.mult, r, chain=False))
                    yield
                    yield
                qT, kT = v4(L[3]), v4(B[0])
                for i, (x, dst, g) in enumerate(((qtok, qT, "qg"), (ktok, kT, "kg"))):
                    for t in range(4):
                        b = bank()
                        for m in range(4):
                            rr = tr(b.t[:, 128 * m:128 * m + 128], x[:, t, 128 * m:128 * m + 128], t_n[4 * i + t], b.free,
                                    inc=m == 3)
                        b.free = t_qk = ts(dst[:, :, 128 * t:128 * t + 128],
                                           b.t[:, :].rearrange("p (m n) -> p m n", m=4), vec(g), None, ALU.mult, None, rr, chain=False)
                    yield
                    yield
                PT = v4(B[1])
                Sb = [SCR[:, 2064:2576], SCR[:, 2576:3088], L[2][:, 1024:1536], L[2][:, 1536:2048]]
                am, asum = SM[:, 132:140], SM[:, 140:148]
                sb_free = [t_first] * 4
                t_pt = [None]

                def scores(n):
                    h = n // 4
                    hp, ps = h // 2, slice(64 * (h % 2), 64 * (h % 2) + 64)
                    i = n % 8
                    got, t_b = [], []
                    for k in (n, n + 1):
                        q, nk = k % 4, 128 * (k % 4 + 1)
                        b = bank()
                        r = mm(b.t[:, 0:nk], qT[ps, hp, 128 * q:128 * q + 128], kT[ps, hp, 0:nk], True, True, t_qk,
                               b.free, inc=True)
                        got.append((b, r, nk, Sb[k % 4]))
                    for k, (b, r, nk, s) in enumerate(got, n):
                        lo = max(0, nk - 256)
                        if lo:
                            ts(s[:, 0:lo], b.t[:, 0:lo], 0.125, bias[:, h, 0:1], ALU.mult, ALU.add, r, t_bi,
                               sb_free[k % 4], chain=False)
                        b.free = stt(s[:, lo:nk], b.t[:, lo:nk], 0.125, bias[:, h, 256 - (nk - lo):256], ALU.mult, ALU.add,
                                     r, t_bi, sb_free[k % 4], chain=False)
                        t_b.append(b.free)
                    for j, (b, r, nk, s) in enumerate(got):
                        V.op(lambda e, j=j, s=s, nk=nk: e.tensor_reduce(am[:, i + j:i + j + 1], s[:, 0:nk], AX.X, ALU.max),
                             t_b[j], chain=False)
                    r = ts(am[:, i:i + 2], am[:, i:i + 2], -1.0, None, ALU.mult, None)
                    for j, (b, _, nk, s) in enumerate(got):
                        a = act(s[:, 0:nk], s[:, 0:nk], ACT.Exp, r, bias=am[:, i + j:i + j + 1],
                                accum_out=asum[:, i + j:i + j + 1], chain=False)
                    r = V.op(lambda e: e.reciprocal(asum[:, i:i + 2], asum[:, i:i + 2]), a, chain=False)
                    return [ts(s[:, 0:nk], s[:, 0:nk], asum[:, i + j:i + j + 1], None, ALU.mult, None, r, eng=G, chain=False)
                            for j, (b, _, nk, s) in enumerate(got)]

                def turned_probs(n, r):
                    q, s = n % 4, Sb[n % 4]
                    b = bank()
                    for m in range(q + 1):
                        rr = tr(b.t[:, 128 * m:128 * m + 128], s[:, 128 * m:128 * m + 128], r, b.free, inc=m == q)
                    sb_free[n % 4] = rr
                    b.free = act(PT[:, 0:q + 1, 128 * q:128 * q + 128],
                                 b.t[:, 0:128 * (q + 1)].rearrange("p (m n) -> p m n", n=128), ACT.Copy, rr, t_pt[0])

                def values(h, t_p):
                    ps = slice(64 * (h % 2), 64 * (h % 2) + 64)
                    b = bank()
                    for m in range(4):
                        r = mm(b.t[ps, 128 * m:512], va[:, m, 64 * h:64 * h + 64], PT[:, m, 128 * m:512], m == 0, m == 3,
                               t_p, t_qkv, b.free, inc=m == 3)
                    t_pt[0] = r
                    b.free = r = stt(sga[ps, h // 2, :], sga[ps, h // 2, :], 0.5, b.t[ps, :], ALU.mult, ALU.mult, r, *t_ga)
                    t_att.append(r)

                wait, ready = {}, []
                for n in range(0, 36, 2):
                    for h, t_p in ready:
                        values(h, t_p)
                    ready = []
                    for k in (n - 4, n - 3):
                        if k >= 0:
                            turned_probs(k, wait[k])
                            if k % 4 == 3:
                                ready.append((k // 4, A.last))
                    yield
                    if n < 32:
                        wait[n], wait[n + 1] = scores(n)
                    yield
                for h, t_p in ready:
                    values(h, t_p)

            for dst in (qtok, ktok, va):
                def ev_n(t, b, tok, dst=dst):
                    b.free = act(dst[:, t, :], b.t[:, :], ACT.Copy, tok, *tpr, chain=False)
                proj_n(xa_x, 4, ev_n, False, kt_tok=t_kt)
                if dst is ktok:
                    for j in range(4):
                        b = bank()
                        rr = mm(b.t[:, :], exch, rev[:, 512 * j:512 * j + 512], True, True, t_w2, b.free, inc=True)
                        b.free = act(GB[:, 512 * j:512 * j + 512], b.t[:, :], ACT.Copy, rr, t_xr)
                    t_bi = memset(G, bias[0:64, :, 192:256], -1e30, b.free)
            t_qkv = A.last

            def silu2(o, b, tok):
                a = act(o, b.t[:, :], ACT.Tanh, tok, *tpr, scale=0.5)
                b.free = stt(o, o, 1.0, b.t[:, :], ALU.add, ALU.mult, a)

            def ev_ga(m, b, tok):
                silu2(sga[:, m, :], b, tok)
            att = attention(t_qkv, t_bi, list(tpr))

            def side():
                next(att, None)

            proj_t(XH, XL, 4, 512, 4, ev_ga, tx, side=side)
            t_ga.append(V.last)
            sh = [SCR[:, 520 * i:520 * i + 513] for i in range(2)]
            tsh = [memset(V, sh[i][:, 0:1], 0.0, A.last) for i in range(2)]

            def shift(o, b, tok, j):
                i = j % 2
                a = b.free = act(sh[i][:, 1:513], b.t[:, :], ACT.Copy, tok, tsh[i], *tpr)
                tt(o, sh[i][:, 0:512], sh[i][:, 1:513], ALU.subtract, a)
                tsh[i] = stt(o, o, vec("mu", j), sh[i][:, 1:513], ALU.mult, ALU.add)
                return tsh[i]

            for n, dst in enumerate((R, K, Vt, Gt)):
                def ev_s(m, b, tok, n=n, dst=dst):
                    r = shift(dst[:, m, :], b, tok, 4 * n + m)
                    if n == 3:
                        th = SCR[:, 1040 + 512 * (m % 2):1552 + 512 * (m % 2)]
                        a = act(th, dst[:, m, :], ACT.Tanh, r, scale=0.5)
                        stt(dst[:, m, :], th, 1.0, dst[:, m, :], ALU.add, ALU.mult, a)
                proj_t(XH, XL, 4, 512, 4, ev_s, tx, side=side)
            t_g = V.last
            t_spg = A.dma(d_g, L[1], dsem(), t_g)

            def ev_w(m, b, tok):
                r = shift(wd, b, tok, 16)
                act(wd[0:64, :], wd[0:64, :], ACT.Tanh, r)
            proj_t(XH, XL, 4, 512, 1, ev_w, tx, side=side)
            t_wd = A.last
            t_xfree = PE.last

            for _ in att:
                pass
            for m in range(4):
                t_ya = split(XH[:, 4 + m, :], XL[:, 4 + m, :], sga[:, m, :], t_att, t_xfree)

            cb = GB
            t_cb = G.dma(GB[:, 0:1312], I["cstb"], dsem(), V.last)
            mSU2, mL1 = cb[:, 0:128], cb[:, 128:192]
            mLT = [cb[:, 192 + 64 * i:256 + 64 * i] for i in range(6)]
            id64, bones = cb[:, 576:640], cb[:, 640:768]
            sel = cb[:, 768:800].rearrange("p (a b) -> p a b", a=4)
            selT = cb[0:8, 800:1312]
            smask = SCR[:, 0:512]
            t_sm = G.dma(smask, I["cstc"].partition_broadcast(P), dsem(), V.last, PE.last, A.last)
            hv = SM[:, 132:140]
            r = ts(hv, VEC[:, vcol["w0"]:vcol["w0"] + 8], 0.5, None, ALU.mult, None)
            oka = SM[:, 140:144]
            ts(oka, VEC[:, vcol["ka"]:vcol["ka"] + 4], -1.0, 1.0, ALU.mult, ALU.add)
            LW, AA, C = v4(B[0]), v4(B[1]), v4(B[2])
            X = [XR[:, 0:2, :].rearrange("p a b -> p (a b)"), XR[:, 2:4, :].rearrange("p a b -> p (a b)")]
            kkv = VEC[:, vcol["kk"]:vcol["kk"] + 4]
            tp = [PE.last, V.last, A.last]
            for m in range(4):
                a = act(v4(X[0])[:, m, :], K[:, m, :], ACT.Square, t_spx, *tp, scale=kkv[:, m:m + 1], chain=False)
            b = bank()
            for m in range(4):
                rr = mm(b.t[0:8, :], sel[:, m, :], v4(X[0])[:, m, :], m == 0, m == 3, a, t_cb, b.free, inc=m == 3)
            rs8 = SCR[0:8, 512:1024]
            b.free = r8 = ts(rs8, b.t[0:8, :], 1e-24, None, ALU.max, None, rr, *tp)
            t_lw, t_aa, t_c = [], [], []
            for m in range(4):
                for half, dst in ((0, LW), (1, AA)):
                    b = bank()
                    p = slice(64 * half, 64 * half + 64)
                    rr = mm(b.t[:, :], w2a2[p, 128 * m:128 * m + 128], wd[p, :], True, True, t_wd, t_w2, b.free, inc=True)
                    a = b.free = act(dst[:, m, :], b.t[:, :], ACT.Tanh, rr, r, *tp, scale=0.5,
                                     bias=hv[:, 4 * half + m:4 * half + m + 1], chain=False)
                    if half == 0:
                        t_lw.append(ts(dst[:, m, :], dst[:, m, :], -EM5 / 2, -EM5 / 2, ALU.mult, ALU.add, a, chain=False))
                    else:
                        t_aa.append(ts(dst[:, m, :], dst[:, m, :], 0.5, 0.5, ALU.mult, ALU.add, a, chain=False))
                t_c.append(V.op(lambda e, m=m: e.tensor_tensor_scan(C[:, m, :], smask, LW[:, m, :], 0.0, ALU.mult, ALU.add),
                                t_sm, t_lw[m], chain=False))
                if m == 0:
                    a8 = act(rs8, rs8, ACT.Sqrt, r8, chain=False)
            r8 = V.op(lambda e: e.reciprocal(rs8, rs8), a8)
            r = tt(B[0], B[2], B[0], ALU.subtract, *t_c)
            t_p1 = act(B[0], B[0], ACT.Exp, r)
            t_p = act(B[3], B[2], ACT.Exp)
            t_pi = act(B[2], B[2], ACT.Exp, scale=-1.0)
            KK = v4(L[3])
            t_kk = []
            for m in range(4):
                b = bank()
                rr = mm(b.t[:, :], selT[:, 128 * m:128 * m + 128], rs8, True, True, r8, b.free, inc=True)
                b.free = stt(KK[:, m, :], K[:, m, :], kkv[:, m:m + 1], b.t[:, :], ALU.mult, ALU.mult, rr, *tp, chain=False)
                t_kk.append(b.free)
            t_x0 = [ts(v4(X[0])[:, m, :], AA[:, m, :], vec("ka", m), oka[:, m:m + 1], ALU.mult, ALU.add, t_kk[-1],
                       chain=False) for m in range(4)]
            r = tt(B[5], B[5], X[0], ALU.mult, *t_x0)
            ar = XR[:, :, :].rearrange("p a b -> p (a b)").rearrange("p (x s j) -> p x s j", s=2, j=64)
            k32 = "p (x j) -> p x j"
            r = stt(ar[:, :, 0, :], L[3].rearrange(k32, j=64), -1.0, B[0].rearrange(k32, j=64), ALU.mult, ALU.mult, t_p1)

            def turned_tiles(src, dst, *toks):
                for t in range(4):
                    b = bank()
                    for m in range(4):
                        rr = tr(b.t[:, 128 * m:128 * m + 128], src[:, m, 128 * t:128 * t + 128], *toks, b.free, inc=m == 3)
                    b.free = act(dst[:, t, :], b.t[:, :], ACT.Copy, rr, *toks, chain=False)

            turned_tiles(Vt, v4(B[0]), r)
            tt(B[1], B[1], L[3], ALU.mult)
            rb = tt(B[1], B[1], B[2], ALU.mult, t_pi)
            r3 = tt(L[3], B[4], B[5], ALU.mult)
            r5 = tt(B[5], B[5], B[2], ALU.mult)
            BtT, KtT = AA, K
            turned_tiles(BtT, v4(B[2]), r5)
            pC = SM[:, 188:220].rearrange("p (a c) -> p a c", a=4)
            V.op(lambda e: e.tensor_copy(pC, B[3].rearrange("p (a c k) -> p a c k", a=4, k=64)[:, :, :, 63]), t_p)
            r4 = tt(ar[:, :, 1, :], B[4].rearrange(k32, j=64), B[3].rearrange(k32, j=64), ALU.mult)
            turned_tiles(KtT, v4(B[4]), r4)
            rkb = v4(SCR[:, 1024:1536])
            for m in range(4):
                r = ts(rkb[:, m, :], bones, vec("rk", m), None, ALU.mult, None, t_cb, chain=False)
            for m in range(4):
                b = bank()
                rr = mm(b.t[:, :], rkb[:, m, :], v4(L[3])[:, m, :], True, True, r, r3, b.free, inc=True)
                b.free = r2 = tt(v4(B[3])[:, m, :], Vt[:, m, :], b.t[:, :], ALU.mult, rr, r4, chain=False)
            t_spb = A.dma(d_b, B[3], dsem(), r2)
            t_tok = A.last
            Vk, Bk, Kk = v4(B[0]), v4(B[2]), v4(B[4])
            ar5 = ar.rearrange("p (a c) s j -> p a c s j", a=4)

            NV, Y0 = v4(L[2]), v4(L[3])
            TTc = [L[0][:, 512 * i:512 * i + 512] for i in range(2)]
            KA = L[0][:, 1024:2048].rearrange("p (h s n) -> p h s n", s=2, n=64)
            BAs = [L[1][:, 1024 * i:1024 * i + 1024].rearrange("p (h s n) -> p h s n", s=2, n=64) for i in range(2)]
            Tt, TTt, Xt, Mk0, Mk1 = [SCR[:, 512 * i:512 * i + 512].rearrange("p (h n) -> p h n", n=64) for i in range(5)]
            Mks = [Mk0, Mk1]
            St = B[3][:, 0:256].rearrange("p (m n) -> p m n", m=4)
            Us = [B[3][:, 512 + 512 * i:1024 + 512 * i] for i in range(2)]
            NG = 2
            HG = 8 // NG
            pps = [slice(0, 64), slice(64, 128)]
            t_ops = [r4, r5]
            t0 = [t_spb, t_spg, t_tok, PE.last, A.last, V.last]
            sfree = {}

            def bc(m, n=8):
                return m.unsqueeze(1).broadcast_to([P, n, 64])

            def b3(b, n=8):
                return b.t[:, 0:64 * n].rearrange("p (h n) -> p h n", n=64)

            def inverse(t):
                BA = BAs[t % 2]
                cols = [slice(128 * t + 64 * cp, 128 * t + 64 * cp + 64) for cp in range(2)]
                mask2 = mSU2.unsqueeze(1).broadcast_to([P, 4, 128])
                t_ka = []
                for src, dst, ba in ((KtT, KA, 0), (BtT, BA, 1)):
                    for par, ps in enumerate(pps):
                        b = bank()
                        for m in range(4):
                            for cp in range(2):
                                rr = mm(b.t[pps[cp], 128 * m:128 * m + 128], src[ps, m, cols[cp]],
                                        ar5[ps, m, 2 * t + cp, :, :].rearrange("p s j -> p (s j)"), True, True,
                                        b.free, *t_ops, inc=m == 3 and cp == 1)
                        b.free = r = tt(dst[:, par::2, :, :].rearrange("p h s n -> p h (s n)"),
                                        b.t[:, :].rearrange("p (h n) -> p h n", h=4), mask2, ALU.mult, rr,
                                        sfree.get(("ba", t - 2)) if ba else sfree.get(("ka", t - 1)),
                                        sfree.get(("tt", t - 1)), r2, t_spg)
                        if not ba:
                            t_ka.append(r)
                    yield
                t_ba = r
                for par, ps in enumerate(pps):
                    b = bank()
                    for m in range(4):
                        for cp in range(2):
                            rr = mm(b.t[pps[cp], 64 * m:64 * m + 64], ar5[ps, m, 2 * t + cp, 0, :],
                                    BtT[ps, m, cols[cp]], True, True, b.free, inc=m == 3 and cp == 1)
                    b.free = tt(Tt[:, par::2, :], b3(b, 4), bc(mL1, 4), ALU.mult, rr)
                tt(TTt, BA[:, :, 0, :], bc(mLT[0]), ALU.mult)
                tt(Tt, Tt, bc(id64), ALU.add)
                r = tt(TTt, TTt, bc(id64), ALU.add)
                mk = [None, tt(Mks[1], BA[:, :, 0, :], bc(mLT[1]), ALU.mult, t_ba, sfree.get(("mk", 1)), eng=G)]
                yield
                for s, dst in ((0, NV), (1, Y0)):
                    b = bank()
                    for h in range(8):
                        for cp in range(2):
                            rr = mm(b.t[pps[cp], 64 * h:64 * h + 64], KA[pps[cp], h, s, :],
                                    Vk[pps[cp], t, 64 * h:64 * h + 64], True, True, t_ka[-1], t_tok, b.free,
                                    inc=h == 7 and cp == 1)
                    b.free = act(dst[:, t, :], b.t[:, :], ACT.Copy, rr)
                sfree["nv", t] = b.free
                sfree["ka", t] = rr
                yield
                tg = [r] * NG
                for lv in range(1, 6):
                    if lv < 5:
                        mk.append(tt(Mks[(lv + 1) % 2], BA[:, :, 0, :], bc(mLT[lv + 1]), ALU.mult,
                                     sfree.get(("mk", (lv + 1) % 2)), eng=G))
                    M = Mks[lv % 2]
                    xa = []
                    for g in range(NG):
                        hs = slice(HG * g, HG * g + HG)
                        b = bank()
                        for h in range(HG * g, HG * g + HG):
                            for cp in range(2):
                                rr = mm(b.t[pps[cp], 64 * (h % HG):64 * (h % HG) + 64], M[pps[cp], h, :], Tt[pps[cp], h, :],
                                        True, True, mk[lv], tg[g], b.free, inc=h % HG == HG - 1 and cp == 1)
                        b.free = a = act(Xt[:, hs, :], b3(b, HG), ACT.Copy, rr, sfree.get(("x", g)), chain=False)
                        xa.append(a)
                    sfree["mk", lv % 2] = rr
                    yield
                    for g in range(NG):
                        hs = slice(HG * g, HG * g + HG)
                        prods = [(Xt, TTt)] if lv == 5 else [(TTt, Xt), (Xt, TTt)]
                        bs = []
                        for l, rg in prods:
                            b = bank()
                            for h in range(HG * g, HG * g + HG):
                                for cp in range(2):
                                    rr = mm(b.t[pps[cp], 64 * (h % HG):64 * (h % HG) + 64], l[pps[cp], h, :],
                                            rg[pps[cp], h, :], True, True, xa[g], b.free,
                                            inc=h % HG == HG - 1 and cp == 1)
                            bs.append((b, rr))
                        sfree["x", g] = rr
                        if lv < 5:
                            t_g = tg[g]
                            bs[0][0].free = tt(Tt[:, hs, :], Tt[:, hs, :], b3(bs[0][0], HG), ALU.add, bs[0][1],
                                               bs[1][1], t_g, chain=False)
                            bs[1][0].free = tg[g] = tt(TTt[:, hs, :], TTt[:, hs, :], b3(bs[1][0], HG), ALU.add, bs[1][1],
                                                       t_g, chain=False)
                        else:
                            bs[0][0].free = r = tt(TTc[t % 2].rearrange("p (h n) -> p h n", n=64)[:, hs, :],
                                                   TTt[:, hs, :], b3(bs[0][0], HG), ALU.add, bs[0][1],
                                                   sfree.get(("s", t - 2)))
                    yield
                sfree["tt", t] = r

            s_tok = [memset(V, B[3][:, 0:256], 0.0, *t0)]
            u_free = [None, None]

            def state(t):
                RB = BAs[t % 2]
                for cp in range(2):
                    c = 2 * t + cp
                    pp = pps[cp]
                    nv = NV[pp, t, :].rearrange("p (m q n) -> p m q n", q=2, n=64)
                    y0 = Y0[pp, t, :].rearrange("p (m q n) -> p m q n", q=2, n=64)
                    ws = []
                    for par, ps in enumerate(pps):
                        w = bank()
                        for m in range(4):
                            rr = mm(w.t[:, 64 * m:64 * m + 64], ar5[ps, m, c, :, :].rearrange("p s j -> p (s j)"),
                                    St[ps, m, :], True, True, s_tok[0], w.free, inc=m == 3)
                        r = tt(nv[:, :, par, :], nv[:, :, par, :], b3(w, 4)[0:64], ALU.add, rr, sfree["nv", t], chain=False)
                        ws.append(w)
                    yield
                    b = bank()
                    for h in range(8):
                        hs = slice(64 * h, 64 * h + 64)
                        rr = mm(b.t[pp, hs], TTc[t % 2][pp, hs], NV[pp, t, hs], True, True, r, sfree["tt", t], b.free,
                                inc=h == 7)
                    U = Us[c % 2]
                    b.free = a = act(U[pp, :], b.t[pp, :], ACT.Copy, rr, u_free[c % 2])
                    yield
                    bd = bank()
                    for h in range(8):
                        hs = slice(64 * h, 64 * h + 64)
                        o = bd.t[pps[h % 2], 64 * (h // 2):64 * (h // 2) + 64]
                        mm(o, Kk[pp, t, hs], Vk[pp, t, hs], True, False, a, bd.free)
                        rd = mm(o, Bk[pp, t, hs], U[pp, hs], False, True, inc=h == 7)
                    by = bank()
                    for h in range(8):
                        hs = slice(64 * h, 64 * h + 64)
                        ry = mm(by.t[pp, hs], RB[pp, h, 1, :], U[pp, hs], True, True, by.free, inc=h == 7)
                    u_free[c % 2] = ry
                    bd.free = tt(St, St, b3(bd, 4), ALU.add, rd)
                    s_tok[0] = tt(St, St, pC[:, :, c].unsqueeze(2).broadcast_to([P, 4, 64]), ALU.mult)
                    for par in range(2):
                        ws[par].free = tt(y0[:, :, par, :], y0[:, :, par, :], b3(ws[par], 4)[64:128], ALU.add)
                    by.free = tt(Y0[pp, t, :], Y0[pp, t, :], by.t[pp, :], ALU.add, ry)
                    yield
                sfree["s", t] = sfree["ba", t] = ry
                yield from normed(t, V.last)

            gt, bt_ = B[3][:, 1536:2048].rearrange("p (m n) -> p m n", m=4), SCR[:, 2560:3072].rearrange("p (m n) -> p m n", m=4)
            gm, gs = SM[:, 64:72], SM[:, 72:80]
            gds, ty, t_gt = dsem(), {}, [t0]

            def tile_of(d, t):
                return d.rearrange("p (m n) -> p m n", m=4)[:, :, 128 * t:128 * t + 128]

            def col4(name):
                return VEC[:, vcol[name]:vcol[name] + 4].unsqueeze(2).broadcast_to([P, 4, 128])

            def normed(t, t_y):
                S.dma(gt, tile_of(d_g, t), gds, t_spg, *t_gt)
                t_in = S.dma(bt_, tile_of(d_b, t), gds, t_spb)
                y = Y0[:, t, :].rearrange("p (h n) -> p h n", n=64)
                y2 = NV[:, t, :]
                V.op(lambda e: e.tensor_reduce(gm, y, AX.X, ALU.add), t_y)
                ts(gm, gm, 1.0 / 64, None, ALU.mult, None)
                r = tt(y, y, gm.unsqueeze(2).broadcast_to([P, 8, 64]), ALU.subtract)
                a = act(y2, Y0[:, t, :], ACT.Square, r)
                yield
                r = V.op(lambda e: e.tensor_reduce(gs, y2.rearrange("p (h n) -> p h n", n=64), AX.X, ALU.add), a)
                ts(gs, gs, 1.0 / 64, 64e-5, ALU.mult, ALU.add, r, eng=G)
                r = tt(gs, gs, nhalf[:, 0:8], ALU.pow, t_nh, eng=G)
                yield
                r = tt(y, y, gs.unsqueeze(2).broadcast_to([P, 8, 64]), ALU.mult, r)
                b = bank()
                for m in range(4):
                    rr = tr(b.t[:, 128 * m:128 * m + 128], Y0[:, t, 128 * m:128 * m + 128], r, b.free, inc=m == 3)
                yT = y2.rearrange("p (m n) -> p m n", m=4)
                b.free = tt(yT, b.t[:, :].rearrange("p (m n) -> p m n", m=4), col4("lxg"), ALU.mult, rr)
                yield
                tt(yT, yT, col4("lxb"), ALU.add)
                tt(yT, yT, bt_, ALU.add, t_in)
                r = stt(yT, yT, 0.5, gt, ALU.mult, ALU.mult)
                t_gt[0] = r
                ty[t] = split(XH[:, 0:4, 128 * t:128 * t + 128], XL[:, 0:4, 128 * t:128 * t + 128], yT, r, t_xfree)

            ones = SCR[:, 0:128]
            dg = SCR[:, 1024:2048].rearrange("p (k n) -> p k n", k=8)
            gate = L[0][:, 1024:2048]
            xs = [B[1][:, 0:1024], B[1][:, 1024:2048], B[5][:, 0:1024], B[5][:, 1024:2048]]
            o = out[0].rearrange("(a p) n -> p a n", p=P)
            ods, fin, t_x, t_gate = dsem(), [], [], []

            def ev_o(t, b, tok, j):
                cs = slice(512 * j, 512 * j + 512)
                x = GB[:, 512 * t:512 * t + 512]
                b.free = tt(x, b.t[:, :], gate[:, cs], ALU.mult, tok, *t_gate)
                r = tt(xs[t][:, cs], xs[t][:, cs], x, ALU.add, *t_x)
                fin.append(A.dma(o[:, t, cs], xs[t][:, cs], ods, r))

            def out_tile(t, gots):
                b = bank()
                for c in range(4):
                    i, wh, wl, tok = gots[c]
                    for k in range(2):
                        kt = 2 * c + k
                        xh, xl = xa_x(kt, t)
                        r = mm3(b.t[:, :], xh, xl, wh[:, k, :], wl[:, k, :], kt == 0, kt == 7, tok, b.free, ty[t], t_ya,
                                inc=k == 1)
                    if t == 3:
                        w_release(i, r)
                    else:
                        yield
                ev_o(t, b, r, 0)

            def out_first(gots):
                toks = [PE.last, V.last, A.last]
                ds = dsem()
                S.dma(B[1], d_x[:, 0:2048], ds, t_spx, *toks)
                t_x.append(S.dma(B[5], d_x[:, 2048:4096], ds))
                memset(V, ones, 1.0, *toks)
                for k in range(8):
                    r = ts(dg[:, k, :], ident, mod[:, 16 + k:17 + k], None, ALU.mult, None)
                yield
                for j in range(2):
                    b = bank()
                    for k in range(4):
                        rr = mm(b.t[:, 128 * k:128 * k + 128], ones, dg[:, 4 * j + k, :], True, True, r, b.free, inc=k == 3)
                    b.free = a = act(gate[:, 512 * j:512 * j + 512], b.t[:, :], ACT.Copy, rr)
                    yield
                t_gate.append(a)
                for t in range(3):
                    yield from out_tile(t, gots)

            for t in range(5):
                if t == 4:
                    gots = [w_get() for _ in range(4)]
                gens = ([state(t - 1)] if t > 0 else []) + [inverse(t) if t < 4 else out_first(gots)]
                while gens:
                    for g in list(gens):
                        if next(g, "end") == "end":
                            gens.remove(g)

            for _ in out_tile(3, gots):
                pass
            proj_n(xa_x, 4, lambda t, b, tok: ev_o(t, b, tok, 1), True, t_ya, *ty.values())
            A.wait(fin[-1])

        cc = VEC[:, vcol["c"]:vcol["c"] + 8]
        cs1 = ca = SM[:, 188:196]
        a = act(cs1, cc, ACT.Tanh, t_vec, scale=0.5)
        ts(cs1, cs1, 0.5, 0.5, ALU.mult, ALU.add, a)
        t_c = tt(cs1, cs1, cc, ALU.mult)
        rp = big(11500, 384)[0:8, :]
        r = A.dma(rp[:, 127:319], I["rel_rev"], dsem())
        V.op(lambda e: e.tensor_copy(rp[:, 0:127], rp[:, 127:128].broadcast_to([8, 127])), r)
        r = V.op(lambda e: e.tensor_copy(rp[:, 319:384], rp[:, 318:319].broadcast_to([8, 65])))
        t_rel = A.dma(d_rel, rp, dsem(), r)
        layers()
        t_xr = V.last
        second()

        block = ctx.enter_context(nc.Block())

        def play(eng):
            def f(e):
                for g in eng.q:
                    g(e)
            return f

        block.tensor(play(PE))
        block.vector(play(V))
        block.scalar(play(A))
        block.gpsimd(play(G))
        block.sync(play(S))


_INS = ["x", "mem", "ab_w_in", "sgu_ln_g", "sgu_ln_b", "sgu_w", "sgu_b", "pool_w", "pool_scale", "ab_w_out",
        "c_w_in", "c_conv_w", "c_w_out", "ln_mix_g", "ln_mix_b", "xa_wq", "xa_wkv", "xa_wo", "ln_xa_g", "ln_xa_b",
        "ffn_w_up", "ffn_conv_w", "ffn_conv_b", "ffn_w_down", "ln_ffn_g", "ln_ffn_b", "c_2", "norm_g_2", "w_ada_2",
        "b_ada_2", "w_in_2", "mu_shift_2", "w0_2", "w2_2", "a0_2", "a2_2", "k_k_2", "k_a_2", "r_k_2", "lnx_g_2",
        "lnx_b_2", "q_norm_g_2", "k_norm_g_2", "rel_bias_2", "w_out_2"]


def constants():
    import numpy as np
    cst = np.zeros((128, 144), np.float32)
    cst[:, 0:128] = np.eye(128)
    cst[:, 128:144] = 1.0 / np.arange(1, 17)
    t = np.arange(128)
    s, q = t[:, None] % 64, t[None, 0:64]

    def level(row, col, n):
        return (row // (2 * n) == col // (2 * n)) & (row // n % 2 == 1) & (col // n % 2 == 0)

    cb = np.zeros((128, 1312), np.float32)
    cb[:, 0:64] = s < q
    cb[:, 64:128] = s <= q
    cb[:, 128:192] = level(s, q, 1)
    for i in range(6):
        cb[:, 192 + 64 * i:256 + 64 * i] = level(q, s, 1 << i)
    cb[:, 576:640] = s == q
    cb[:, 640:768] = t[:, None] // 64 == t[None, :] // 64
    for m in range(4):
        for p in range(2):
            cb[64 * p:64 * p + 64, 768 + 8 * m + 2 * m + p] = 1
            cb[2 * m + p, 800 + 128 * m + 64 * p:800 + 128 * m + 64 * p + 64] = 1
    cc = np.ones(512, np.float32)
    cc[0::64] = 0
    return {"cst": cst, "cstb": cb, "cstc": cc, "cstd": np.ascontiguousarray(np.eye(128, dtype=np.float32)[::-1])}


def kernel(**inputs):
    import numpy as _np
    import concourse.bacc as _bacc
    from concourse import mybir as _mybir
    from concourse.bass_utils import run_bass_kernel_spmd as _run

    nc = _bacc.Bacc("TRN2", target_bir_lowering=False, num_devices=1)
    arrays, I = {}, {}
    for name in _INS:
        arrays[name] = _np.ascontiguousarray(inputs[name])
    arrays["rel_rev"] = _np.ascontiguousarray(inputs["rel_bias_2"][0, :, ::-1])
    arrays.update(constants())
    for name, a in arrays.items():
        I[name] = nc.dram_tensor(name, a.shape, _mybir.dt.from_np(a.dtype), kind="ExternalInput").ap()
    o = nc.dram_tensor("out0", (1, 512, 1024), F, kind="ExternalOutput").ap()
    build(nc, I, o)
    r = _run(nc, [arrays], core_ids=[0])
    return r.results[0]["out0"]
```
